# Optimizing a Trainium2 kernel written in Bass

```python
import math
import jax, jax.numpy as jnp
from jax import lax
import numpy as np

D_MODEL = 1024
BATCH = 1
SEQ = 512
DEPTH = 2

GRID_W = 64
CTX_LEN = 256
HEAD_DIM = 64
ROPE_THETA = 10000.0
EPS = 1e-6
Q_BLOCK = 128
NEG = -1e30

A_HEADS = 4
A_DQK = 64
A_DV = 2 * A_DQK
B_HEADS = 8
B_KV_HEADS = 2
B_DH = 64
WINDOW = 128
C_HEADS = 8
C_Q_RANK = 256
C_KV_RANK = 128
C_NOPE = 64
C_ROPE = 32
C_DV = 64
D_HEADS = 4
D_DK = 64
D_DV = 128
D_GATE_RANK = 16
D_GATE_TAU = 16.0
D_CHUNK = 64
P_HEADS = 8
P_NKEYS = 128
P_EXPERTS = P_NKEYS * P_NKEYS
P_DKEY = 256
P_TOPK = 16
P_TOK_BLOCK = 128

EVEN_SIZES = (A_HEADS * 2 * A_DQK, A_HEADS * 2 * A_DQK, A_HEADS * A_DV,
              B_HEADS * B_DH, B_KV_HEADS * B_DH, B_KV_HEADS * B_DH)
ODD_SIZES = (C_Q_RANK, C_KV_RANK, C_ROPE,
             D_HEADS * D_DK, D_HEADS * D_DK, D_HEADS * D_DV, D_GATE_RANK, D_GATE_RANK, D_HEADS * D_DV)
EVEN_IN = sum(EVEN_SIZES)
ODD_IN = sum(ODD_SIZES)

kernel_name = "hybrid_diffusion_diffattn_swa_mla_gla_peer"

F32 = jnp.float32

def rmsnorm(x, g):
    xf = x.astype(F32)
    y = xf * lax.rsqrt(jnp.mean(xf * xf, axis=-1, keepdims=True) + EPS)
    return (y * g.astype(F32)).astype(x.dtype)

def modulate(h, shift, scale):
    return h * (1 + scale) + shift

def modulation(cvec, w_mod, b_mod):
    m = jax.nn.silu(cvec) @ w_mod + b_mod
    return jnp.split(m, 6, axis=-1)

def split_cols(z, sizes):
    out, o = [], 0
    for s in sizes:
        out.append(z[..., o:o + s])
        o += s
    return out

def axial_rope_tables(n_tok, rot_dim):
    rows = n_tok // GRID_W
    r, cc = jnp.meshgrid(jnp.arange(rows, dtype=F32), jnp.arange(GRID_W, dtype=F32), indexing="ij")
    axis_dim = rot_dim // 2
    inv = 1.0 / (ROPE_THETA ** (jnp.arange(0, axis_dim, 2, dtype=F32) / axis_dim))
    ang = jnp.concatenate([r.reshape(-1, 1) * inv, cc.reshape(-1, 1) * inv], axis=-1)
    return jnp.cos(ang), jnp.sin(ang)

def apply_rope(t, cos, sin):
    shp = (1, cos.shape[0]) + (1,) * (t.ndim - 3) + (cos.shape[-1],)
    cs, sn = cos.reshape(shp), sin.reshape(shp)
    t1, t2 = t[..., 0::2].astype(F32), t[..., 1::2].astype(F32)
    out = jnp.stack([t1 * cs - t2 * sn, t1 * sn + t2 * cs], axis=-1).reshape(t.shape)
    return out.astype(t.dtype)

def sweep_query_blocks(fn, q, *ops):
    B, T = q.shape[:2]
    nb = T // Q_BLOCK
    qb = jnp.moveaxis(q.reshape((B, nb, Q_BLOCK) + q.shape[2:]), 1, 0)
    out = lax.map(lambda qq: fn(qq, *ops), qb)
    out = jnp.moveaxis(out, 0, 1)
    return out.reshape((B, T) + out.shape[3:])

def diff_attn(q, k, v, lam):
    s = jnp.einsum("bqhmd,bkhmd->bhmqk", q, k).astype(F32) * (A_DQK ** -0.5)
    p = jax.nn.softmax(s, axis=-1)
    w = p[:, :, 0] - lam * p[:, :, 1]
    return jnp.einsum("bhqk,bkhv->bqhv", w.astype(v.dtype), v)

def softmax_attn(q, k, v, scale):
    s = jnp.einsum("bqhd,bkhd->bhqk", q, k).astype(F32) * scale
    p = jax.nn.softmax(s, axis=-1)
    return jnp.einsum("bhqk,bkhv->bqhv", p.astype(v.dtype), v)

def window_gqa_latent(q, k, v, kc, vc, sink):
    B, S, Hq, d = q.shape
    Hkv = k.shape[2]
    G = Hq // Hkv
    nb = S // Q_BLOCK
    L = kc.shape[1]
    scale = d ** -0.5

    def band(t):
        tp = jnp.pad(t, ((0, 0), (Q_BLOCK, Q_BLOCK), (0, 0), (0, 0))).reshape(B, nb + 2, Q_BLOCK, Hkv, d)
        return jnp.concatenate([tp[:, :-2], tp[:, 1:-1], tp[:, 2:]], axis=2)

    kb = jnp.moveaxis(band(k), 1, 0)
    vb = jnp.moveaxis(band(v), 1, 0)
    qb = jnp.moveaxis(q.reshape(B, nb, Q_BLOCK, Hkv, G, d), 1, 0)
    starts = jnp.arange(nb) * Q_BLOCK
    rel = jnp.arange(3 * Q_BLOCK)[None, :] - Q_BLOCK - jnp.arange(Q_BLOCK)[:, None]
    sink_l = sink.reshape(Hkv, G).astype(F32)

    def one(args):
        qq, kk, vv, st = args
        kpos = st - Q_BLOCK + jnp.arange(3 * Q_BLOCK)
        valid = (jnp.abs(rel) <= WINDOW) & ((kpos >= 0) & (kpos < S))[None, :]
        s_loc = jnp.einsum("bqhgd,bkhd->bhgqk", qq, kk).astype(F32) * scale
        s_loc = jnp.where(valid, s_loc, NEG)
        s_ctx = jnp.einsum("bqhgd,blhd->bhgql", qq, kc).astype(F32) * scale
        s_snk = jnp.broadcast_to(sink_l[None, :, :, None, None], s_ctx.shape[:-1] + (1,))
        p = jax.nn.softmax(jnp.concatenate([s_ctx, s_loc, s_snk], axis=-1), axis=-1)
        o = (jnp.einsum("bhgql,blhd->bqhgd", p[..., :L].astype(vc.dtype), vc)
             + jnp.einsum("bhgqk,bkhd->bqhgd", p[..., L:L + 3 * Q_BLOCK].astype(vv.dtype), vv))
        return o.reshape(B, Q_BLOCK, Hq, d)

    out = lax.map(one, (qb, kb, vb, starts))
    return jnp.moveaxis(out, 0, 1).reshape(B, S, Hq, d)

def ctx_gqa_sink(q, k, v, sink):
    B, L, Hq, d = q.shape
    Hkv = k.shape[2]
    G = Hq // Hkv
    qg = q.reshape(B, L, Hkv, G, d)
    s = jnp.einsum("bqhgd,bkhd->bhgqk", qg, k).astype(F32) * (d ** -0.5)
    snk = jnp.broadcast_to(sink.reshape(Hkv, G).astype(F32)[None, :, :, None, None], s.shape[:-1] + (1,))
    p = jax.nn.softmax(jnp.concatenate([s, snk], axis=-1), axis=-1)[..., :-1]
    return jnp.einsum("bhgqk,bkhd->bqhgd", p.astype(v.dtype), v).reshape(B, L, Hq, d)

def gla_chunked(q, k, v, g, s0):
    B, T, H, dk = q.shape
    dv = v.shape[-1]
    C = D_CHUNK
    n = T // C
    rs = lambda t: t.astype(F32).reshape(B, n, C, H, t.shape[-1])
    qf, kf, vf, gf = rs(q), rs(k), rs(v), rs(g)
    b = jnp.cumsum(gf, axis=2)
    b_last = b[:, :, -1:]
    q_t = qf * jnp.exp(b)
    k_in = kf * jnp.exp(-b)
    k_st = kf * jnp.exp(b_last - b)
    mask = jnp.tril(jnp.ones((C, C), dtype=bool))
    a = jnp.where(mask, jnp.einsum("bnchk,bnshk->bnhcs", q_t, k_in), 0.0)
    o_intra = jnp.einsum("bnhcs,bnshv->bnchv", a, vf)
    ds = jnp.einsum("bnchk,bnchv->nbhkv", k_st, vf)
    decay = jnp.moveaxis(jnp.exp(b_last[:, :, 0]), 1, 0)

    def step(s, inp):
        dcy, dsn = inp
        return dcy[..., None] * s + dsn, s

    s_fin, s_start = lax.scan(step, s0.astype(F32), (decay, ds))
    o_inter = jnp.einsum("bnchk,nbhkv->bnchv", q_t, s_start)
    o = (o_intra + o_inter).reshape(B, T, H, dv)
    return o.astype(v.dtype), s_fin

def mix_even(hx, hc, w_in, w_out, a_qn, a_kn, a_lq1, a_lk1, a_lq2, a_lk2, a_gn, b_qn, b_kn, b_sink,
             lam_init, rope, need_ctx):
    cos, sin = rope

    def proj(h):
        B, T = h.shape[:2]
        aq, ak, av, bq, bk, bv = split_cols(h @ w_in, EVEN_SIZES)
        aq = rmsnorm(aq.reshape(B, T, A_HEADS, 2, A_DQK), a_qn)
        ak = rmsnorm(ak.reshape(B, T, A_HEADS, 2, A_DQK), a_kn)
        av = av.reshape(B, T, A_HEADS, A_DV)
        bq = rmsnorm(bq.reshape(B, T, B_HEADS, B_DH), b_qn)
        bk = rmsnorm(bk.reshape(B, T, B_KV_HEADS, B_DH), b_kn)
        bv = bv.reshape(B, T, B_KV_HEADS, B_DH)
        return aq, ak, av, bq, bk, bv

    xaq, xak, xav, xbq, xbk, xbv = proj(hx)
    caq, cak, cav, cbq, cbk, cbv = proj(hc)
    xaq, xak = apply_rope(xaq, cos, sin), apply_rope(xak, cos, sin)
    xbq, xbk = apply_rope(xbq, cos, sin), apply_rope(xbk, cos, sin)
    lam = (jnp.exp(jnp.sum(a_lq1.astype(F32) * a_lk1.astype(F32)))
           - jnp.exp(jnp.sum(a_lq2.astype(F32) * a_lk2.astype(F32))) + lam_init)

    ka = jnp.concatenate([cak, xak], axis=1)
    va = jnp.concatenate([cav, xav], axis=1)
    ox_a = sweep_query_blocks(diff_attn, xaq, ka, va, lam)
    ox_b = window_gqa_latent(xbq, xbk, xbv, cbk, cbv, b_sink)

    def merge(oa, ob):
        B, T = oa.shape[:2]
        oa = rmsnorm(oa, a_gn) * (1.0 - lam_init)
        return jnp.concatenate([oa.reshape(B, T, -1), ob.reshape(B, T, -1).astype(oa.dtype)], axis=-1) @ w_out

    out_x = merge(ox_a, ox_b)
    out_c = merge(diff_attn(caq, cak, cav, lam), ctx_gqa_sink(cbq, cbk, cbv, b_sink)) if need_ctx else None
    return out_x, out_c

def mix_odd(hx, hc, w_in, w_out, c_gq, c_gkv, c_wq_up, c_wkv_up, c_qn, c_kn,
            d_wg_f, d_bg_f, d_wg_b, d_bg_b, d_gn, rope, need_ctx):
    cos, sin = rope

    def proj(h):
        B, T = h.shape[:2]
        cq, ckv, kpe, dq, dk, dv, gf, gb, r = split_cols(h @ w_in, ODD_SIZES)
        q = (rmsnorm(cq, c_gq) @ c_wq_up).reshape(B, T, C_HEADS, C_NOPE + C_ROPE)
        kv = (rmsnorm(ckv, c_gkv) @ c_wkv_up).reshape(B, T, C_HEADS, C_NOPE + C_DV)
        k = jnp.concatenate([kv[..., :C_NOPE],
                             jnp.broadcast_to(kpe[:, :, None, :], (B, T, C_HEADS, C_ROPE))], axis=-1)
        q, k = rmsnorm(q, c_qn), rmsnorm(k, c_kn)
        v = kv[..., C_NOPE:]
        dq = dq.reshape(B, T, D_HEADS, D_DK) * (D_DK ** -0.5)
        dk = dk.reshape(B, T, D_HEADS, D_DK)
        dv = dv.reshape(B, T, D_HEADS, D_DV)
        lg_f = (jax.nn.log_sigmoid((gf @ d_wg_f + d_bg_f).astype(F32)) / D_GATE_TAU).reshape(B, T, D_HEADS, D_DK)
        lg_b = (jax.nn.log_sigmoid((gb @ d_wg_b + d_bg_b).astype(F32)) / D_GATE_TAU).reshape(B, T, D_HEADS, D_DK)
        r = r.reshape(B, T, D_HEADS, D_DV)
        return q, k, v, dq, dk, dv, lg_f, lg_b, r

    xq, xk, xv, xdq, xdk, xdv, xlf, xlb, xr = proj(hx)
    cq, ck, cv, cdq, cdk, cdv, clf, clb, cr = proj(hc)

    def rope_tail(t):
        return jnp.concatenate([t[..., :C_NOPE], apply_rope(t[..., C_NOPE:], cos, sin)], axis=-1)

    xq, xk = rope_tail(xq), rope_tail(xk)
    scale = (C_NOPE + C_ROPE) ** -0.5
    kc_all = jnp.concatenate([ck, xk], axis=1)
    vc_all = jnp.concatenate([cv, xv], axis=1)
    ox_c = sweep_query_blocks(softmax_attn, xq, kc_all, vc_all, scale)

    B = hx.shape[0]
    zeros = jnp.zeros((B, D_HEADS, D_DK, D_DV), F32)
    flip = lambda t: jnp.flip(t, axis=1)
    oc_f, sc_f = gla_chunked(cdq, cdk, cdv, clf, zeros)
    ox_f, _ = gla_chunked(xdq, xdk, xdv, xlf, sc_f)
    oc_br, sc_b = gla_chunked(flip(cdq), flip(cdk), flip(cdv), flip(clb), zeros)
    ox_br, _ = gla_chunked(flip(xdq), flip(xdk), flip(xdv), flip(xlb), sc_b)

    def merge(oc_mla, o_gla, r):
        Bn, T = oc_mla.shape[:2]
        g = (rmsnorm(o_gla, d_gn) * jax.nn.silu(r)).astype(oc_mla.dtype)
        return jnp.concatenate([oc_mla.reshape(Bn, T, -1), g.reshape(Bn, T, -1)], axis=-1) @ w_out

    out_x = merge(ox_c, ox_f + flip(ox_br), xr)
    out_c = merge(softmax_attn(cq, ck, cv, scale), oc_f + flip(oc_br), cr) if need_ctx else None
    return out_x, out_c

def peer(h, wq, sub_keys, u_tab, v_tab):
    T, D = h.shape
    q = (h @ wq).reshape(T, P_HEADS, 2, P_DKEY // 2)
    s = jnp.einsum("thpd,hpnd->thpn", q, sub_keys).astype(F32)
    sv, si = lax.top_k(s, P_TOPK)
    cand = (sv[:, :, 0, :, None] + sv[:, :, 1, None, :]).reshape(T, P_HEADS, P_TOPK * P_TOPK)
    cidx = (si[:, :, 0, :, None] * P_NKEYS + si[:, :, 1, None, :]).reshape(T, P_HEADS, P_TOPK * P_TOPK)
    fv, fi = lax.top_k(cand, P_TOPK)
    eidx = jnp.take_along_axis(cidx, fi, axis=-1).reshape(T, P_HEADS * P_TOPK)
    gate = jax.nn.softmax(fv, axis=-1).reshape(T, P_HEADS * P_TOPK)
    nb = T // P_TOK_BLOCK

    def blk(args):
        hb, ib, gb = args
        a = jax.nn.gelu(jnp.einsum("tkd,td->tk", u_tab[ib], hb).astype(F32), approximate=False) * gb
        return jnp.einsum("tk,tkd->td", a.astype(hb.dtype), v_tab[ib])

    out = lax.map(blk, (h.reshape(nb, P_TOK_BLOCK, D), eidx.reshape(nb, P_TOK_BLOCK, -1),
                        gate.reshape(nb, P_TOK_BLOCK, -1)))
    return out.reshape(T, D)

def setup_inputs(seed: int = 0) -> dict:
    key = jax.random.key(seed)
    ks = iter(jax.random.split(key, 64))
    nrm = lambda shape, scale: jax.random.normal(next(ks), shape, F32) * scale
    gain = lambda shape: 1.0 + nrm(shape, 0.02)
    D = D_MODEL
    NE = (DEPTH + 1) // 2
    NO = DEPTH // 2
    return {
        "x": nrm((BATCH, SEQ, D), 1.0),
        "c": nrm((BATCH, D), 1.0),
        "ctx": nrm((BATCH, CTX_LEN, D), 1.0),
        "c_ctx": nrm((D,), 1.0),
        "w_mod": nrm((DEPTH, D, 6 * D), 0.5 * D ** -0.5),
        "b_mod": nrm((DEPTH, 6 * D), 0.02),
        "norm1": gain((DEPTH, D)),
        "norm2": gain((DEPTH, D)),
        "e_w_in": nrm((NE, D, EVEN_IN), D ** -0.5),
        "e_w_out": nrm((NE, D, D), D ** -0.5),
        "a_qn": gain((NE, A_DQK)),
        "a_kn": gain((NE, A_DQK)),
        "a_lq1": nrm((NE, A_DQK), 0.1),
        "a_lk1": nrm((NE, A_DQK), 0.1),
        "a_lq2": nrm((NE, A_DQK), 0.1),
        "a_lk2": nrm((NE, A_DQK), 0.1),
        "a_gn": gain((NE, A_DV)),
        "b_qn": gain((NE, B_DH)),
        "b_kn": gain((NE, B_DH)),
        "b_sink": nrm((NE, B_HEADS), 0.5),
        "o_w_in": nrm((NO, D, ODD_IN), D ** -0.5),
        "o_w_out": nrm((NO, D, D), D ** -0.5),
        "c_gq": gain((NO, C_Q_RANK)),
        "c_gkv": gain((NO, C_KV_RANK)),
        "c_wq_up": nrm((NO, C_Q_RANK, C_HEADS * (C_NOPE + C_ROPE)), C_Q_RANK ** -0.5),
        "c_wkv_up": nrm((NO, C_KV_RANK, C_HEADS * (C_NOPE + C_DV)), C_KV_RANK ** -0.5),
        "c_qn": gain((NO, C_NOPE + C_ROPE)),
        "c_kn": gain((NO, C_NOPE + C_ROPE)),
        "d_wg_f": nrm((NO, D_GATE_RANK, D_HEADS * D_DK), D_GATE_RANK ** -0.5),
        "d_bg_f": nrm((NO, D_HEADS * D_DK), 0.1),
        "d_wg_b": nrm((NO, D_GATE_RANK, D_HEADS * D_DK), D_GATE_RANK ** -0.5),
        "d_bg_b": nrm((NO, D_HEADS * D_DK), 0.1),
        "d_gn": gain((NO, D_DV)),
        "p_wq": nrm((DEPTH, D, P_HEADS * P_DKEY), D ** -0.5),
        "p_keys": nrm((DEPTH, P_HEADS, 2, P_NKEYS, P_DKEY // 2), (P_DKEY // 2) ** -0.5),
        "p_u": nrm((DEPTH, P_EXPERTS, D), D ** -0.5),
        "p_v": nrm((DEPTH, P_EXPERTS, D), 1.0),
    }

def reference(x, c, ctx, c_ctx, w_mod, b_mod, norm1, norm2, e_w_in, e_w_out, a_qn, a_kn, a_lq1, a_lk1,
              a_lq2, a_lk2, a_gn, b_qn, b_kn, b_sink, o_w_in, o_w_out, c_gq, c_gkv, c_wq_up, c_wkv_up,
              c_qn, c_kn, d_wg_f, d_bg_f, d_wg_b, d_bg_b, d_gn, p_wq, p_keys, p_u, p_v):
    B, S, D = x.shape
    L = ctx.shape[1]
    rope_ab = axial_rope_tables(S, HEAD_DIM)
    rope_c = axial_rope_tables(S, C_ROPE)
    h = ctx
    for i in range(DEPTH):
        last = i == DEPTH - 1
        j = i // 2
        mx = [m[:, None, :] for m in modulation(c, w_mod[i], b_mod[i])]
        mc = modulation(c_ctx, w_mod[i], b_mod[i])
        hx = modulate(rmsnorm(x, norm1[i]), mx[0], mx[1])
        hc = modulate(rmsnorm(h, norm1[i]), mc[0], mc[1])
        if i % 2 == 0:
            lam_init = 0.8 - 0.6 * math.exp(-0.3 * i)
            ox, oc = mix_even(hx, hc, e_w_in[j], e_w_out[j], a_qn[j], a_kn[j], a_lq1[j], a_lk1[j],
                              a_lq2[j], a_lk2[j], a_gn[j], b_qn[j], b_kn[j], b_sink[j],
                              lam_init, rope_ab, not last)
        else:
            ox, oc = mix_odd(hx, hc, o_w_in[j], o_w_out[j], c_gq[j], c_gkv[j], c_wq_up[j], c_wkv_up[j],
                             c_qn[j], c_kn[j], d_wg_f[j], d_bg_f[j], d_wg_b[j], d_bg_b[j], d_gn[j],
                             rope_c, not last)
        x = x + mx[2] * ox
        hx = modulate(rmsnorm(x, norm2[i]), mx[3], mx[4])
        x = x + mx[5] * peer(hx.reshape(B * S, D), p_wq[i], p_keys[i], p_u[i], p_v[i]).reshape(B, S, D)
        if not last:
            h = h + mc[2] * oc
            hc = modulate(rmsnorm(h, norm2[i]), mc[3], mc[4])
            h = h + mc[5] * peer(hc.reshape(B * L, D), p_wq[i], p_keys[i], p_u[i], p_v[i]).reshape(B, L, D)
    return x


_drawn_inputs = setup_inputs


def setup_inputs(seed=0):
    import zlib

    import numpy as np

    out = dict(_drawn_inputs(seed))
    spreads = {}
    factors = {'norm1': 3.047,
     'a_qn': 4.469,
     'a_kn': 4.64,
     'a_lq2': 5.924,
     'a_gn': 2.983,
     'b_qn': 6.882,
     'b_kn': 7.065,
     'b_sink': 8.0,
     'c_gq': 8.0,
     'c_gkv': 8.0,
     'c_qn': 8.0,
     'c_kn': 8.0,
     'd_bg_f': 4.976,
     'd_bg_b': 4.737,
     'd_gn': 6.187}
    for name, (base, spread) in spreads.items():
        noise = np.random.default_rng([zlib.crc32(name.encode()), seed]).standard_normal(out[name].shape)
        drawn = base * np.exp(spread * noise) if base else spread * noise
        out[name] = __import__('jax').numpy.asarray(drawn.astype(out[name].dtype))
    for name, factor in factors.items():
        out[name] = (out[name] * factor).astype(out[name].dtype)
    return out
```

```python
from contextlib import ExitStack, contextmanager

import numpy as np

import concourse.bass as bass
from concourse import mybir

P = 128
D = 1024
KC = D // P
CTX, SEQ = 256, 512
CT, XT = CTX // P, SEQ // P
NT = CT + XT
TOK = NT * P
BANK = 512
EPS = 1e-6
NEG = -1e30
GRID_W = 64
THETA = 10000.0

A_HEADS, A_DQK, A_DV = 4, 64, 128
B_HEADS, B_KV, B_DH = 8, 2, 64
AQ, AK, AV = 0, 512, 1024
BQ, BK, BV = 1536, 2048, 2176
EVEN_IN = 2304
LAM_INIT = 0.8 - 0.6

C_HEADS, C_NOPE, C_ROPE, C_DV = 8, 64, 32, 64
C_DQ = C_NOPE + C_ROPE
G_HEADS, G_DK, G_DV, G_CHUNK, G_RANK, G_TAU = 4, 64, 128, 64, 16, 16.0
CQ, CKV, KPE, DQ, DK, DV, GF, DR = 0, 256, 384, 416, 672, 928, 1440, 1472
ODD_IN = 1984

PH, NK, TOPK = 8, 128, 16
SLOTS = PH * TOPK
RING = 8

F32 = mybir.dt.float32
U32 = mybir.dt.uint32
ALU = mybir.AluOpType
ACT = mybir.ActivationFunctionType
AX = mybir.AxisListType
ds = bass.ds


@contextmanager
def repeat(eng, n):
    if n == 1:
        yield 0
    else:
        with eng.Fori(0, n) as i:
            yield i


def rows(ap, n=P):
    return ap.broadcast_to([n, ap.shape[-1]])


class Memory:
    pass


class Stage:

    def __init__(self, nc, name):
        self.nc, self.name, self.ctx = nc, name, ExitStack()
        self.used = []

    def __enter__(self):
        return self

    def __exit__(self, *err):
        for sem in self.used:
            self.nc.sync.sem_clear(sem)
        return self.ctx.__exit__(*err)

    def sb(self, name, shape, dt=F32):
        return self.ctx.enter_context(self.nc.sbuf_tensor(f"{self.name}_{name}", shape, dt))

    def sem(self, name):
        self.used.append(self.ctx.enter_context(self.nc.semaphore(f"{self.name}_{name}")))
        return self.used[-1]

    def pool_dma_sems(self, m, name, n):
        return [m.ctx.enter_context(self.nc.semaphore(f"{self.name}_{name}{i}")) for i in range(n)]

    def sems(self, name, n):
        return [self.sem(f"{name}{i}") for i in range(n)]


def modulation_rows(nc, m, a):
    NCH = 6 * D // BANK
    RG = 4
    with Stage(nc, "mod") as s:
        craw = s.sb("craw", [P, 2, KC])
        den = s.sb("den", [P, 2, KC])
        csil = s.sb("csil", [P, KC, 2])
        w = s.sb("w", [P, RG, KC, BANK])
        bias = s.sb("bias", [2, RG, BANK])
        row = s.sb("row", [2, RG, BANK])
        c_loaded, exp_done, silu_done = s.sem("c_loaded"), s.sem("exp_done"), s.sem("silu_done")
        loaded, used = s.sems("loaded", RG), s.sems("used", RG)
        row_ready, row_stored = s.sems("row_ready", RG), s.pool_dma_sems(m, "row_stored", RG)
        with nc.Block() as block:
            @block.sync
            def _(sp):
                sp.dma_start(craw[:, 0, :], a["c"].rearrange("o (p k) -> p (o k)", k=KC)).then_inc(c_loaded, 16)
                sp.dma_start(craw[:, 1, :], a["c_ctx"].rearrange("(p k) -> p k", k=KC)).then_inc(c_loaded, 16)
                with sp.Fori(0, 2) as l:
                    for n in range(NCH):
                        q, use = n % RG, l * (NCH // RG) + n // RG
                        sp.wait_ge(used[q], use)
                        sp.wait_ge(row_ready[q], use)
                        sp.dma_start(w[:, q], a["w_mod"][ds(l, 1), :, n * BANK:(n + 1) * BANK]
                                     .rearrange("o (p k) n -> p (o k) n", k=KC)).then_inc(loaded[q], 16)
                        sp.dma_start(bias[:, q], a["b_mod"][ds(l, 1), n * BANK:(n + 1) * BANK]
                                     .broadcast_to([2, BANK])).then_inc(loaded[q], 16)

            @block.scalar
            def _(act):
                act.wait_ge(c_loaded, 32)
                act.activation(den[:, :, :], craw[:, :, :], ACT.Exp, scale=-1.0).then_inc(exp_done, 1)

            @block.tensor
            def _(pe):
                pe.wait_ge(silu_done, 1)
                with pe.Fori(0, 2) as l:
                    for n in range(NCH):
                        q, use = n % RG, l * (NCH // RG) + n // RG
                        pe.wait_ge(loaded[q], use * 32 + 32)
                        pe.wait_ge(row_ready[q], use)
                        for k in range(KC):
                            mm = pe.matmul(m.ps[0:2, q, :], csil[:, k, :], w[:, q, k, :],
                                           start=(k == 0), stop=(k == KC - 1))
                        mm.then_inc(used[q], 1)

            @block.vector
            def _(dve):
                dve.wait_ge(exp_done, 1)
                dve.tensor_scalar(den[:, :, :], den[:, :, :], 1.0, None, ALU.add)
                dve.drain()
                dve.reciprocal(den[:, :, :], den[:, :, :])
                dve.drain()
                dve.tensor_tensor(csil[:, :, :].rearrange("p k s -> p s k"), craw[:, :, :], den[:, :, :],
                                  ALU.mult).then_inc(silu_done, 1)
                with dve.Fori(0, 2) as l:
                    for n in range(NCH):
                        q, use = n % RG, l * (NCH // RG) + n // RG
                        dve.wait_ge(used[q], use + 1)
                        dve.wait_ge(row_stored[q], use * 16)
                        dve.tensor_tensor(row[:, q, :], m.ps[0:2, q, :], bias[:, q, :], ALU.add)\
                           .then_inc(row_ready[q], 1)

            @block.gpsimd
            def _(pool):
                with pool.Fori(0, 2) as l:
                    for n in range(NCH):
                        q, use = n % RG, l * (NCH // RG) + n // RG
                        pool.wait_ge(row_ready[q], use + 1)
                        pool.dma_start(m.mods[ds(l, 1), :, n * BANK:(n + 1) * BANK]
                                       .rearrange("o s n -> (o s) n"), row[:, q, :]).then_inc(row_stored[q], 16)
                for q in range(RG):
                    pool.wait_ge(row_stored[q], 2 * (NCH // RG) * 16)


def load_streams(nc, m, a):
    with Stage(nc, "ld") as s:
        done = s.sem("done")
        with nc.Block() as block:
            @block.vector
            def _(dve):
                dve.memset(m.eps[:, :], EPS)

            @block.sync
            def _(sp):
                sp.dma_start(m.R[:, 0:CT, :], a["ctx"].rearrange("b (t p) d -> p (b t) d", p=P)).then_inc(done, 16)
                sp.dma_start(m.R[:, CT:NT, :], a["x"].rearrange("b (t p) d -> p (b t) d", p=P)).then_inc(done, 16)
                sp.dma_start(m.ident[:, :], a["ident"]).then_inc(done, 16)
                sp.wait_ge(done, 48)


def modulated_norm(nc, m, a, layer, sub, gain_name, tiles):
    shift_at, scale_at = 3 * sub * D, (3 * sub + 1) * D
    with Stage(nc, f"n{layer}{sub}") as s:
        gain = s.sb("gain", [P, D])
        scale, shift = s.sb("scale", [P, 2, D]), s.sb("shift", [P, 2, D])
        sq = s.sb("sq", [P, D])
        ss = s.sb("ss", [P, NT])
        loaded, rms_ready, h_ready = s.sem("loaded"), s.sem("rms_ready"), s.sem("h_ready")
        turned, copied = s.sem("turned"), s.sem("copied")
        with nc.Block() as block:
            @block.sync
            def _(sp):
                sp.dma_start(gain[:, :], rows(a[gain_name][layer:layer + 1, :])).then_inc(loaded, 16)
                for st in range(2):
                    sp.dma_start(scale[:, st, :], rows(m.mods[layer, st:st + 1, scale_at:scale_at + D])).then_inc(loaded, 16)
                    sp.dma_start(shift[:, st, :], rows(m.mods[layer, st:st + 1, shift_at:shift_at + D])).then_inc(loaded, 16)

            @block.scalar
            def _(act):
                for t in tiles:
                    act.activation(sq[:, :], m.R[:, t, :], ACT.Square, accum_out=ss[:, t:t + 1])
                    act.drain()
                act.activation(ss[:, tiles[0]:NT], ss[:, tiles[0]:NT], ACT.Sqrt, bias=m.eps[:, :],
                               scale=1.0 / D).then_inc(rms_ready, 1)
                for n, t in enumerate(tiles):
                    act.wait_ge(turned, n + 1)
                    act.copy(m.hT[:, :, t * P:(t + 1) * P],
                             m.ps[:, 2 * (n % 2):2 * (n % 2) + 2, :].rearrange("p b (k c) -> p (b k) c", c=P))\
                       .then_inc(copied, 1)

            @block.vector
            def _(dve):
                dve.wait_ge(loaded, 80)
                for st in range(2):
                    dve.scalar_tensor_tensor(out=scale[:, st, :], in0=scale[:, st, :], scalar=1.0,
                                             in1=gain[:, :], op0=ALU.add, op1=ALU.mult)
                dve.wait_ge(rms_ready, 1)
                dve.reciprocal(ss[:, tiles[0]:NT], ss[:, tiles[0]:NT])
                dve.drain()
                for t in tiles:
                    st = 1 if t < CT else 0
                    dve.scalar_tensor_tensor(out=m.H[:, t, :], in0=m.R[:, t, :], scalar=ss[:, t:t + 1],
                                             in1=scale[:, st, :], op0=ALU.mult, op1=ALU.mult)
                    dve.drain()
                    dve.tensor_tensor(m.H[:, t, :], m.H[:, t, :], shift[:, st, :], ALU.add).then_inc(h_ready, 1)

            @block.tensor
            def _(pe):
                for n, t in enumerate(tiles):
                    pe.wait_ge(h_ready, n + 1)
                    if n >= 2:
                        pe.wait_ge(copied, n - 1)
                    for k in range(KC):
                        tr = pe.transpose(m.ps[:, 2 * (n % 2) + k // 4, (k % 4) * P:(k % 4 + 1) * P],
                                          m.H[:, t, k * P:(k + 1) * P], m.ident[:, :])
                    tr.then_inc(turned, 1)


def turn_h(nc, m, name, tiles):
    with Stage(nc, name) as s:
        turned, copied = s.sem("turned"), s.sem("copied")
        with nc.Block() as block:
            @block.tensor
            def _(pe):
                for n, t in enumerate(tiles):
                    if n >= 2:
                        pe.wait_ge(copied, n - 1)
                    for k in range(KC):
                        tr = pe.transpose(m.ps[:, 2 * (n % 2) + k // 4, (k % 4) * P:(k % 4 + 1) * P],
                                          m.H[:, t, k * P:(k + 1) * P], m.ident[:, :])
                    tr.then_inc(turned, 1)

            @block.scalar
            def _(act):
                for n, t in enumerate(tiles):
                    act.wait_ge(turned, n + 1)
                    act.copy(m.hT[:, :, t * P:(t + 1) * P],
                             m.ps[:, 2 * (n % 2):2 * (n % 2) + 2, :].rearrange("p b (k c) -> p (b k) c", c=P))\
                       .then_inc(copied, 1)


def project(nc, m, name, weight, tiles, chunk, out=None, gate=None):
    pairs = weight.shape[1] // chunk // 2
    n_t = len(tiles)
    body = 2 * n_t
    with Stage(nc, name) as s:
        w = s.sb("w", [P, 2, KC, chunk])
        loaded, used = s.sems("loaded", 2), s.sems("used", 2)
        done, free = s.sems("done", 4), s.sems("free", 4)
        if gate is not None:
            g = s.sb("g", [P, 2, D])
            tmp = s.sb("tmp", [P, 2, chunk])
            g_loaded, scaled, added = s.sem("g_loaded"), s.sem("scaled"), s.sem("added")
        with nc.Block() as block:
            @block.sync
            def _(sp):
                if gate is not None:
                    for st in range(2):
                        sp.dma_start(g[:, st, :], rows(gate[st:st + 1, :])).then_inc(g_loaded, 16)
                with repeat(sp, pairs) as i:
                    for q in range(2):
                        sp.wait_ge(used[q], i)
                        sp.dma_start(w[:, q], weight[:, ds((i * 2 + q) * chunk, chunk)]
                                     .rearrange("(k p) n -> p k n", p=P)).then_inc(loaded[q], 16)

            @block.tensor
            def _(pe):
                with repeat(pe, pairs) as i:
                    for q in range(2):
                        pe.wait_ge(loaded[q], i * 16 + 16)
                        for n, t in enumerate(tiles):
                            b, use = (q * n_t + n) % 4, (q * n_t + n) // 4
                            pe.wait_ge(free[b], i * (body // 4) + use)
                            for k in range(KC):
                                mm = pe.matmul(m.ps[:, b, 0:chunk], m.hT[:, k, t * P:(t + 1) * P], w[:, q, k, :],
                                               start=(k == 0), stop=(k == KC - 1))
                            mm.then_inc(done[b], 1)
                            if n == n_t - 1:
                                pe.drain()
                                pe.sem_inc(used[q], 1)

            if gate is None:
                def evict(eng, copy, parity):
                    with repeat(eng, pairs) as i:
                        for c in range(parity, body, 2):
                            q, t, b, use = c // n_t, tiles[c % n_t], c % 4, c // 4
                            eng.wait_ge(done[b], i * (body // 4) + use + 1)
                            copy(out[:, t, ds((i * 2 + q) * chunk, chunk)], m.ps[:, b, 0:chunk]).then_inc(free[b], 1)

                @block.scalar
                def _(act):
                    evict(act, act.copy, 0)

                @block.vector
                def _(dve):
                    evict(dve, dve.tensor_copy, 1)
            else:
                @block.vector
                def _(dve):
                    dve.wait_ge(g_loaded, 32)
                    for c in range(body):
                        q, t, b, use = c // n_t, tiles[c % n_t], c % 4, c // 4
                        cols = slice(q * chunk, (q + 1) * chunk)
                        dve.wait_ge(done[b], use + 1)
                        if c >= 2:
                            dve.wait_ge(added, c - 1)
                        dve.tensor_tensor(tmp[:, c % 2, :], m.ps[:, b, 0:chunk], g[:, 1 if t < CT else 0, cols],
                                          ALU.mult).then_inc(free[b], 1)
                        dve.drain()
                        dve.sem_inc(scaled, 1)

                @block.gpsimd
                def _(pool):
                    for c in range(body):
                        q, t = c // n_t, tiles[c % n_t]
                        cols = slice(q * chunk, (q + 1) * chunk)
                        pool.wait_ge(scaled, c + 1)
                        pool.tensor_tensor(m.R[:, t, cols], m.R[:, t, cols], tmp[:, c % 2, :], ALU.add)\
                            .then_inc(added, 1)


def head_norm(nc, m, a, name, buf, tiles, segs, rope=None, factor=1.0):
    turns = len(tiles) // 2
    S = sum(g * d for _, g, d, _ in segs)
    G = sum(g for _, g, _, _ in segs)
    with Stage(nc, name) as s:
        sq = s.sb("sq", [P, 2, S])
        ss = s.sb("ss", [P, 2, G])
        gains = s.sb("gains", [P, sum(d for _, _, d, _ in segs)])
        loaded = s.sem("loaded")
        squared, summed, rooted = s.sems("squared", 2), s.sems("summed", 2), s.sems("rooted", 2)
        if rope:
            r0, nr, tables = rope
            cos, sin = s.sb("cos", [P, NT, nr]), s.sb("sin", [P, NT, nr])
            near, far = s.sb("near", [P, 2, G, nr]), s.sb("far", [P, 2, G, nr])
            scaled, near_ready = s.sems("scaled", 2), s.sems("near_ready", 2)

        def parts(i, q):
            at = g0 = gain0 = 0
            for c, g, d, _ in segs:
                yield (buf[:, i * 2 + q + (tiles[0] if tiles[0] and buf.shape[1] == NT else 0), c:c + g * d]
                       .rearrange("p (g d) -> p g d", d=d),
                       sq[:, q, at:at + g * d].rearrange("p (g d) -> p g d", d=d), ss[:, q, g0:g0 + g],
                       gains[:, gain0:gain0 + d], g, d, g0)
                at, g0, gain0 = at + g * d, g0 + g, gain0 + d

        def table(tab, i, q, g):
            return tab[:, ds(i * 2 + q + tiles[0], 1), :].broadcast_to([P, g, nr])

        def pairs(x, which):
            return x.rearrange("p g (f two) -> p g f two", two=2)[:, :, :, which]

        with nc.Block() as block:
            @block.sync
            def _(sp):
                at = 0
                for _, _, d, gain in segs:
                    sp.dma_start(gains[:, at:at + d], rows(gain)).then_inc(loaded, 16)
                    at += d
                if rope:
                    sp.dma_start(cos[:, :, :], a[tables + "_cos"].rearrange("(t p) d -> p t d", p=P)).then_inc(loaded, 16)
                    sp.dma_start(sin[:, :, :], a[tables + "_sin"].rearrange("(t p) d -> p t d", p=P)).then_inc(loaded, 16)

            n_loads = len(segs) + (2 if rope else 0)

            @block.scalar
            def _(act):
                with repeat(act, turns) as i:
                    for q in range(2):
                        act.wait_ge(rooted[q], i)
                        act.wait_ge(summed[q], i)
                        for x, x2, *_ in parts(i, q):
                            sqr = act.activation(x2, x, ACT.Square)
                        sqr.then_inc(squared[q], 1)
                    for q in range(2):
                        act.wait_ge(summed[q], i + 1)
                        for x, x2, r, gn, g, d, g0 in parts(i, q):
                            root = act.activation(r, r, ACT.Sqrt, bias=m.eps[:, :], scale=1.0 / d)
                        root.then_inc(rooted[q], 1)

            @block.vector
            def _(dve):
                dve.wait_ge(loaded, 16 * n_loads)
                if factor != 1.0:
                    dve.tensor_scalar(gains[:, :], gains[:, :], factor, None, ALU.mult)
                    dve.drain()
                with repeat(dve, turns) as i:
                    for q in range(2):
                        dve.wait_ge(squared[q], i + 1)
                        for x, x2, r, gn, g, d, g0 in parts(i, q):
                            red = dve.tensor_reduce(r, x2, AX.X, ALU.add)
                        red.then_inc(summed[q], 1)
                    for q in range(2):
                        dve.wait_ge(rooted[q], i + 1)
                        dve.reciprocal(ss[:, q, :], ss[:, q, :])
                        dve.drain()
                        for x, x2, r, gn, g, d, g0 in parts(i, q):
                            dve.tensor_tensor(x, x, r.unsqueeze(2).broadcast_to([P, g, d]), ALU.mult)
                        dve.drain()
                        for x, x2, r, gn, g, d, g0 in parts(i, q):
                            mul = dve.tensor_tensor(x, x, gn.unsqueeze(1).broadcast_to([P, g, d]), ALU.mult)
                        if rope:
                            mul.then_inc(scaled[q], 1)
                            dve.drain()
                            for x, x2, r, gn, g, d, g0 in parts(i, q):
                                tail, f = x[:, :, r0:r0 + nr], far[:, q, g0:g0 + g, :]
                                tab = table(sin, i, q, g)
                                for e in range(2):
                                    dve.tensor_tensor(pairs(f, e), pairs(tail, 1 - e), pairs(tab, e), ALU.mult)
                            dve.drain()
                            dve.wait_ge(near_ready[q], i + 1)
                            for x, x2, r, gn, g, d, g0 in parts(i, q):
                                dve.tensor_tensor(x[:, :, r0:r0 + nr], near[:, q, g0:g0 + g, :],
                                                  far[:, q, g0:g0 + g, :], ALU.add)

            if rope:
                @block.gpsimd
                def _(pool):
                    pool.wait_ge(loaded, 16 * n_loads)
                    with repeat(pool, turns) as i:
                        for q in range(2):
                            pool.wait_ge(scaled[q], i + 1)
                            for x, x2, r, gn, g, d, g0 in parts(i, q):
                                mul = pool.tensor_tensor(near[:, q, g0:g0 + g, :], x[:, :, r0:r0 + nr],
                                                         table(cos, i, q, g), ALU.mult)
                            mul.then_inc(near_ready[q], 1)


def lambda_and_sinks(nc, m, a):
    with Stage(nc, "lam") as s:
        v = s.sb("v", [P, 4, A_DQK])
        junk = s.sb("junk", [P, 2, A_DQK])
        dots = s.sb("dots", [P, 2])
        loaded, dots_ready, exp_done = s.sem("loaded"), s.sem("dots_ready"), s.sem("exp_done")
        with nc.Block() as block:
            @block.sync
            def _(sp):
                for n, key in enumerate(("a_lq1", "a_lk1", "a_lq2", "a_lk2")):
                    sp.dma_start(v[:, n, :], rows(a[key])).then_inc(loaded, 16)
                sp.dma_start(m.sink[:, :], rows(a["b_sink"])).then_inc(loaded, 16)
                sp.dma_start(m.band[:, :, :], a["band"].rearrange("s p k -> p s k")).then_inc(loaded, 16)

            @block.vector
            def _(dve):
                dve.wait_ge(loaded, 96)
                for n in range(2):
                    dve.scalar_tensor_tensor(out=junk[:, n, :], in0=v[:, 2 * n, :], scalar=1.0, in1=v[:, 2 * n + 1, :],
                                             op0=ALU.mult, op1=ALU.mult, accum_out=dots[:, n:n + 1])
                dve.tensor_scalar(m.neg_sink[:, :], m.sink[:, :], -1.0, None, ALU.mult)
                dve.drain()
                dve.sem_inc(dots_ready, 1)
                dve.wait_ge(exp_done, 1)
                dve.scalar_tensor_tensor(out=m.neg_lam[:, :], in0=dots[:, 1:2], scalar=-LAM_INIT, in1=dots[:, 0:1],
                                         op0=ALU.add, op1=ALU.subtract)

            @block.scalar
            def _(act):
                act.wait_ge(dots_ready, 1)
                act.activation(dots[:, :], dots[:, :], ACT.Exp).then_inc(exp_done, 1)


def attention(nc, m, kind, scale, turns, maps, dq, dv, tiles, blocks_of, q_of, k_of, v_of, out_of):
    per = 2 if kind == "A" else 1
    jobs = [(t, mp) for t in tiles for mp in range(maps)]
    vals = jobs if per == 1 else [(t, 0) for t in tiles]
    NS, NV, NQ = len(jobs), len(vals), len(tiles)
    W = NT * P

    def runs(t):
        out = []
        for j, kt in enumerate(blocks_of(t)):
            if out and (j * P) % BANK and out[-1][1] + out[-1][2] == kt:
                out[-1][2] += 1
            else:
                out.append([j * P, kt, 1])
        return out

    with Stage(nc, f"at{kind}") as s:
        wq_ = dq if maps == 1 else 2 * dq
        q_in, k_in = s.sb("q_in", [P, NQ, wq_]), s.sb("k_in", [P, NT, wq_])
        qT, kT = s.sb("qT", [P, NQ * P]), s.sb("kT", [P, TOK])
        probs = s.sb("probs", [P, 4, W])
        probsT = s.sb("probsT", [P, 2, W])
        top, bias, den, rec = (s.sb(x, [P, 4]) for x in ("top", "bias", "den", "rec"))
        if kind == "A":
            mixed = s.sb("mixed", [P, 2, W])
            mixed_ready = s.sems("mixed_ready", 2)
        if kind == "B":
            sunk = s.sb("sunk", [P, 4])
        staged, q_turned, k_turned, q_ready, k_ready = (s.sem(x) for x in (
            "staged", "q_turned", "k_turned", "q_ready", "k_ready"))
        scored, biased, exped = s.sems("scored", 2), s.sems("biased", 2), s.sems("exped", 2)
        probs_turned, probsT_ready = s.sem("probs_turned"), s.sem("probsT_ready")
        valued, taken = s.sems("valued", 2), s.sems("taken", 2)

        def width(n):
            return len(blocks_of(jobs[n][0])) * P

        def score_bank(n):
            return m.ps[:, 2 * (n % 2):2 * (n % 2) + 2, :].rearrange("p b c -> p (b c)")

        turn_bank = m.ps[:, 4:6, :].rearrange("p b c -> p (b c)")
        k_bank = m.ps[:, 6:8, :].rearrange("p b c -> p (b c)")

        with nc.Block() as block:
            @block.gpsimd
            def _(pool):
                with pool.Fori(0, turns) as i:
                    pool.wait_ge(k_turned, i)
                    pool.sem_inc(staged, 1)
                    pool.tensor_copy(q_in[:, :, :], q_of(pool, i))
                    for part, src in k_of(pool, i):
                        last = pool.tensor_copy(k_in[:, :, part], src)
                    last.then_inc(staged, 1)

            @block.tensor
            def _(pe):
                with pe.Fori(0, turns) as i:
                    pe.wait_ge(staged, 2 * i + 2)
                    pe.wait_ge(probsT_ready, i * NV)
                    for n in range(NQ):
                        tr = pe.transpose(turn_bank[0:wq_, n * P:(n + 1) * P], q_in[:, n, :], m.ident[:, :])
                    tr.then_inc(q_turned, 1)
                    for b in range(2):
                        pe.wait_ge(taken[b], i * (NV // 2))
                    for n in range(NT):
                        tr = pe.transpose(k_bank[0:wq_, n * P:(n + 1) * P], k_in[:, n, :], m.ident[:, :])
                    tr.then_inc(k_turned, 1)
                    pe.wait_ge(q_ready, i + 1)
                    pe.wait_ge(k_ready, i + 1)

                    def score(n):
                        t, mp = jobs[n]
                        r = slice(mp * dq, (mp + 1) * dq)
                        pe.wait_ge(exped[n % 2], i * (NS // 2) + n // 2)
                        for c, kt, cnt in runs(t):
                            mm = pe.matmul(score_bank(n)[:, c:c + cnt * P], qT[r, tiles.index(t) * P:(tiles.index(t) + 1) * P],
                                           kT[r, kt * P:(kt + cnt) * P], start=True, stop=True)
                        mm.then_inc(scored[n % 2], 1)

                    def turn(v):
                        if per == 2:
                            pe.wait_ge(mixed_ready[v % 2], i * (NV // 2) + v // 2 + 1)
                            src = mixed[:, v % 2, :]
                        else:
                            pe.wait_ge(exped[v % 2], i * (NS // 2) + v // 2 + 1)
                            src = probs[:, v % 4, :]
                        pe.wait_ge(probsT_ready, i * NV + v)
                        for j in range(len(blocks_of(vals[v][0]))):
                            tr = pe.transpose(turn_bank[:, j * P:(j + 1) * P], src[:, j * P:(j + 1) * P], m.ident[:, :])
                        tr.then_inc(probs_turned, 1)

                    def value(v):
                        pe.wait_ge(probsT_ready, i * NV + v + 1)
                        pe.wait_ge(taken[v % 2], i * (NV // 2) + v // 2)
                        bl = blocks_of(vals[v][0])
                        for j, kt in enumerate(bl):
                            mm = pe.matmul(m.ps[:, 6 + v % 2, 0:dv], probsT[:, v % 2, j * P:(j + 1) * P],
                                           v_of(pe, i, kt), start=(j == 0), stop=(j == len(bl) - 1))
                        mm.then_inc(valued[v % 2], 1)

                    for n in range(per):
                        score(n)
                    for v in range(NV):
                        for n in range((v + 1) * per, min((v + 2) * per, NS)):
                            score(n)
                        turn(v)
                        if v:
                            value(v - 1)
                    value(NV - 1)

            @block.vector
            def _(dve):
                with dve.Fori(0, turns) as i:
                    dve.wait_ge(k_turned, i + 1)
                    dve.tensor_copy(kT[0:wq_, :], k_bank[0:wq_, 0:TOK]).then_inc(k_ready, 1)

                    def find_max(n):
                        t, mp = jobs[n]
                        sl = slice(n % 4, n % 4 + 1)
                        dve.wait_ge(scored[n % 2], i * (NS // 2) + n // 2 + 1)
                        if kind == "B" and t >= CT:
                            for j, kt in enumerate(blocks_of(t)):
                                if kt >= CT and kt != t:
                                    cols = score_bank(n)[:, j * P:(j + 1) * P]
                                    dve.tensor_tensor(cols, cols, m.band[:, 0 if kt < t else 1, :], ALU.add)
                            dve.drain()
                        dve.tensor_reduce(top[:, sl], score_bank(n)[:, 0:width(n)], AX.X, ALU.max)
                        dve.drain()
                        if kind == "B":
                            b = dve.tensor_scalar(bias[:, sl], top[:, sl], -scale, m.neg_sink[:, ds(i * 2 + mp, 1)],
                                                  ALU.mult, ALU.min)
                        else:
                            b = dve.tensor_scalar(bias[:, sl], top[:, sl], -scale, None, ALU.mult)
                        b.then_inc(biased[n % 2], 1)

                    def mix(v):
                        for b in range(2):
                            dve.wait_ge(exped[b], i * (NS // 2) + v + 1)
                        c0 = (2 * v) % 4
                        w = width(2 * v)
                        dve.reciprocal(rec[:, c0:c0 + 2], den[:, c0:c0 + 2])
                        dve.drain()
                        dve.tensor_scalar(rec[:, c0 + 1:c0 + 2], rec[:, c0 + 1:c0 + 2], m.neg_lam[:, :], None, ALU.mult)
                        dve.tensor_scalar(mixed[:, v % 2, 0:w], probs[:, c0, 0:w], rec[:, c0:c0 + 1], None, ALU.mult)
                        dve.drain()
                        dve.scalar_tensor_tensor(out=mixed[:, v % 2, 0:w], in0=probs[:, c0 + 1, 0:w],
                                                 scalar=rec[:, c0 + 1:c0 + 2], in1=mixed[:, v % 2, 0:w],
                                                 op0=ALU.mult, op1=ALU.add).then_inc(mixed_ready[v % 2], 1)

                    def take(v):
                        t, mp = vals[v]
                        sl = slice(v % 4, v % 4 + 1)
                        if per == 1:
                            dve.wait_ge(exped[v % 2], i * (NS // 2) + v // 2 + 1)
                            if kind == "B":
                                dve.tensor_tensor(den[:, sl], den[:, sl], sunk[:, sl], ALU.add)
                                dve.drain()
                            dve.reciprocal(rec[:, sl], den[:, sl])
                            dve.drain()
                        dve.wait_ge(valued[v % 2], i * (NV // 2) + v // 2 + 1)
                        src, dst = m.ps[:, 6 + v % 2, 0:dv], out_of(i, t, mp)
                        if per == 2:
                            o = dve.tensor_copy(dst, src)
                        else:
                            o = dve.tensor_scalar(dst, src, rec[:, sl], None, ALU.mult)
                        o.then_inc(taken[v % 2], 1)

                    for n in range(per):
                        find_max(n)
                    for v in range(NV):
                        if per == 2:
                            mix(v)
                        for n in range((v + 1) * per, min((v + 2) * per, NS)):
                            find_max(n)
                        if v:
                            take(v - 1)
                    take(NV - 1)

            @block.scalar
            def _(act):
                with act.Fori(0, turns) as i:
                    act.wait_ge(q_turned, i + 1)
                    act.copy(qT[0:wq_, :], turn_bank[0:wq_, 0:NQ * P]).then_inc(q_ready, 1)

                    def exponential(n):
                        mp = jobs[n][1]
                        sl = slice(n % 4, n % 4 + 1)
                        act.wait_ge(biased[n % 2], i * (NS // 2) + n // 2 + 1)
                        e = act.activation(probs[:, n % 4, 0:width(n)], score_bank(n)[:, 0:width(n)], ACT.Exp,
                                           bias=bias[:, sl], scale=scale, accum_out=den[:, sl])
                        if kind == "B":
                            e = act.activation(sunk[:, sl], m.sink[:, ds(i * 2 + mp, 1)], ACT.Exp, bias=bias[:, sl])
                        e.then_inc(exped[n % 2], 1)

                    def copy_turned(v):
                        w = len(blocks_of(vals[v][0])) * P
                        act.wait_ge(probs_turned, i * NV + v + 1)
                        act.copy(probsT[:, v % 2, 0:w], turn_bank[:, 0:w]).then_inc(probsT_ready, 1)

                    for n in range(per):
                        exponential(n)
                    for v in range(NV):
                        for n in range((v + 1) * per, min((v + 2) * per, NS)):
                            exponential(n)
                        copy_turned(v)


def differential_attention(nc, m):
    attention(nc, m, "A", A_DQK ** -0.5, A_HEADS, 2, A_DQK, A_DV, list(range(NT)),
              lambda t: list(range(NT if t >= CT else CT)),
              lambda e, i: m.Z[:, :, ds(AQ + i * 2 * A_DQK, 2 * A_DQK)],
              lambda e, i: [(slice(0, 2 * A_DQK), m.Z[:, :, ds(AK + i * 2 * A_DQK, 2 * A_DQK)])],
              lambda e, i, kt: m.Z[:, kt, ds(AV + i * A_DV, A_DV)],
              lambda i, t, mp: m.H[:, t, ds(i * A_DV, A_DV)])


def windowed_attention(nc, m):
    def blocks_of(t):
        if t < CT:
            return list(range(CT))
        return list(range(CT)) + list(range(max(t - 1, CT), min(t + 1, NT - 1) + 1))

    def kv(e, i):
        return e.snap(i // 2)

    def k_of(e, i):
        src = m.Z[:, :, ds(kv(e, i) * B_DH + BK, B_DH)]
        return [(slice(0, B_DH), src), (slice(B_DH, 2 * B_DH), src)]

    attention(nc, m, "B", B_DH ** -0.5, B_HEADS // 2, 2, B_DH, B_DH, list(range(NT)), blocks_of,
              lambda e, i: m.Z[:, :, ds(BQ + i * 2 * B_DH, 2 * B_DH)], k_of,
              lambda e, i, kt: m.Z[:, kt, ds(kv(e, i) * B_DH + BV, B_DH)],
              lambda i, t, mp: m.H[:, t, ds(A_HEADS * A_DV + (i * 2 + mp) * B_DH, B_DH)])


def latent_up(nc, m, a):
    QW, KVW, GW = C_HEADS * C_DQ, C_HEADS * (C_NOPE + C_DV), 2 * G_HEADS * G_DK
    with Stage(nc, "up") as s:
        wq, wkv, wg = s.sb("wq", [P, 2, QW]), s.sb("wkv", [P, KVW]), s.sb("wg", [2 * G_RANK, GW])
        gate_bias = s.sb("gate_bias", [P, GW])
        lat = s.sb("lat", [P, 2, 4, P])
        cleared, loaded = s.sem("cleared"), s.sem("loaded")
        turned, lat_ready = s.sem("turned"), s.sem("lat_ready")
        upped, act_taken, dve_taken = s.sem("upped"), s.sem("act_taken"), s.sem("dve_taken")
        with nc.Block() as block:
            @block.sync
            def _(sp):
                half = GW // 2
                sp.wait_ge(cleared, 1)
                sp.dma_start(wg[0:G_RANK, 0:half], a["d_wg_f"][0]).then_inc(loaded, 16)
                sp.dma_start(wg[G_RANK:2 * G_RANK, half:GW], a["d_wg_b"][0]).then_inc(loaded, 16)
                sp.dma_start(gate_bias[:, 0:half], rows(a["d_bg_f"])).then_inc(loaded, 16)
                sp.dma_start(gate_bias[:, half:GW], rows(a["d_bg_b"])).then_inc(loaded, 16)
                sp.dma_start(wq[:, :, :], a["c_wq_up"][0].rearrange("(k p) n -> p k n", p=P)).then_inc(loaded, 16)
                sp.dma_start(wkv[:, :], a["c_wkv_up"][0]).then_inc(loaded, 16)

            @block.tensor
            def _(pe):
                def turn(t):
                    if t >= 2:
                        pe.wait_ge(lat_ready, t - 1)
                    cols = [CKV, GF] + ([CQ, CQ + P] if t >= CT else [])
                    for n, c in enumerate(cols):
                        w = 2 * G_RANK if c == GF else P
                        tr = pe.transpose(m.ps[0:w, t % 2, n * P:(n + 1) * P], m.Z[:, t, c:c + w], m.ident[:, :])
                    tr.then_inc(turned, 1)

                def up(t):
                    pe.wait_ge(lat_ready, t + 1)
                    if t >= 1:
                        pe.wait_ge(act_taken, t)
                        pe.wait_ge(dve_taken, t)
                    for h in range(2):
                        mm = pe.matmul(m.ps[:, 2 + h, :], lat[:, t % 2, 0, :], wkv[:, h * BANK:(h + 1) * BANK], start=True, stop=True)
                    mm = pe.matmul(m.ps[:, 4, :], lat[0:2 * G_RANK, t % 2, 1, :], wg[:, :], start=True, stop=True)
                    if t >= CT:
                        for c, w in ((0, BANK), (BANK, QW - BANK)):
                            for k in range(2):
                                mm = pe.matmul(m.ps[:, 6 + c // BANK, 0:w], lat[:, t % 2, 2 + k, :], wq[:, k, c:c + w],
                                               start=(k == 0), stop=(k == 1))
                    mm.then_inc(upped, 1)

                pe.wait_ge(loaded, 96)
                for t in range(NT):
                    turn(t)
                    if t:
                        up(t - 1)
                up(NT - 1)

            @block.scalar
            def _(act):
                def take(t):
                    act.wait_ge(upped, t + 1)
                    c = act.copy(m.KV[:, t, :], m.ps[:, 2:4, :].rearrange("p b c -> p (b c)"))
                    if t >= CT:
                        c = act.copy(m.Q[:, t - CT, :], m.ps[:, 6:8, :].rearrange("p b c -> p (b c)")[:, 0:QW])
                    c.then_inc(act_taken, 1)

                for t in range(NT):
                    act.wait_ge(turned, t + 1)
                    n = 4 if t >= CT else 1
                    act.copy(lat[0:2 * G_RANK, t % 2, 1, :], m.ps[0:2 * G_RANK, t % 2, P:2 * P])
                    if t >= CT:
                        act.copy(lat[:, t % 2, 2:4, :].rearrange("p k c -> p (k c)"), m.ps[:, t % 2, 2 * P:4 * P])
                    act.copy(lat[:, t % 2, 0, :], m.ps[:, t % 2, 0:P]).then_inc(lat_ready, 1)
                    if t:
                        take(t - 1)
                take(NT - 1)

            @block.vector
            def _(dve):
                dve.memset(wg[:, :], 0.0).then_inc(cleared, 1)
                dve.wait_ge(loaded, 96)
                for t in range(NT):
                    dve.wait_ge(upped, t + 1)
                    dve.tensor_tensor(m.LG[:, t, :], m.ps[:, 4, :], gate_bias[:, :], ALU.add).then_inc(dve_taken, 1)

            @block.gpsimd
            def _(pool):
                for t in range(NT):
                    pool.wait_ge(act_taken, t + 1)
                    kh = m.K[:, t, :].rearrange("p (h d) -> p h d", d=C_DQ)
                    pool.tensor_copy(kh[:, :, 0:C_NOPE], m.KV[:, t, :].rearrange("p (h d) -> p h d", h=C_HEADS)[:, :, 0:C_NOPE])
                    pool.tensor_copy(kh[:, :, C_NOPE:C_DQ], m.Z[:, t, KPE:KPE + C_ROPE].unsqueeze(1)
                                     .broadcast_to([P, C_HEADS, C_ROPE]))


def latent_attention(nc, m):
    KVD = C_NOPE + C_DV
    attention(nc, m, "C", C_DQ ** -0.5, C_HEADS, 1, C_DQ, C_DV, list(range(CT, NT)), lambda t: list(range(NT)),
              lambda e, i: m.Q[:, :, ds(i * C_DQ, C_DQ)],
              lambda e, i: [(slice(0, C_DQ), m.K[:, :, ds(i * C_DQ, C_DQ)])],
              lambda e, i, kt: m.KV[:, kt, ds(i * KVD + C_NOPE, C_DV)],
              lambda i, t, mp: m.H[:, t, ds(i * C_DV, C_DV)])


def linear_attention(nc, m, a):
    KW = G_HEADS * G_DK
    W = 2 * KW
    NCH = NT * P // G_CHUNK
    CCH, XCH = CT * 2, XT * 2
    VW = G_HEADS * G_DV
    with ExitStack() as ctx:
        sb = lambda name, shape: ctx.enter_context(nc.sbuf_tensor("gla_" + name, shape, F32))
        tri = sb("tri", [P, 3, P])
        qT, kT = sb("qT", [P, 4, XT * P]), sb("kT", [P, 4, XT * P])
        decay = sb("decay", [P, 4, NCH])
        state = sb("state", [P, 2, NCH + 1, 2 * G_DV])

        with Stage(nc, "gg") as s:
            one = s.sb("one", [P, 1])
            soft = s.sb("soft", [P, NT, W])
            loaded, one_ready, soft_ready = s.sem("loaded"), s.sem("one_ready"), s.sem("soft_ready")
            with nc.Block() as block:
                @block.sync
                def _(sp):
                    sp.dma_start(tri[:, :, :], a["tri"].rearrange("s p c -> p s c")).then_inc(loaded, 16)
                    sp.wait_ge(loaded, 16)

                @block.scalar
                def _(act):
                    act.wait_ge(one_ready, 1)
                    act.activation(soft[:, :, :], m.LG[:, :, :], ACT.Abs)
                    act.drain()
                    act.activation(soft[:, :, :], soft[:, :, :], ACT.Exp, scale=-1.0)
                    act.drain()
                    act.activation(soft[:, :, :], soft[:, :, :], ACT.Ln, bias=one[:, :]).then_inc(soft_ready, 1)

                @block.vector
                def _(dve):
                    dve.memset(one[:, :], 1.0).then_inc(one_ready, 1)
                    dve.wait_ge(soft_ready, 1)
                    dve.scalar_tensor_tensor(out=m.LG[:, :, :], in0=m.LG[:, :, :], scalar=0.0, in1=soft[:, :, :],
                                             op0=ALU.min, op1=ALU.subtract)
                    dve.drain()
                    dve.tensor_scalar(m.LG[:, :, :], m.LG[:, :, :], 1.0 / G_TAU, None, ALU.mult)

        with Stage(nc, "gs") as s:
            up, down, stay = (s.sb(x, [P, 2, W]) for x in ("up", "down", "stay"))
            summed, exped, diffed = s.sem("summed"), s.sem("exped"), s.sem("diffed")
            stay_ready, scaled, banks_free = s.sem("stay_ready"), s.sem("scaled"), s.sem("banks_free")
            turned, copied = s.sem("turned"), s.sem("copied")
            with nc.Block() as block:
                @block.tensor
                def _(pe):
                    def turn(t):
                        x = t - CT
                        pe.wait_ge(scaled, t + 1)
                        if x >= 1:
                            pe.wait_ge(copied, x)
                        for n in range(4):
                            tr = pe.transpose(m.ps[:, 4, n * P:(n + 1) * P], up[:, t % 2, n * P:(n + 1) * P], m.ident[:, :])
                            tr = pe.transpose(m.ps[:, 5, n * P:(n + 1) * P], down[:, t % 2, n * P:(n + 1) * P], m.ident[:, :])
                        tr.then_inc(turned, 1)

                    for t in range(NT):
                        if t >= 1:
                            pe.wait_ge(banks_free, t)
                            pe.wait_ge(exped, t)
                        for d in range(2):
                            pe.matmul(m.ps[:, 0, d * KW:(d + 1) * KW], tri[:, d, :], m.LG[:, t, d * KW:(d + 1) * KW],
                                      start=True, stop=True)
                        pe.matmul(m.ps[:, 1, :], tri[:, 2, :], m.LG[:, t, :], start=True, stop=True)
                        for n in range(4):
                            mm = pe.matmul(m.ps[:, 2, 2 * n:2 * n + 2], m.LG[:, t, n * P:(n + 1) * P],
                                           tri[:, 2, 0:P:G_CHUNK], start=True, stop=True)
                        mm.then_inc(summed, 1)
                        if t > CT:
                            turn(t - 1)
                    turn(NT - 1)

                def copy(act, t):
                    x = t - CT
                    act.wait_ge(turned, x + 1)
                    act.copy(qT[:, :, x * P:(x + 1) * P], m.ps[:, 4, :].rearrange("p (n c) -> p n c", c=P))
                    act.copy(kT[:, :, x * P:(x + 1) * P], m.ps[:, 5, :].rearrange("p (n c) -> p n c", c=P)).then_inc(copied, 1)

                @block.scalar
                def _(act):
                    for t in range(NT):
                        act.wait_ge(summed, t + 1)
                        if t >= 2:
                            act.wait_ge(scaled, t - 1)
                            if t - 2 >= CT:
                                act.wait_ge(turned, t - 1 - CT)
                        act.activation(up[:, t % 2, :], m.ps[:, 0, :], ACT.Exp)
                        act.activation(down[:, t % 2, :], m.ps[:, 0, :], ACT.Exp, scale=-1.0)
                        act.activation(decay[:, :, 2 * t:2 * t + 2],
                                       m.ps[:, 2, 0:8].rearrange("p (n c) -> p n c", c=2), ACT.Exp).then_inc(exped, 1)
                        act.wait_ge(diffed, t + 1)
                        act.activation(stay[:, t % 2, :], stay[:, t % 2, :], ACT.Exp).then_inc(stay_ready, 1)
                        if t > CT:
                            copy(act, t - 1)
                    copy(act, NT - 1)

                @block.vector
                def _(dve):
                    for t in range(NT):
                        dve.wait_ge(exped, t + 1)
                        dve.tensor_copy(stay[:, t % 2, :], m.ps[:, 0, :])
                        dve.drain()
                        dve.tensor_tensor(stay[:, t % 2, :], m.ps[:, 1, :], stay[:, t % 2, :], ALU.subtract)
                        dve.drain()
                        dve.sem_inc(diffed, 1)
                        dve.sem_inc(banks_free, 1)
                        k2 = m.Z[:, t, DK:DK + KW].unsqueeze(1).broadcast_to([P, 2, KW])
                        q2 = m.Z[:, t, DQ:DQ + KW].unsqueeze(1).broadcast_to([P, 2, KW])
                        both = lambda x: x[:, t % 2, :].rearrange("p (d n) -> p d n", d=2)
                        if t >= CT:
                            dve.scalar_tensor_tensor(out=both(up), in0=both(up), scalar=G_DK ** -0.5, in1=q2,
                                                     op0=ALU.mult, op1=ALU.mult)
                            dve.tensor_tensor(both(down), both(down), k2, ALU.mult)
                        dve.wait_ge(stay_ready, t + 1)
                        dve.tensor_tensor(m.LG[:, t, :].rearrange("p (d n) -> p d n", d=2), both(stay), k2,
                                          ALU.mult).then_inc(scaled, 1)

        def chunk_at(d, n):
            if d == 0:
                return n
            return CCH - 1 - n if n < CCH else CCH + XCH - 1 - (n - CCH)

        with Stage(nc, "gc") as s:
            kv_done, bank_read = s.sems("kv_done", 4), s.sems("bank_read", 4)
            with nc.Block() as block:
                @block.tensor
                def _(pe):
                    for n in range(NCH - 1):
                        for d in range(2):
                            b, use = (2 * n + d) % 4, (2 * n + d) // 4
                            c = chunk_at(d, n)
                            r = slice((c % 2) * G_CHUNK, (c % 2 + 1) * G_CHUNK)
                            pe.wait_ge(bank_read[b], use)
                            for pair in range(2):
                                at = d * KW + pair * P
                                mm = pe.matmul(m.ps[:, b, pair * 2 * G_DV:(pair + 1) * 2 * G_DV], m.LG[r, c // 2, at:at + P],
                                               m.Z[r, c // 2, DV + pair * 2 * G_DV:DV + (pair + 1) * 2 * G_DV],
                                               start=True, stop=True)
                            mm.then_inc(kv_done[b], 1)

                @block.vector
                def _(dve):
                    dve.memset(state[:, :, 0, :], 0.0)
                    dve.drain()
                    for n in range(NCH - 1):
                        for d in range(2):
                            b, use = (2 * n + d) % 4, (2 * n + d) // 4
                            c = chunk_at(d, n)
                            dve.wait_ge(kv_done[b], use + 1)
                            for h in range(G_HEADS):
                                pair, r = h // 2, slice((h % 2) * G_DK, (h % 2 + 1) * G_DK)
                                cols = slice(pair * G_DV, (pair + 1) * G_DV)
                                upd = dve.scalar_tensor_tensor(
                                    out=state[r, d, n + 1, cols], in0=state[r, d, n, cols],
                                    scalar=decay[r, 2 * d + pair, c:c + 1],
                                    in1=m.ps[r, b, h * G_DV:(h + 1) * G_DV], op0=ALU.mult, op1=ALU.add)
                            upd.then_inc(bank_read[b], 1)
                        dve.drain()

        with Stage(nc, "go") as s:
            within = s.sb("within", [P, 2, 2, P])
            cleared = s.sem("cleared")
            products, masked = s.sems("products", 4), s.sems("masked", 4)
            o_done, o_taken = s.sems("o_done", 2), s.sems("o_taken", 2)
            units = [(x, h, d) for x in range(XT) for h in range(G_HEADS) for d in range(2)]
            with nc.Block() as block:
                @block.tensor
                def _(pe):
                    def product(u):
                        x, h, d = units[u]
                        r = slice((h % 2) * G_DK, (h % 2 + 1) * G_DK)
                        n, cols = 2 * d + h // 2, slice(x * P, (x + 1) * P)
                        pe.wait_ge(masked[u % 4], u // 4)
                        pe.matmul(m.ps[:, 4 + u % 4, 0:P], kT[r, n, cols], qT[r, n, cols], start=True, stop=True)\
                            .then_inc(products[u % 4], 1)

                    def output(u):
                        x, h, d = units[u]
                        r = slice((h % 2) * G_DK, (h % 2 + 1) * G_DK)
                        n, cols = 2 * d + h // 2, slice(h // 2 * G_DV, (h // 2 + 1) * G_DV)
                        bank = 2 * (x % 2) + h % 2
                        if h == 0 and d == 0:
                            pe.wait_ge(o_taken[x % 2], x // 2)
                        pe.wait_ge(masked[u % 4], u // 4 + 1)
                        pe.matmul(m.ps[:, bank, cols], within[:, d, (u // 2) % 2, :],
                                  m.Z[:, CT + x, DV + h * G_DV:DV + (h + 1) * G_DV], start=(d == 0), stop=False,
                                  skip_group_check=True)
                        for c in range(2):
                            chunk = 2 * x + c
                            step = CCH + (chunk if d == 0 else XCH - 1 - chunk)
                            tok = slice(x * P + c * G_CHUNK, x * P + (c + 1) * G_CHUNK)
                            mm = pe.matmul(m.ps[c * G_CHUNK:(c + 1) * G_CHUNK, bank, cols], qT[r, n, tok],
                                           state[r, d, step, (h // 2) * G_DV:(h // 2 + 1) * G_DV],
                                           start=False, stop=(d == 1), skip_group_check=True)
                        if h == G_HEADS - 1 and d == 1:
                            mm.then_inc(o_done[x % 2], 1)

                    product(0)
                    product(1)
                    for u in range(len(units)):
                        if u + 2 < len(units):
                            product(u + 2)
                        output(u)

                @block.vector
                def _(dve):
                    dve.memset(within[:, :, :, :], 0.0)
                    dve.drain()
                    for u, (x, h, d) in enumerate(units):
                        dve.wait_ge(products[u % 4], u // 4 + 1)
                        dve.copy_predicated(within[:, d, (u // 2) % 2, :], tri[:, d, :].bitcast(U32),
                                            m.ps[:, 4 + u % 4, 0:P]).then_inc(masked[u % 4], 1)

                @block.scalar
                def _(act):
                    for x in range(XT):
                        act.wait_ge(o_done[x % 2], x // 2 + 1)
                        act.copy(m.H[:, CT + x, C_HEADS * C_DV:D].rearrange("p (a b v) -> p b a v", b=2, v=G_DV),
                                 m.ps[:, 2 * (x % 2):2 * (x % 2) + 2, 0:2 * G_DV].rearrange("p b (a v) -> p b a v", v=G_DV))\
                            .then_inc(o_taken[x % 2], 1)

        head_norm(nc, m, a, "gn1", m.H, range(CT, NT), [(C_HEADS * C_DV, G_HEADS, G_DV, a["d_gn"])])
        with Stage(nc, "gr") as s:
            den = s.sb("den", [P, XT, VW])
            exped = s.sem("exped")
            with nc.Block() as block:
                @block.scalar
                def _(act):
                    act.activation(den[:, :, :], m.Z[:, CT:NT, DR:DR + VW], ACT.Exp, scale=-1.0).then_inc(exped, 1)

                @block.vector
                def _(dve):
                    dve.wait_ge(exped, 1)
                    dve.tensor_scalar(den[:, :, :], den[:, :, :], 1.0, None, ALU.add)
                    dve.drain()
                    dve.reciprocal(den[:, :, :], den[:, :, :])
                    dve.drain()
                    dve.tensor_tensor(den[:, :, :], den[:, :, :], m.Z[:, CT:NT, DR:DR + VW], ALU.mult)
                    dve.drain()
                    out = m.H[:, CT:NT, C_HEADS * C_DV:D]
                    dve.tensor_tensor(out, out, den[:, :, :], ALU.mult)


def expert_scores(nc, m, a, layer, tiles):
    NH, HALF = 2 * PH, len(tiles) * P // 2
    t0, PER = tiles[0], 8
    with Stage(nc, f"es{layer}") as s:
        keys, keysT = s.sb("keys", [P, NH, P]), s.sb("keysT", [P, NH, P])
        w = s.sb("w", [P, 2, KC, BANK])
        qT = s.sb("qT", [P, 2, 2, HALF])
        keys_loaded, keys_turned, keysT_ready = s.sem("keys_loaded"), s.sem("keys_turned"), s.sem("keysT_ready")
        loaded, used = s.sems("loaded", 2), s.sems("used", 2)
        q_done, qT_ready = s.sems("q_done", 2), s.sems("qT_ready", 2)
        scored, taken = s.sems("scored", 2), s.sems("taken", 2)
        with nc.Block() as block:
            @block.sync
            def _(sp):
                sp.dma_start(keys[:, :, :], a["p_keys"][layer].rearrange("h s n d -> n (h s) d")).then_inc(keys_loaded, 16)
                with sp.Fori(0, NH // PER) as i:
                    for q in range(2):
                        sp.wait_ge(used[q], i)
                        sp.dma_start(w[:, q], a["p_wq"][layer][:, ds((i * 2 + q) * BANK, BANK)]
                                     .rearrange("(k p) n -> p k n", p=P)).then_inc(loaded[q], 16)

            @block.tensor
            def _(pe):
                pe.wait_ge(keys_loaded, 16)
                for h in range(NH):
                    tr = pe.transpose(m.ps[:, h // 4, (h % 4) * P:(h % 4 + 1) * P], keys[:, h, :], m.ident[:, :])
                tr.then_inc(keys_turned, 1)
                pe.wait_ge(keysT_ready, 1)
                with pe.Fori(0, NH // PER) as i:
                    def query(h):
                        b, use = h % 2, i * (PER // 2) + h // 2
                        if h % 4 == 0:
                            pe.wait_ge(loaded[h // 4], i * 16 + 16)
                        pe.wait_ge(qT_ready[b], use)
                        for half in range(2):
                            for k in range(KC):
                                mm = pe.matmul(m.ps[:, 2 * b + half, 0:HALF], w[:, h // 4, k, (h % 4) * P:(h % 4 + 1) * P],
                                               m.hT[:, k, t0 * P + half * HALF:t0 * P + (half + 1) * HALF],
                                               start=(k == 0), stop=(k == KC - 1))
                        mm.then_inc(q_done[b], 1)
                        if h % 4 == 3:
                            pe.drain()
                            pe.sem_inc(used[h // 4], 1)

                    def score(h):
                        b, use = h % 2, i * (PER // 2) + h // 2
                        pe.wait_ge(qT_ready[b], use + 1)
                        pe.wait_ge(taken[b], use)
                        for n in range(len(tiles)):
                            mm = pe.matmul(m.ps[:, 4 + 2 * b + n // 4, (n % 4) * P:(n % 4 + 1) * P],
                                           qT[:, b, :, :].rearrange("p a c -> p (a c)")[:, n * P:(n + 1) * P],
                                           keysT[:, ds(i * PER + h, 1), :].rearrange("p o n -> p (o n)"),
                                           start=True, stop=True)
                        mm.then_inc(scored[b], 1)

                    for h in range(PER):
                        query(h)
                        if h:
                            score(h - 1)
                    score(PER - 1)

            @block.scalar
            def _(act):
                act.wait_ge(keys_turned, 1)
                act.copy(keysT[:, :, :].rearrange("p h n -> p (h n)"),
                         m.ps[:, 0:4, :].rearrange("p b c -> p (b c)")).then_inc(keysT_ready, 1)
                with act.Fori(0, NH // PER) as i:
                    for h in range(PER):
                        b, use = h % 2, i * (PER // 2) + h // 2
                        act.wait_ge(q_done[b], use + 1)
                        act.wait_ge(scored[b], use)
                        act.copy(qT[:, b, :, :], m.ps[:, 2 * b:2 * b + 2, 0:HALF]).then_inc(qT_ready[b], 1)

            @block.vector
            def _(dve):
                with dve.Fori(0, NH // PER) as i:
                    for h in range(PER):
                        b, use = h % 2, i * (PER // 2) + h // 2
                        dve.wait_ge(scored[b], use + 1)
                        src = m.ps[:, 4 + 2 * b:6 + 2 * b, :].rearrange("p b (t n) -> p (b t) n", n=P)
                        dve.tensor_copy(m.scores[:, t0:NT, ds((i * PER + h) * P, P)], src[:, 0:len(tiles), :])\
                            .then_inc(taken[b], 1)


def choose_experts(nc, m, a, layer, tiles):
    NH, T, t0 = 2 * PH, len(tiles), tiles[0]
    LOW = -3.0e38
    with Stage(nc, f"ce{layer}") as s:
        sc, rest = s.sb("sc", [P, NH, NK]), s.sb("rest", [P, NH, NK])
        val, pos, posf = s.sb("val", [P, NH, TOPK]), s.sb("pos", [P, NH, TOPK], U32), s.sb("posf", [P, NH, TOPK])
        cand, left = s.sb("cand", [P, PH, TOPK * TOPK]), s.sb("left", [P, PH, TOPK * TOPK])
        best, at_ = s.sb("best", [P, PH, TOPK]), s.sb("at", [P, PH, TOPK], U32)
        part, partf = s.sb("part", [P, 2, SLOTS], U32), s.sb("partf", [P, 2, SLOTS])
        iota = s.sb("iota", [P, TOPK])
        hot = s.sb("hot", [P, 2, SLOTS, TOPK])
        num, expert = s.sb("num", [P, 2, SLOTS]), s.sb("expert", [P, SLOTS])
        total = s.sb("total", [P, PH])
        loaded, sc_ready, sc_claimed, sc_read = s.sem("loaded"), s.sem("sc_claimed"), s.sem("sc_ready"), s.sem("sc_read")
        shifted, exped = s.sem("shifted"), s.sem("exped")

        def top16(dve, n, values, src, spare, index):
            for h in range(n):
                dve.max(values[:, h, 0:8], src[:, h, :])
            dve.drain()
            for h in range(n):
                dve.max_index(index[:, h, 0:8], values[:, h, 0:8], src[:, h, :])
                dve.match_replace(spare[:, h, :], values[:, h, 0:8], src[:, h, :], LOW)
            dve.drain()
            for h in range(n):
                dve.max(values[:, h, 8:16], spare[:, h, :])
            dve.drain()
            for h in range(n):
                dve.max_index(index[:, h, 8:16], values[:, h, 8:16], spare[:, h, :])
            dve.drain()

        with nc.Block() as block:
            @block.sync
            def _(sp):
                sp.dma_start(iota[:, :], rows(a["iota"])).then_inc(loaded, 16)

            @block.scalar
            def _(act):
                with act.Fori(0, T) as i:
                    act.wait_ge(sc_read, i)
                    act.sem_inc(sc_ready, 1)
                    act.copy(sc[:, :, :].rearrange("p h n -> p (h n)"), m.scores[:, i + t0, :]).then_inc(sc_ready, 1)
                    act.wait_ge(shifted, i + 1)
                    act.activation(best[:, :, :], best[:, :, :], ACT.Exp).then_inc(exped, 1)

            @block.vector
            def _(dve):
                dve.wait_ge(loaded, 16)
                with dve.Fori(0, T) as i:
                    dve.wait_ge(sc_ready, 2 * i + 2)
                    dve.sem_inc(sc_claimed, 1)
                    top16(dve, NH, val, sc, rest, pos)
                    dve.sem_inc(sc_read, 1)
                    dve.tensor_copy(posf[:, :, :], pos[:, :, :])
                    pairs = val[:, :, :].rearrange("p (h s) k -> p h s k", s=2)
                    dve.tensor_tensor(cand[:, :, :].rearrange("p h (i j) -> p h i j", j=TOPK),
                                      pairs[:, :, 0, :].unsqueeze(3).broadcast_to([P, PH, TOPK, TOPK]),
                                      pairs[:, :, 1, :].unsqueeze(2).broadcast_to([P, PH, TOPK, TOPK]), ALU.add)
                    dve.drain()
                    top16(dve, PH, best, cand, left, at_)
                    flat = at_[:, :, :].rearrange("p h k -> p (h k)")
                    dve.tensor_scalar(part[:, 0, :], flat, 4, None, ALU.logical_shift_right)
                    dve.tensor_scalar(part[:, 1, :], flat, TOPK - 1, None, ALU.bitwise_and)
                    dve.tensor_tensor(left[:, :, 0:TOPK], best[:, :, :],
                                      best[:, :, 0:1].broadcast_to([P, PH, TOPK]), ALU.subtract)
                    dve.drain()
                    dve.tensor_copy(best[:, :, :], left[:, :, 0:TOPK])
                    dve.tensor_copy(partf[:, :, :], part[:, :, :])
                    dve.drain()
                    dve.sem_inc(shifted, 1)
                    for half in range(2):
                        dve.tensor_tensor(hot[:, half], iota[:, :].unsqueeze(1).broadcast_to([P, SLOTS, TOPK]),
                                          partf[:, half, :].unsqueeze(2).broadcast_to([P, SLOTS, TOPK]), ALU.is_equal)
                    dve.drain()
                    halves = posf[:, :, :].rearrange("p (h s) k -> p h s k", s=2)
                    for half in range(2):
                        h4 = hot[:, half].rearrange("p (h k) i -> p h k i", k=TOPK)
                        dve.tensor_tensor(h4, h4, halves[:, :, half, :].unsqueeze(2).broadcast_to([P, PH, TOPK, TOPK]), ALU.mult)
                    dve.drain()
                    dve.tensor_reduce(num[:, :, :], hot[:, :, :, :], AX.X, ALU.add)
                    dve.drain()
                    dve.scalar_tensor_tensor(out=expert[:, :], in0=num[:, 0, :], scalar=float(NK), in1=num[:, 1, :],
                                             op0=ALU.mult, op1=ALU.add)
                    dve.drain()
                    dve.tensor_scalar(m.expert[:, ds((i + t0) * SLOTS, SLOTS)], expert[:, :], float(layer * NK * NK),
                                      None, ALU.add)
                    dve.wait_ge(exped, i + 1)
                    dve.tensor_reduce(total[:, :], best[:, :, :], AX.X, ALU.add)
                    dve.drain()
                    dve.reciprocal(total[:, :], total[:, :])
                    dve.drain()
                    dve.tensor_tensor(m.gates[:, ds((i + t0) * SLOTS, SLOTS)].rearrange("p (h k) -> p h k", k=TOPK),
                                      best[:, :, :], total[:, :].unsqueeze(2).broadcast_to([P, PH, TOPK]), ALU.mult)
                    dve.drain()


def run_experts(nc, m, a, layer, tiles):
    T, t0 = len(tiles), tiles[0]
    GROUPS = SLOTS // RING
    u_rows, v_rows = a["p_u"].rearrange("l e d -> (l e) d"), a["p_v"].rearrange("l e d -> (l e) d")
    with Stage(nc, f"ex{layer}") as s:
        u_ring, v_ring = s.sb("u_ring", [P, RING, D]), s.sb("v_ring", [P, RING, D])
        u_idx, v_idx = s.sb("u_idx", [P, 2, RING], U32), s.sb("v_idx", [P, 2, RING], U32)
        v_weight = s.sb("v_weight", [P, 2, RING])
        dots, product = s.sb("dots", [P, NT * SLOTS]), s.sb("product", [P, 2, D])
        act_out = s.sb("act_out", [P, SLOTS])
        diag = s.sb("diag", [P, 4, P])
        zeros = s.sb("zeros", [P, BANK], mybir.dt.bfloat16)
        zeroed = s.sem("zeroed")
        u_staged, v_staged, staging = s.sem("u_staged"), s.sem("v_staged"), s.sem("staging")
        u_claimed, v_claimed = s.sem("u_claimed"), s.sem("v_claimed")
        u_landed, u_used = s.pool_dma_sems(m, "u_landed", RING), s.sems("u_used", RING)
        v_landed, v_used = s.pool_dma_sems(m, "v_landed", RING), s.sems("v_used", RING)
        dots_ready, gelu_done, weights_ready = s.sem("dots_ready"), s.sem("gelu_done"), s.sem("weights_ready")
        diag_ready, mix_taken = s.sem("diag_ready"), s.sem("mix_taken")

        def passes(eng, step, before=None, after=None):
            def one(tu, tv):
                if before:
                    before(tu, tv)
                with eng.Fori(0, GROUPS // 2) as g:
                    for half in range(2):
                        step(None if tu is None else tu * GROUPS + g * 2 + half,
                             None if tv is None else tv * GROUPS + g * 2 + half, half, tu, tv)
                if after:
                    after(tu, tv)
            one(0, None)
            if T > 1:
                with eng.Fori(0, T - 1) as t:
                    one(t + 1, t)
            one(None, T - 1)

        with nc.Block() as block:
            @block.gpsimd
            def _(pool):
                def step(gu, gv, half, tu, tv):
                    for r in range(RING):
                        if gu is not None:
                            if r == 0:
                                pool.wait_ge(u_staged, gu + 1)
                            pool.wait_ge(u_used[r], gu)
                            pool.sem_inc(u_claimed, 1)
                            pool.indirect_dma_start(u_ring[:, r, :], None, u_rows,
                                                    bass.IndirectOffsetOnAxis(ap=u_idx[:, half, r:r + 1], axis=0),
                                                    ).then_inc(u_landed[r], 16)
                        if gv is not None:
                            if r == 0:
                                pool.wait_ge(v_staged, gv + 1)
                            pool.wait_ge(v_used[r], gv)
                            pool.sem_inc(v_claimed, 1)
                            pool.indirect_dma_start(v_ring[:, r, :], None, v_rows,
                                                    bass.IndirectOffsetOnAxis(ap=v_idx[:, half, r:r + 1], axis=0),
                                                    ).then_inc(v_landed[r], 16)
                passes(pool, step)

            @block.vector
            def _(dve):
                dve.memset(zeros[:, :], 0.0).then_inc(zeroed, 1)

                def step(gu, gv, half, tu, tv):
                    if gu is None:
                        return
                    for r in range(RING):
                        dve.wait_ge(u_landed[r], gu * 16 + 16)
                        dve.scalar_tensor_tensor(out=product[:, r % 2, :], in0=u_ring[:, r, :], scalar=1.0,
                                                 in1=m.H[:, tu + t0, :], op0=ALU.mult, op1=ALU.mult,
                                                 accum_out=dots[:, ds(gu * RING + r, 1)]).then_inc(u_used[r], 1)
                        if r % 2:
                            dve.drain()

                def after(tu, tv):
                    if tu is None:
                        return
                    dve.drain()
                    dve.sem_inc(dots_ready, 1)
                    dve.wait_ge(gelu_done, tu + 1)
                    dve.tensor_tensor(act_out[:, :], act_out[:, :], m.gates[:, ds((tu + t0) * SLOTS, SLOTS)], ALU.mult)
                    dve.drain()
                    dve.tensor_copy(dots[:, ds(tu * SLOTS, SLOTS)], act_out[:, :]).then_inc(weights_ready, 1)

                passes(dve, step, after=after)

            @block.scalar
            def _(act):
                def step(gu, gv, half, tu, tv):
                    if gu is not None:
                        for r in range(RING):
                            act.wait_ge(u_landed[r], gu * 16)
                        act.sem_inc(staging, 1)
                        act.copy(u_idx[:, half, :], m.expert[:, ds((gu + t0 * GROUPS) * RING, RING)]).then_inc(u_staged, 1)
                    if gv is not None:
                        for r in range(RING):
                            act.wait_ge(v_landed[r], gv * 16)
                        act.sem_inc(staging, 1)
                        act.copy(v_idx[:, half, :], m.expert[:, ds((gv + t0 * GROUPS) * RING, RING)]).then_inc(v_staged, 1)
                        act.copy(v_weight[:, half, :], dots[:, ds(gv * RING, RING)])
                        act.drain()
                        for r in range(RING):
                            if r < 4:
                                act.wait_ge(v_used[r + 4], gv)
                            else:
                                act.wait_ge(v_used[r - 4], gv + 1)
                            act.activation(diag[:, r % 4, :], m.ident[:, :], ACT.Copy,
                                           scale=v_weight[:, half, r:r + 1]).then_inc(diag_ready, 1)

                def before(tu, tv):
                    if tv is not None:
                        act.wait_ge(weights_ready, tv + 1)

                def after(tu, tv):
                    if tv is not None:
                        for r in range(RING):
                            act.wait_ge(v_used[r], (tv + 1) * GROUPS)
                        act.sem_inc(staging, 1)
                        act.copy(m.mix[:, tv + t0, :], m.ps[:, 0:2, :].rearrange("p b c -> p (b c)")).then_inc(mix_taken, 1)
                    if tu is not None:
                        act.wait_ge(dots_ready, tu + 1)
                        act.sem_inc(staging, 1)
                        act.activation(act_out[:, :], dots[:, ds(tu * SLOTS, SLOTS)], ACT.Gelu).then_inc(gelu_done, 1)

                passes(act, step, before=before, after=after)

            @block.tensor
            def _(pe):
                pe.wait_ge(zeroed, 1)

                def before(tu, tv):
                    if tv is None:
                        return
                    pe.wait_ge(mix_taken, tv)
                    for b in range(2):
                        pe.matmul(m.ps[:, b, :], zeros[:, 0:P], zeros[:, :], start=True, stop=False, skip_group_check=True)

                def step(gu, gv, half, tu, tv):
                    if gv is None:
                        return
                    for r in range(RING):
                        pe.wait_ge(diag_ready, gv * RING + r + 1)
                        pe.wait_ge(v_landed[r], gv * 16 + 16)
                        for b in range(2):
                            mm = pe.matmul(m.ps[:, b, :], diag[:, r % 4, :], v_ring[:, r, b * BANK:(b + 1) * BANK],
                                           start=False, stop=False, skip_group_check=True)
                        mm.then_inc(v_used[r], 1)

                passes(pe, step, before=before)


def add_experts(nc, m, layer, tiles, last):
    with Stage(nc, f"ad{layer}") as s:
        g = s.sb("g", [P, 2, D])
        loaded, scaled, added = s.sem("loaded"), s.sem("scaled"), s.sem("added")
        stored = s.sem("stored")
        with nc.Block() as block:
            @block.sync
            def _(sp):
                for st in range(2):
                    sp.dma_start(g[:, st, :], rows(m.mods[layer, st:st + 1, 5 * D:6 * D])).then_inc(loaded, 16)
                if last:
                    for n, t in enumerate(tiles):
                        sp.wait_ge(added, n + 1)
                        sp.dma_start(m.out[0, (t - CT) * P:(t - CT + 1) * P, :], m.R[:, t, :]).then_inc(stored, 16)
                    sp.wait_ge(stored, 16 * len(tiles))

            @block.vector
            def _(dve):
                dve.wait_ge(loaded, 32)
                for t in tiles:
                    dve.tensor_tensor(m.mix[:, t, :], m.mix[:, t, :], g[:, 1 if t < CT else 0, :], ALU.mult).then_inc(scaled, 1)

            @block.gpsimd
            def _(pool):
                for n, t in enumerate(tiles):
                    pool.wait_ge(scaled, n + 1)
                    pool.tensor_tensor(m.R[:, t, :], m.R[:, t, :], m.mix[:, t, :], ALU.add).then_inc(added, 1)


def experts(nc, m, a, layer, tiles, last):
    modulated_norm(nc, m, a, layer, 1, "norm2", tiles)
    with (nc.sbuf_tensor(f"expert{layer}", [P, NT * SLOTS], U32) as m.expert,
          nc.sbuf_tensor(f"gates{layer}", [P, NT * SLOTS], F32) as m.gates):
        with nc.sbuf_tensor(f"scores{layer}", [P, NT, 2 * PH * NK], F32) as m.scores:
            expert_scores(nc, m, a, layer, tiles)
            choose_experts(nc, m, a, layer, tiles)
        with nc.sbuf_tensor(f"mix{layer}", [P, NT, D], F32) as m.mix:
            run_experts(nc, m, a, layer, tiles)
            add_experts(nc, m, layer, tiles, last)


def shape_constants():
    def rope(dim, name):
        pos = np.arange(SEQ)
        axis = dim // 2
        inv = (1.0 / (THETA ** (np.arange(0, axis, 2, dtype=np.float32) / axis))).astype(np.float32)
        ang = np.concatenate([(pos // GRID_W)[:, None].astype(np.float32) * inv,
                              (pos % GRID_W)[:, None].astype(np.float32) * inv], axis=-1)
        cos = np.ones((TOK, dim), np.float32)
        sin = np.zeros((TOK, dim), np.float32)
        cos[CTX:] = np.repeat(np.cos(ang), 2, axis=1)
        sin[CTX:] = np.repeat(np.sin(ang), 2, axis=1) * np.tile([-1.0, 1.0], dim // 2)
        return {name + "_cos": cos, name + "_sin": sin}

    k, q = np.arange(P)[None, :], np.arange(P)[:, None]
    band = np.stack([np.where(k >= q, 0.0, NEG), np.where(k <= q, 0.0, NEG)]).astype(np.float32)
    s_, c_ = np.arange(P)[:, None], np.arange(P)[None, :]
    same = s_ // G_CHUNK == c_ // G_CHUNK
    tri = np.stack([same & (s_ <= c_), same & (s_ >= c_), same]).astype(np.float32)
    return {"tri": tri, "iota": np.arange(TOPK, dtype=np.float32)[None, :], "ident": np.eye(P, dtype=np.float32), "band": band} | rope(B_DH, "rope_ab") | rope(C_ROPE, "rope_c")


def program(nc, a, out):
    with ExitStack() as ctx:
        m = Memory()
        m.ctx = ctx
        m.mods = nc.dram_tensor("modulations", [2, 2, 6 * D], F32, kind="Internal").ap()
        m.R = ctx.enter_context(nc.sbuf_tensor("R", [P, NT, D], F32))
        m.H = ctx.enter_context(nc.sbuf_tensor("H", [P, NT, D], F32))
        m.hT = ctx.enter_context(nc.sbuf_tensor("hT", [P, KC, TOK], F32))
        m.ident = ctx.enter_context(nc.sbuf_tensor("ident_sb", [P, P], F32))
        m.eps = ctx.enter_context(nc.sbuf_tensor("eps", [P, 1], F32))
        m.ps = ctx.enter_context(nc.psum_tensor("ps", [P, 8, BANK], F32))
        m.neg_lam = ctx.enter_context(nc.sbuf_tensor("neg_lam", [P, 1], F32))
        m.sink = ctx.enter_context(nc.sbuf_tensor("sink", [P, B_HEADS], F32))
        m.neg_sink = ctx.enter_context(nc.sbuf_tensor("neg_sink", [P, B_HEADS], F32))
        m.band = ctx.enter_context(nc.sbuf_tensor("band_sb", [P, 2, P], F32))
        m.Z = None
        m.out = out

        load_streams(nc, m, a)
        modulation_rows(nc, m, a)
        modulated_norm(nc, m, a, 0, 0, "norm1", range(NT))
        with nc.sbuf_tensor("Z", [P, NT, EVEN_IN], F32) as m.Z:
            project(nc, m, "pin0", a["e_w_in"][0], range(NT), EVEN_IN // 6, out=m.Z)
            head_norm(nc, m, a, "qk0", m.Z, range(NT),
                      [(AQ, 2 * A_HEADS, A_DQK, a["a_qn"]), (AK, 2 * A_HEADS, A_DQK, a["a_kn"]),
                       (BQ, B_HEADS, B_DH, a["b_qn"]), (BK, B_KV, B_DH, a["b_kn"])], rope=(0, B_DH, "rope_ab"))
            lambda_and_sinks(nc, m, a)
            differential_attention(nc, m)
            windowed_attention(nc, m)
        m.Z = None
        head_norm(nc, m, a, "gn0", m.H, range(NT), [(0, A_HEADS, A_DV, a["a_gn"])], factor=1.0 - LAM_INIT)
        turn_h(nc, m, "th0", range(NT))
        project(nc, m, "pout0", a["e_w_out"][0], range(NT), BANK, gate=m.mods[0, :, 2 * D:3 * D])
        experts(nc, m, a, 0, range(NT), False)

        XTILES = range(CT, NT)
        modulated_norm(nc, m, a, 1, 0, "norm1", range(NT))
        with nc.sbuf_tensor("Z1", [P, NT, ODD_IN], F32) as m.Z:
            project(nc, m, "pin1", a["o_w_in"][0], range(NT), ODD_IN // 4, out=m.Z)
            head_norm(nc, m, a, "lat", m.Z, range(NT), [(CQ, 1, CKV - CQ, a["c_gq"]), (CKV, 1, KPE - CKV, a["c_gkv"])])
            with nc.sbuf_tensor("LG", [P, NT, 2 * G_HEADS * G_DK], F32) as m.LG:
                m.KV = m.hT[:, :, :].rearrange("p k c -> p (k c)").rearrange("p (t d) -> p t d", d=D)
                with (nc.sbuf_tensor("Q", [P, XT, C_HEADS * C_DQ], F32) as m.Q,
                      nc.sbuf_tensor("K", [P, NT, C_HEADS * C_DQ], F32) as m.K):
                    latent_up(nc, m, a)
                    head_norm(nc, m, a, "qn1", m.Q, XTILES, [(0, C_HEADS, C_DQ, a["c_qn"])], rope=(C_NOPE, C_ROPE, "rope_c"))
                    head_norm(nc, m, a, "kn1", m.K, range(NT), [(0, C_HEADS, C_DQ, a["c_kn"])], rope=(C_NOPE, C_ROPE, "rope_c"))
                    latent_attention(nc, m)
                linear_attention(nc, m, a)
        m.Z = None
        turn_h(nc, m, "th1", XTILES)
        project(nc, m, "pout1", a["o_w_out"][0], XTILES, BANK, gate=m.mods[1, :, 2 * D:3 * D])
        experts(nc, m, a, 1, XTILES, True)


def _(sp):
                sp.dma_start(debug["out_r"].rearrange("p (t d) -> p t d", t=NT), m.R[:, :, :]).then_inc(done, 16)
                sp.dma_start(debug["out_h"].rearrange("p (t d) -> p t d", t=NT), m.H[:, :, :]).then_inc(done, 16)
                n = 2
                if m.Z is not None:
                    sp.dma_start(debug["out_z"].rearrange("p (t d) -> p t d", t=NT), m.Z[:, :, :]).then_inc(done, 16)
                    n = 3
                sp.wait_ge(done, 16 * n)


def kernel(**inputs):
    import concourse.bacc as bacc
    from concourse.bass_utils import run_bass_kernel_spmd

    nc = bacc.Bacc("TRN2", target_bir_lowering=False, num_devices=1)
    arrays, a = {}, {}
    for name, x in (inputs | shape_constants()).items():
        x = np.ascontiguousarray(x)
        arrays[f"in_{name}"] = x
        a[name] = nc.dram_tensor(f"in_{name}", x.shape, mybir.dt.from_np(x.dtype), kind="ExternalInput").ap()
    out = nc.dram_tensor("out_x", (1, SEQ, D), F32, kind="ExternalOutput").ap()
    program(nc, a, out)
    return run_bass_kernel_spmd(nc, [arrays], core_ids=[0]).results[0]["out_x"]
```

```python
from contextlib import ExitStack, contextmanager

import numpy as np

import concourse.bass as bass
from concourse import mybir

P = 128
D = 1024
KC = D // P
CTX, SEQ = 256, 512
CT, XT = CTX // P, SEQ // P
NT = CT + XT
TOK = NT * P
BANK = 512
EPS = 1e-6
NEG = -1e30
GRID_W = 64
THETA = 10000.0

A_HEADS, A_DQK, A_DV = 4, 64, 128
B_HEADS, B_KV, B_DH = 8, 2, 64
AQ, AK, AV = 0, 512, 1024
BQ, BK, BV = 1536, 2048, 2176
EVEN_IN = 2304
LAM_INIT = 0.8 - 0.6

C_HEADS, C_NOPE, C_ROPE, C_DV = 8, 64, 32, 64
C_DQ = C_NOPE + C_ROPE
G_HEADS, G_DK, G_DV, G_CHUNK, G_RANK, G_TAU = 4, 64, 128, 64, 16, 16.0
CQ, CKV, KPE, DQ, DK, DV, GF, DR = 0, 256, 384, 416, 672, 928, 1440, 1472
ODD_IN = 1984

PH, NK, TOPK = 8, 128, 16
SLOTS = PH * TOPK

F32 = mybir.dt.float32
U32 = mybir.dt.uint32
ALU = mybir.AluOpType
ACT = mybir.ActivationFunctionType
AX = mybir.AxisListType
ds = bass.ds


@contextmanager
def repeat(eng, n):
    if n == 1:
        yield 0
    else:
        with eng.Fori(0, n) as i:
            yield i


def rows(ap, n=P):
    return ap.broadcast_to([n, ap.shape[-1]])


class Memory:
    pass


class Stage:

    def __init__(self, nc, name):
        self.nc, self.name, self.ctx = nc, name, ExitStack()
        self.used = []

    def __enter__(self):
        return self

    def __exit__(self, *err):
        for sem in self.used:
            self.nc.sync.sem_clear(sem)
        return self.ctx.__exit__(*err)

    def sb(self, name, shape, dt=F32):
        return self.ctx.enter_context(self.nc.sbuf_tensor(f"{self.name}_{name}", shape, dt))

    def sem(self, name):
        self.used.append(self.ctx.enter_context(self.nc.semaphore(f"{self.name}_{name}")))
        return self.used[-1]

    def pool_dma_sems(self, m, name, n):
        return [m.ctx.enter_context(self.nc.semaphore(f"{self.name}_{name}{i}")) for i in range(n)]

    def sems(self, name, n):
        return [self.sem(f"{name}{i}") for i in range(n)]


def modulation_rows(nc, m, a):
    NCH = 6 * D // BANK
    RG = 4
    with Stage(nc, "mod") as s:
        craw = s.sb("craw", [P, 2, KC])
        den = s.sb("den", [P, 2, KC])
        csil = s.sb("csil", [P, KC, 2])
        w = s.sb("w", [P, RG, KC, BANK])
        bias = s.sb("bias", [2, RG, BANK])
        row = s.sb("row", [2, RG, BANK])
        c_loaded, exp_done, silu_done = s.sem("c_loaded"), s.sem("exp_done"), s.sem("silu_done")
        loaded, used = s.sems("loaded", RG), s.sems("used", RG)
        row_ready, row_stored = s.sems("row_ready", RG), s.pool_dma_sems(m, "row_stored", RG)
        with nc.Block() as block:
            @block.sync
            def _(sp):
                sp.dma_start(craw[:, 0, :], a["c"].rearrange("o (p k) -> p (o k)", k=KC)).then_inc(c_loaded, 16)
                sp.dma_start(craw[:, 1, :], a["c_ctx"].rearrange("(p k) -> p k", k=KC)).then_inc(c_loaded, 16)
                with sp.Fori(0, 2) as l:
                    for n in range(NCH):
                        q, use = n % RG, l * (NCH // RG) + n // RG
                        sp.wait_ge(used[q], use)
                        sp.wait_ge(row_ready[q], use)
                        sp.dma_start(w[:, q], a["w_mod"][ds(l, 1), :, n * BANK:(n + 1) * BANK]
                                     .rearrange("o (p k) n -> p (o k) n", k=KC)).then_inc(loaded[q], 16)
                        sp.dma_start(bias[:, q], a["b_mod"][ds(l, 1), n * BANK:(n + 1) * BANK]
                                     .broadcast_to([2, BANK])).then_inc(loaded[q], 16)

            @block.scalar
            def _(act):
                act.wait_ge(c_loaded, 32)
                act.activation(den[:, :, :], craw[:, :, :], ACT.Exp, scale=-1.0).then_inc(exp_done, 1)

            @block.tensor
            def _(pe):
                pe.wait_ge(silu_done, 1)
                with pe.Fori(0, 2) as l:
                    for n in range(NCH):
                        q, use = n % RG, l * (NCH // RG) + n // RG
                        pe.wait_ge(loaded[q], use * 32 + 32)
                        pe.wait_ge(row_ready[q], use)
                        for k in range(KC):
                            mm = pe.matmul(m.ps[0:2, q, :], csil[:, k, :], w[:, q, k, :],
                                           start=(k == 0), stop=(k == KC - 1))
                        mm.then_inc(used[q], 1)

            @block.vector
            def _(dve):
                dve.wait_ge(exp_done, 1)
                dve.tensor_scalar(den[:, :, :], den[:, :, :], 1.0, None, ALU.add)
                dve.drain()
                dve.reciprocal(den[:, :, :], den[:, :, :])
                dve.drain()
                dve.tensor_tensor(csil[:, :, :].rearrange("p k s -> p s k"), craw[:, :, :], den[:, :, :],
                                  ALU.mult).then_inc(silu_done, 1)
                with dve.Fori(0, 2) as l:
                    for n in range(NCH):
                        q, use = n % RG, l * (NCH // RG) + n // RG
                        dve.wait_ge(used[q], use + 1)
                        dve.wait_ge(row_stored[q], use * 16)
                        dve.tensor_tensor(row[:, q, :], m.ps[0:2, q, :], bias[:, q, :], ALU.add)\
                           .then_inc(row_ready[q], 1)

            @block.gpsimd
            def _(pool):
                with pool.Fori(0, 2) as l:
                    for n in range(NCH):
                        q, use = n % RG, l * (NCH // RG) + n // RG
                        pool.wait_ge(row_ready[q], use + 1)
                        pool.dma_start(m.mods[ds(l, 1), :, n * BANK:(n + 1) * BANK]
                                       .rearrange("o s n -> (o s) n"), row[:, q, :]).then_inc(row_stored[q], 16)
                for q in range(RG):
                    pool.wait_ge(row_stored[q], 2 * (NCH // RG) * 16)


def load_streams(nc, m, a):
    with Stage(nc, "ld") as s:
        done = s.sem("done")
        with nc.Block() as block:
            @block.vector
            def _(dve):
                dve.memset(m.eps[:, :], EPS)

            @block.sync
            def _(sp):
                sp.dma_start(m.R[:, 0:CT, :], a["ctx"].rearrange("b (t p) d -> p (b t) d", p=P)).then_inc(done, 16)
                sp.dma_start(m.R[:, CT:NT, :], a["x"].rearrange("b (t p) d -> p (b t) d", p=P)).then_inc(done, 16)
                sp.dma_start(m.ident[:, :], a["ident"]).then_inc(done, 16)
                sp.wait_ge(done, 48)


def modulated_norm(nc, m, a, layer, sub, gain_name, tiles):
    shift_at, scale_at = 3 * sub * D, (3 * sub + 1) * D
    with Stage(nc, f"n{layer}{sub}") as s:
        gain = s.sb("gain", [P, D])
        scale, shift = s.sb("scale", [P, 2, D]), s.sb("shift", [P, 2, D])
        sq = s.sb("sq", [P, D])
        ss = s.sb("ss", [P, NT])
        loaded, rms_ready, h_ready = s.sem("loaded"), s.sem("rms_ready"), s.sem("h_ready")
        turned, copied = s.sem("turned"), s.sem("copied")
        with nc.Block() as block:
            @block.sync
            def _(sp):
                sp.dma_start(gain[:, :], rows(a[gain_name][layer:layer + 1, :])).then_inc(loaded, 16)
                for st in range(2):
                    sp.dma_start(scale[:, st, :], rows(m.mods[layer, st:st + 1, scale_at:scale_at + D])).then_inc(loaded, 16)
                    sp.dma_start(shift[:, st, :], rows(m.mods[layer, st:st + 1, shift_at:shift_at + D])).then_inc(loaded, 16)

            @block.scalar
            def _(act):
                for t in tiles:
                    act.activation(sq[:, :], m.R[:, t, :], ACT.Square, accum_out=ss[:, t:t + 1])
                    act.drain()
                act.activation(ss[:, tiles[0]:NT], ss[:, tiles[0]:NT], ACT.Sqrt, bias=m.eps[:, :],
                               scale=1.0 / D).then_inc(rms_ready, 1)
                for n, t in enumerate(tiles):
                    act.wait_ge(turned, n + 1)
                    act.copy(m.hT[:, :, t * P:(t + 1) * P],
                             m.ps[:, 2 * (n % 2):2 * (n % 2) + 2, :].rearrange("p b (k c) -> p (b k) c", c=P))\
                       .then_inc(copied, 1)

            @block.vector
            def _(dve):
                dve.wait_ge(loaded, 80)
                for st in range(2):
                    dve.scalar_tensor_tensor(out=scale[:, st, :], in0=scale[:, st, :], scalar=1.0,
                                             in1=gain[:, :], op0=ALU.add, op1=ALU.mult)
                dve.wait_ge(rms_ready, 1)
                dve.reciprocal(ss[:, tiles[0]:NT], ss[:, tiles[0]:NT])
                dve.drain()
                for t in tiles:
                    st = 1 if t < CT else 0
                    dve.scalar_tensor_tensor(out=m.H[:, t, :], in0=m.R[:, t, :], scalar=ss[:, t:t + 1],
                                             in1=scale[:, st, :], op0=ALU.mult, op1=ALU.mult)
                    dve.drain()
                    dve.tensor_tensor(m.H[:, t, :], m.H[:, t, :], shift[:, st, :], ALU.add).then_inc(h_ready, 1)

            @block.tensor
            def _(pe):
                for n, t in enumerate(tiles):
                    pe.wait_ge(h_ready, n + 1)
                    if n >= 2:
                        pe.wait_ge(copied, n - 1)
                    for k in range(KC):
                        tr = pe.transpose(m.ps[:, 2 * (n % 2) + k // 4, (k % 4) * P:(k % 4 + 1) * P],
                                          m.H[:, t, k * P:(k + 1) * P], m.ident[:, :])
                    tr.then_inc(turned, 1)


def turn_h(nc, m, name, tiles):
    with Stage(nc, name) as s:
        turned, copied = s.sem("turned"), s.sem("copied")
        with nc.Block() as block:
            @block.tensor
            def _(pe):
                for n, t in enumerate(tiles):
                    if n >= 2:
                        pe.wait_ge(copied, n - 1)
                    for k in range(KC):
                        tr = pe.transpose(m.ps[:, 2 * (n % 2) + k // 4, (k % 4) * P:(k % 4 + 1) * P],
                                          m.H[:, t, k * P:(k + 1) * P], m.ident[:, :])
                    tr.then_inc(turned, 1)

            @block.scalar
            def _(act):
                for n, t in enumerate(tiles):
                    act.wait_ge(turned, n + 1)
                    act.copy(m.hT[:, :, t * P:(t + 1) * P],
                             m.ps[:, 2 * (n % 2):2 * (n % 2) + 2, :].rearrange("p b (k c) -> p (b k) c", c=P))\
                       .then_inc(copied, 1)


def project(nc, m, name, weight, tiles, chunk, out=None, gate=None):
    pairs = weight.shape[1] // chunk // 2
    n_t = len(tiles)
    body = 2 * n_t
    with Stage(nc, name) as s:
        w = s.sb("w", [P, 2, KC, chunk])
        loaded, used = s.sems("loaded", 2), s.sems("used", 2)
        done, free = s.sems("done", 4), s.sems("free", 4)
        if gate is not None:
            g = s.sb("g", [P, 2, D])
            tmp = s.sb("tmp", [P, 2, chunk])
            g_loaded, scaled, added = s.sem("g_loaded"), s.sem("scaled"), s.sem("added")
        with nc.Block() as block:
            @block.sync
            def _(sp):
                if gate is not None:
                    for st in range(2):
                        sp.dma_start(g[:, st, :], rows(gate[st:st + 1, :])).then_inc(g_loaded, 16)
                with repeat(sp, pairs) as i:
                    for q in range(2):
                        sp.wait_ge(used[q], i)
                        sp.dma_start(w[:, q], weight[:, ds((i * 2 + q) * chunk, chunk)]
                                     .rearrange("(k p) n -> p k n", p=P)).then_inc(loaded[q], 16)

            @block.tensor
            def _(pe):
                with repeat(pe, pairs) as i:
                    for q in range(2):
                        pe.wait_ge(loaded[q], i * 16 + 16)
                        for n, t in enumerate(tiles):
                            b, use = (q * n_t + n) % 4, (q * n_t + n) // 4
                            pe.wait_ge(free[b], i * (body // 4) + use)
                            for k in range(KC):
                                mm = pe.matmul(m.ps[:, b, 0:chunk], m.hT[:, k, t * P:(t + 1) * P], w[:, q, k, :],
                                               start=(k == 0), stop=(k == KC - 1))
                            mm.then_inc(done[b], 1)
                            if n == n_t - 1:
                                pe.drain()
                                pe.sem_inc(used[q], 1)

            if gate is None:
                def evict(eng, copy, parity):
                    with repeat(eng, pairs) as i:
                        for c in range(parity, body, 2):
                            q, t, b, use = c // n_t, tiles[c % n_t], c % 4, c // 4
                            eng.wait_ge(done[b], i * (body // 4) + use + 1)
                            copy(out[:, t, ds((i * 2 + q) * chunk, chunk)], m.ps[:, b, 0:chunk]).then_inc(free[b], 1)

                @block.scalar
                def _(act):
                    evict(act, act.copy, 0)

                @block.vector
                def _(dve):
                    evict(dve, dve.tensor_copy, 1)
            else:
                @block.vector
                def _(dve):
                    dve.wait_ge(g_loaded, 32)
                    for c in range(body):
                        q, t, b, use = c // n_t, tiles[c % n_t], c % 4, c // 4
                        cols = slice(q * chunk, (q + 1) * chunk)
                        dve.wait_ge(done[b], use + 1)
                        if c >= 2:
                            dve.wait_ge(added, c - 1)
                        dve.tensor_tensor(tmp[:, c % 2, :], m.ps[:, b, 0:chunk], g[:, 1 if t < CT else 0, cols],
                                          ALU.mult).then_inc(free[b], 1)
                        dve.drain()
                        dve.sem_inc(scaled, 1)

                @block.gpsimd
                def _(pool):
                    for c in range(body):
                        q, t = c // n_t, tiles[c % n_t]
                        cols = slice(q * chunk, (q + 1) * chunk)
                        pool.wait_ge(scaled, c + 1)
                        pool.tensor_tensor(m.R[:, t, cols], m.R[:, t, cols], tmp[:, c % 2, :], ALU.add)\
                            .then_inc(added, 1)


def head_norm(nc, m, a, name, buf, tiles, segs, rope=None, factor=1.0):
    turns = len(tiles) // 2
    S = sum(g * d for _, g, d, _ in segs)
    G = sum(g for _, g, _, _ in segs)
    with Stage(nc, name) as s:
        sq = s.sb("sq", [P, 2, S])
        ss = s.sb("ss", [P, 2, G])
        gains = s.sb("gains", [P, sum(d for _, _, d, _ in segs)])
        loaded = s.sem("loaded")
        squared, summed, rooted = s.sems("squared", 2), s.sems("summed", 2), s.sems("rooted", 2)
        if rope:
            r0, nr, tables = rope
            cos, sin = s.sb("cos", [P, NT, nr]), s.sb("sin", [P, NT, nr])
            near, far = s.sb("near", [P, 2, G, nr]), s.sb("far", [P, 2, G, nr])
            scaled, near_ready = s.sems("scaled", 2), s.sems("near_ready", 2)

        def parts(i, q):
            at = g0 = gain0 = 0
            for c, g, d, _ in segs:
                yield (buf[:, i * 2 + q + (tiles[0] if tiles[0] and buf.shape[1] == NT else 0), c:c + g * d]
                       .rearrange("p (g d) -> p g d", d=d),
                       sq[:, q, at:at + g * d].rearrange("p (g d) -> p g d", d=d), ss[:, q, g0:g0 + g],
                       gains[:, gain0:gain0 + d], g, d, g0)
                at, g0, gain0 = at + g * d, g0 + g, gain0 + d

        def table(tab, i, q, g):
            return tab[:, ds(i * 2 + q + tiles[0], 1), :].broadcast_to([P, g, nr])

        def pairs(x, which):
            return x.rearrange("p g (f two) -> p g f two", two=2)[:, :, :, which]

        with nc.Block() as block:
            @block.sync
            def _(sp):
                at = 0
                for _, _, d, gain in segs:
                    sp.dma_start(gains[:, at:at + d], rows(gain)).then_inc(loaded, 16)
                    at += d
                if rope:
                    sp.dma_start(cos[:, :, :], a[tables + "_cos"].rearrange("(t p) d -> p t d", p=P)).then_inc(loaded, 16)
                    sp.dma_start(sin[:, :, :], a[tables + "_sin"].rearrange("(t p) d -> p t d", p=P)).then_inc(loaded, 16)

            n_loads = len(segs) + (2 if rope else 0)

            @block.scalar
            def _(act):
                with repeat(act, turns) as i:
                    for q in range(2):
                        act.wait_ge(rooted[q], i)
                        act.wait_ge(summed[q], i)
                        for x, x2, *_ in parts(i, q):
                            sqr = act.activation(x2, x, ACT.Square)
                        sqr.then_inc(squared[q], 1)
                    for q in range(2):
                        act.wait_ge(summed[q], i + 1)
                        for x, x2, r, gn, g, d, g0 in parts(i, q):
                            root = act.activation(r, r, ACT.Sqrt, bias=m.eps[:, :], scale=1.0 / d)
                        root.then_inc(rooted[q], 1)

            @block.vector
            def _(dve):
                dve.wait_ge(loaded, 16 * n_loads)
                if factor != 1.0:
                    dve.tensor_scalar(gains[:, :], gains[:, :], factor, None, ALU.mult)
                    dve.drain()
                with repeat(dve, turns) as i:
                    for q in range(2):
                        dve.wait_ge(squared[q], i + 1)
                        for x, x2, r, gn, g, d, g0 in parts(i, q):
                            red = dve.tensor_reduce(r, x2, AX.X, ALU.add)
                        red.then_inc(summed[q], 1)
                    for q in range(2):
                        dve.wait_ge(rooted[q], i + 1)
                        dve.reciprocal(ss[:, q, :], ss[:, q, :])
                        dve.drain()
                        for x, x2, r, gn, g, d, g0 in parts(i, q):
                            dve.tensor_tensor(x, x, r.unsqueeze(2).broadcast_to([P, g, d]), ALU.mult)
                        dve.drain()
                        for x, x2, r, gn, g, d, g0 in parts(i, q):
                            mul = dve.tensor_tensor(x, x, gn.unsqueeze(1).broadcast_to([P, g, d]), ALU.mult)
                        if rope:
                            mul.then_inc(scaled[q], 1)
                            dve.drain()
                            for x, x2, r, gn, g, d, g0 in parts(i, q):
                                tail, f = x[:, :, r0:r0 + nr], far[:, q, g0:g0 + g, :]
                                tab = table(sin, i, q, g)
                                for e in range(2):
                                    dve.tensor_tensor(pairs(f, e), pairs(tail, 1 - e), pairs(tab, e), ALU.mult)
                            dve.drain()
                            dve.wait_ge(near_ready[q], i + 1)
                            for x, x2, r, gn, g, d, g0 in parts(i, q):
                                dve.tensor_tensor(x[:, :, r0:r0 + nr], near[:, q, g0:g0 + g, :],
                                                  far[:, q, g0:g0 + g, :], ALU.add)

            if rope:
                @block.gpsimd
                def _(pool):
                    pool.wait_ge(loaded, 16 * n_loads)
                    with repeat(pool, turns) as i:
                        for q in range(2):
                            pool.wait_ge(scaled[q], i + 1)
                            for x, x2, r, gn, g, d, g0 in parts(i, q):
                                mul = pool.tensor_tensor(near[:, q, g0:g0 + g, :], x[:, :, r0:r0 + nr],
                                                         table(cos, i, q, g), ALU.mult)
                            mul.then_inc(near_ready[q], 1)


def lambda_and_sinks(nc, m, a):
    with Stage(nc, "lam") as s:
        v = s.sb("v", [P, 4, A_DQK])
        junk = s.sb("junk", [P, 2, A_DQK])
        dots = s.sb("dots", [P, 2])
        loaded, dots_ready, exp_done = s.sem("loaded"), s.sem("dots_ready"), s.sem("exp_done")
        with nc.Block() as block:
            @block.sync
            def _(sp):
                for n, key in enumerate(("a_lq1", "a_lk1", "a_lq2", "a_lk2")):
                    sp.dma_start(v[:, n, :], rows(a[key])).then_inc(loaded, 16)
                sp.dma_start(m.sink[:, :], rows(a["b_sink"])).then_inc(loaded, 16)
                sp.dma_start(m.band[:, :, :], a["band"].rearrange("s p k -> p s k")).then_inc(loaded, 16)

            @block.vector
            def _(dve):
                dve.wait_ge(loaded, 96)
                for n in range(2):
                    dve.scalar_tensor_tensor(out=junk[:, n, :], in0=v[:, 2 * n, :], scalar=1.0, in1=v[:, 2 * n + 1, :],
                                             op0=ALU.mult, op1=ALU.mult, accum_out=dots[:, n:n + 1])
                dve.tensor_scalar(m.neg_sink[:, :], m.sink[:, :], -1.0, None, ALU.mult)
                dve.drain()
                dve.sem_inc(dots_ready, 1)
                dve.wait_ge(exp_done, 1)
                dve.scalar_tensor_tensor(out=m.neg_lam[:, :], in0=dots[:, 1:2], scalar=-LAM_INIT, in1=dots[:, 0:1],
                                         op0=ALU.add, op1=ALU.subtract)

            @block.scalar
            def _(act):
                act.wait_ge(dots_ready, 1)
                act.activation(dots[:, :], dots[:, :], ACT.Exp).then_inc(exp_done, 1)


def attention(nc, m, kind, scale, turns, maps, dq, dv, tiles, blocks_of, q_of, k_of, v_of, out_of):
    per = 2 if kind == "A" else 1
    jobs = [(t, mp) for t in tiles for mp in range(maps)]
    vals = jobs if per == 1 else [(t, 0) for t in tiles]
    NS, NV, NQ = len(jobs), len(vals), len(tiles)
    W = NT * P

    def runs(t):
        out = []
        for j, kt in enumerate(blocks_of(t)):
            if out and (j * P) % BANK and out[-1][1] + out[-1][2] == kt:
                out[-1][2] += 1
            else:
                out.append([j * P, kt, 1])
        return out

    with Stage(nc, f"at{kind}") as s:
        wq_ = dq if maps == 1 else 2 * dq
        q_in, k_in = s.sb("q_in", [P, NQ, wq_]), s.sb("k_in", [P, NT, wq_])
        qT, kT = s.sb("qT", [P, NQ * P]), s.sb("kT", [P, TOK])
        probs = s.sb("probs", [P, 4, W])
        probsT = s.sb("probsT", [P, 2, W])
        top, bias, den, rec = (s.sb(x, [P, 4]) for x in ("top", "bias", "den", "rec"))
        if kind == "A":
            mixed = s.sb("mixed", [P, 2, W])
            mixed_ready = s.sems("mixed_ready", 2)
        if kind == "B":
            sunk = s.sb("sunk", [P, 4])
        staged, q_turned, k_turned, q_ready, k_ready = (s.sem(x) for x in (
            "staged", "q_turned", "k_turned", "q_ready", "k_ready"))
        scored, biased, exped = s.sems("scored", 2), s.sems("biased", 2), s.sems("exped", 2)
        probs_turned, probsT_ready = s.sem("probs_turned"), s.sem("probsT_ready")
        valued, taken = s.sems("valued", 2), s.sems("taken", 2)

        def width(n):
            return len(blocks_of(jobs[n][0])) * P

        def score_bank(n):
            return m.ps[:, 2 * (n % 2):2 * (n % 2) + 2, :].rearrange("p b c -> p (b c)")

        turn_bank = m.ps[:, 4:6, :].rearrange("p b c -> p (b c)")
        k_bank = m.ps[:, 6:8, :].rearrange("p b c -> p (b c)")

        with nc.Block() as block:
            @block.gpsimd
            def _(pool):
                with pool.Fori(0, turns) as i:
                    pool.wait_ge(k_turned, i)
                    pool.sem_inc(staged, 1)
                    pool.tensor_copy(q_in[:, :, :], q_of(pool, i))
                    for part, src in k_of(pool, i):
                        last = pool.tensor_copy(k_in[:, :, part], src)
                    last.then_inc(staged, 1)

            @block.tensor
            def _(pe):
                with pe.Fori(0, turns) as i:
                    pe.wait_ge(staged, 2 * i + 2)
                    pe.wait_ge(probsT_ready, i * NV)
                    for n in range(NQ):
                        tr = pe.transpose(turn_bank[0:wq_, n * P:(n + 1) * P], q_in[:, n, :], m.ident[:, :])
                    tr.then_inc(q_turned, 1)
                    for b in range(2):
                        pe.wait_ge(taken[b], i * (NV // 2))
                    for n in range(NT):
                        tr = pe.transpose(k_bank[0:wq_, n * P:(n + 1) * P], k_in[:, n, :], m.ident[:, :])
                    tr.then_inc(k_turned, 1)
                    pe.wait_ge(q_ready, i + 1)
                    pe.wait_ge(k_ready, i + 1)

                    def score(n):
                        t, mp = jobs[n]
                        r = slice(mp * dq, (mp + 1) * dq)
                        pe.wait_ge(exped[n % 2], i * (NS // 2) + n // 2)
                        for c, kt, cnt in runs(t):
                            mm = pe.matmul(score_bank(n)[:, c:c + cnt * P], qT[r, tiles.index(t) * P:(tiles.index(t) + 1) * P],
                                           kT[r, kt * P:(kt + cnt) * P], start=True, stop=True)
                        mm.then_inc(scored[n % 2], 1)

                    def turn(v):
                        if per == 2:
                            pe.wait_ge(mixed_ready[v % 2], i * (NV // 2) + v // 2 + 1)
                            src = mixed[:, v % 2, :]
                        else:
                            pe.wait_ge(exped[v % 2], i * (NS // 2) + v // 2 + 1)
                            src = probs[:, v % 4, :]
                        pe.wait_ge(probsT_ready, i * NV + v)
                        for j in range(len(blocks_of(vals[v][0]))):
                            tr = pe.transpose(turn_bank[:, j * P:(j + 1) * P], src[:, j * P:(j + 1) * P], m.ident[:, :])
                        tr.then_inc(probs_turned, 1)

                    def value(v):
                        pe.wait_ge(probsT_ready, i * NV + v + 1)
                        pe.wait_ge(taken[v % 2], i * (NV // 2) + v // 2)
                        bl = blocks_of(vals[v][0])
                        for j, kt in enumerate(bl):
                            mm = pe.matmul(m.ps[:, 6 + v % 2, 0:dv], probsT[:, v % 2, j * P:(j + 1) * P],
                                           v_of(pe, i, kt), start=(j == 0), stop=(j == len(bl) - 1))
                        mm.then_inc(valued[v % 2], 1)

                    for n in range(per):
                        score(n)
                    for v in range(NV):
                        for n in range((v + 1) * per, min((v + 2) * per, NS)):
                            score(n)
                        turn(v)
                        if v:
                            value(v - 1)
                    value(NV - 1)

            @block.vector
            def _(dve):
                with dve.Fori(0, turns) as i:
                    dve.wait_ge(k_turned, i + 1)
                    dve.tensor_copy(kT[0:wq_, :], k_bank[0:wq_, 0:TOK]).then_inc(k_ready, 1)

                    def find_max(n):
                        t, mp = jobs[n]
                        sl = slice(n % 4, n % 4 + 1)
                        dve.wait_ge(scored[n % 2], i * (NS // 2) + n // 2 + 1)
                        if kind == "B" and t >= CT:
                            for j, kt in enumerate(blocks_of(t)):
                                if kt >= CT and kt != t:
                                    cols = score_bank(n)[:, j * P:(j + 1) * P]
                                    dve.tensor_tensor(cols, cols, m.band[:, 0 if kt < t else 1, :], ALU.add)
                            dve.drain()
                        dve.tensor_reduce(top[:, sl], score_bank(n)[:, 0:width(n)], AX.X, ALU.max)
                        dve.drain()
                        if kind == "B":
                            b = dve.tensor_scalar(bias[:, sl], top[:, sl], -scale, m.neg_sink[:, ds(i * 2 + mp, 1)],
                                                  ALU.mult, ALU.min)
                        else:
                            b = dve.tensor_scalar(bias[:, sl], top[:, sl], -scale, None, ALU.mult)
                        b.then_inc(biased[n % 2], 1)

                    def mix(v):
                        for b in range(2):
                            dve.wait_ge(exped[b], i * (NS // 2) + v + 1)
                        c0 = (2 * v) % 4
                        w = width(2 * v)
                        dve.reciprocal(rec[:, c0:c0 + 2], den[:, c0:c0 + 2])
                        dve.drain()
                        dve.tensor_scalar(rec[:, c0 + 1:c0 + 2], rec[:, c0 + 1:c0 + 2], m.neg_lam[:, :], None, ALU.mult)
                        dve.tensor_scalar(mixed[:, v % 2, 0:w], probs[:, c0, 0:w], rec[:, c0:c0 + 1], None, ALU.mult)
                        dve.drain()
                        dve.scalar_tensor_tensor(out=mixed[:, v % 2, 0:w], in0=probs[:, c0 + 1, 0:w],
                                                 scalar=rec[:, c0 + 1:c0 + 2], in1=mixed[:, v % 2, 0:w],
                                                 op0=ALU.mult, op1=ALU.add).then_inc(mixed_ready[v % 2], 1)

                    def take(v):
                        t, mp = vals[v]
                        sl = slice(v % 4, v % 4 + 1)
                        if per == 1:
                            dve.wait_ge(exped[v % 2], i * (NS // 2) + v // 2 + 1)
                            if kind == "B":
                                dve.tensor_tensor(den[:, sl], den[:, sl], sunk[:, sl], ALU.add)
                                dve.drain()
                            dve.reciprocal(rec[:, sl], den[:, sl])
                            dve.drain()
                        dve.wait_ge(valued[v % 2], i * (NV // 2) + v // 2 + 1)
                        src, dst = m.ps[:, 6 + v % 2, 0:dv], out_of(i, t, mp)
                        if per == 2:
                            o = dve.tensor_copy(dst, src)
                        else:
                            o = dve.tensor_scalar(dst, src, rec[:, sl], None, ALU.mult)
                        o.then_inc(taken[v % 2], 1)

                    for n in range(per):
                        find_max(n)
                    for v in range(NV):
                        if per == 2:
                            mix(v)
                        for n in range((v + 1) * per, min((v + 2) * per, NS)):
                            find_max(n)
                        if v:
                            take(v - 1)
                    take(NV - 1)

            @block.scalar
            def _(act):
                with act.Fori(0, turns) as i:
                    act.wait_ge(q_turned, i + 1)
                    act.copy(qT[0:wq_, :], turn_bank[0:wq_, 0:NQ * P]).then_inc(q_ready, 1)

                    def exponential(n):
                        mp = jobs[n][1]
                        sl = slice(n % 4, n % 4 + 1)
                        act.wait_ge(biased[n % 2], i * (NS // 2) + n // 2 + 1)
                        e = act.activation(probs[:, n % 4, 0:width(n)], score_bank(n)[:, 0:width(n)], ACT.Exp,
                                           bias=bias[:, sl], scale=scale, accum_out=den[:, sl])
                        if kind == "B":
                            e = act.activation(sunk[:, sl], m.sink[:, ds(i * 2 + mp, 1)], ACT.Exp, bias=bias[:, sl])
                        e.then_inc(exped[n % 2], 1)

                    def copy_turned(v):
                        w = len(blocks_of(vals[v][0])) * P
                        act.wait_ge(probs_turned, i * NV + v + 1)
                        act.copy(probsT[:, v % 2, 0:w], turn_bank[:, 0:w]).then_inc(probsT_ready, 1)

                    for n in range(per):
                        exponential(n)
                    for v in range(NV):
                        for n in range((v + 1) * per, min((v + 2) * per, NS)):
                            exponential(n)
                        copy_turned(v)


def differential_attention(nc, m):
    attention(nc, m, "A", A_DQK ** -0.5, A_HEADS, 2, A_DQK, A_DV, list(range(NT)),
              lambda t: list(range(NT if t >= CT else CT)),
              lambda e, i: m.Z[:, :, ds(AQ + i * 2 * A_DQK, 2 * A_DQK)],
              lambda e, i: [(slice(0, 2 * A_DQK), m.Z[:, :, ds(AK + i * 2 * A_DQK, 2 * A_DQK)])],
              lambda e, i, kt: m.Z[:, kt, ds(AV + i * A_DV, A_DV)],
              lambda i, t, mp: m.H[:, t, ds(i * A_DV, A_DV)])


def windowed_attention(nc, m):
    def blocks_of(t):
        if t < CT:
            return list(range(CT))
        return list(range(CT)) + list(range(max(t - 1, CT), min(t + 1, NT - 1) + 1))

    def kv(e, i):
        return e.snap(i // 2)

    def k_of(e, i):
        src = m.Z[:, :, ds(kv(e, i) * B_DH + BK, B_DH)]
        return [(slice(0, B_DH), src), (slice(B_DH, 2 * B_DH), src)]

    attention(nc, m, "B", B_DH ** -0.5, B_HEADS // 2, 2, B_DH, B_DH, list(range(NT)), blocks_of,
              lambda e, i: m.Z[:, :, ds(BQ + i * 2 * B_DH, 2 * B_DH)], k_of,
              lambda e, i, kt: m.Z[:, kt, ds(kv(e, i) * B_DH + BV, B_DH)],
              lambda i, t, mp: m.H[:, t, ds(A_HEADS * A_DV + (i * 2 + mp) * B_DH, B_DH)])


def latent_up(nc, m, a):
    QW, KVW, GW = C_HEADS * C_DQ, C_HEADS * (C_NOPE + C_DV), 2 * G_HEADS * G_DK
    with Stage(nc, "up") as s:
        wq, wkv, wg = s.sb("wq", [P, 2, QW]), s.sb("wkv", [P, KVW]), s.sb("wg", [2 * G_RANK, GW])
        gate_bias = s.sb("gate_bias", [P, GW])
        lat = s.sb("lat", [P, 2, 4, P])
        cleared, loaded = s.sem("cleared"), s.sem("loaded")
        turned, lat_ready = s.sem("turned"), s.sem("lat_ready")
        upped, act_taken, dve_taken = s.sem("upped"), s.sem("act_taken"), s.sem("dve_taken")
        with nc.Block() as block:
            @block.sync
            def _(sp):
                half = GW // 2
                sp.wait_ge(cleared, 1)
                sp.dma_start(wg[0:G_RANK, 0:half], a["d_wg_f"][0]).then_inc(loaded, 16)
                sp.dma_start(wg[G_RANK:2 * G_RANK, half:GW], a["d_wg_b"][0]).then_inc(loaded, 16)
                sp.dma_start(gate_bias[:, 0:half], rows(a["d_bg_f"])).then_inc(loaded, 16)
                sp.dma_start(gate_bias[:, half:GW], rows(a["d_bg_b"])).then_inc(loaded, 16)
                sp.dma_start(wq[:, :, :], a["c_wq_up"][0].rearrange("(k p) n -> p k n", p=P)).then_inc(loaded, 16)
                sp.dma_start(wkv[:, :], a["c_wkv_up"][0]).then_inc(loaded, 16)

            @block.tensor
            def _(pe):
                def turn(t):
                    if t >= 2:
                        pe.wait_ge(lat_ready, t - 1)
                    cols = [CKV, GF] + ([CQ, CQ + P] if t >= CT else [])
                    for n, c in enumerate(cols):
                        w = 2 * G_RANK if c == GF else P
                        tr = pe.transpose(m.ps[0:w, t % 2, n * P:(n + 1) * P], m.Z[:, t, c:c + w], m.ident[:, :])
                    tr.then_inc(turned, 1)

                def up(t):
                    pe.wait_ge(lat_ready, t + 1)
                    if t >= 1:
                        pe.wait_ge(act_taken, t)
                        pe.wait_ge(dve_taken, t)
                    for h in range(2):
                        mm = pe.matmul(m.ps[:, 2 + h, :], lat[:, t % 2, 0, :], wkv[:, h * BANK:(h + 1) * BANK], start=True, stop=True)
                    mm = pe.matmul(m.ps[:, 4, :], lat[0:2 * G_RANK, t % 2, 1, :], wg[:, :], start=True, stop=True)
                    if t >= CT:
                        for c, w in ((0, BANK), (BANK, QW - BANK)):
                            for k in range(2):
                                mm = pe.matmul(m.ps[:, 6 + c // BANK, 0:w], lat[:, t % 2, 2 + k, :], wq[:, k, c:c + w],
                                               start=(k == 0), stop=(k == 1))
                    mm.then_inc(upped, 1)

                pe.wait_ge(loaded, 96)
                for t in range(NT):
                    turn(t)
                    if t:
                        up(t - 1)
                up(NT - 1)

            @block.scalar
            def _(act):
                def take(t):
                    act.wait_ge(upped, t + 1)
                    c = act.copy(m.KV[:, t, :], m.ps[:, 2:4, :].rearrange("p b c -> p (b c)"))
                    if t >= CT:
                        c = act.copy(m.Q[:, t - CT, :], m.ps[:, 6:8, :].rearrange("p b c -> p (b c)")[:, 0:QW])
                    c.then_inc(act_taken, 1)

                for t in range(NT):
                    act.wait_ge(turned, t + 1)
                    n = 4 if t >= CT else 1
                    act.copy(lat[0:2 * G_RANK, t % 2, 1, :], m.ps[0:2 * G_RANK, t % 2, P:2 * P])
                    if t >= CT:
                        act.copy(lat[:, t % 2, 2:4, :].rearrange("p k c -> p (k c)"), m.ps[:, t % 2, 2 * P:4 * P])
                    act.copy(lat[:, t % 2, 0, :], m.ps[:, t % 2, 0:P]).then_inc(lat_ready, 1)
                    if t:
                        take(t - 1)
                take(NT - 1)

            @block.vector
            def _(dve):
                dve.memset(wg[:, :], 0.0).then_inc(cleared, 1)
                dve.wait_ge(loaded, 96)
                for t in range(NT):
                    dve.wait_ge(upped, t + 1)
                    dve.tensor_tensor(m.LG[:, t, :], m.ps[:, 4, :], gate_bias[:, :], ALU.add).then_inc(dve_taken, 1)

            @block.gpsimd
            def _(pool):
                for t in range(NT):
                    pool.wait_ge(act_taken, t + 1)
                    kh = m.K[:, t, :].rearrange("p (h d) -> p h d", d=C_DQ)
                    pool.tensor_copy(kh[:, :, 0:C_NOPE], m.KV[:, t, :].rearrange("p (h d) -> p h d", h=C_HEADS)[:, :, 0:C_NOPE])
                    pool.tensor_copy(kh[:, :, C_NOPE:C_DQ], m.Z[:, t, KPE:KPE + C_ROPE].unsqueeze(1)
                                     .broadcast_to([P, C_HEADS, C_ROPE]))


def latent_attention(nc, m):
    KVD = C_NOPE + C_DV
    attention(nc, m, "C", C_DQ ** -0.5, C_HEADS, 1, C_DQ, C_DV, list(range(CT, NT)), lambda t: list(range(NT)),
              lambda e, i: m.Q[:, :, ds(i * C_DQ, C_DQ)],
              lambda e, i: [(slice(0, C_DQ), m.K[:, :, ds(i * C_DQ, C_DQ)])],
              lambda e, i, kt: m.KV[:, kt, ds(i * KVD + C_NOPE, C_DV)],
              lambda i, t, mp: m.H[:, t, ds(i * C_DV, C_DV)])


def linear_attention(nc, m, a):
    KW = G_HEADS * G_DK
    W = 2 * KW
    NCH = NT * P // G_CHUNK
    CCH, XCH = CT * 2, XT * 2
    VW = G_HEADS * G_DV
    with ExitStack() as ctx:
        sb = lambda name, shape: ctx.enter_context(nc.sbuf_tensor("gla_" + name, shape, F32))
        tri = sb("tri", [P, 3, P])
        qT, kT = sb("qT", [P, 4, XT * P]), sb("kT", [P, 4, XT * P])
        decay = sb("decay", [P, 4, NCH])
        state = sb("state", [P, 2, NCH + 1, 2 * G_DV])

        with Stage(nc, "gg") as s:
            one = s.sb("one", [P, 1])
            soft = s.sb("soft", [P, NT, W])
            loaded, one_ready, soft_ready = s.sem("loaded"), s.sem("one_ready"), s.sem("soft_ready")
            with nc.Block() as block:
                @block.sync
                def _(sp):
                    sp.dma_start(tri[:, :, :], a["tri"].rearrange("s p c -> p s c")).then_inc(loaded, 16)
                    sp.wait_ge(loaded, 16)

                @block.scalar
                def _(act):
                    act.wait_ge(one_ready, 1)
                    act.activation(soft[:, :, :], m.LG[:, :, :], ACT.Abs)
                    act.drain()
                    act.activation(soft[:, :, :], soft[:, :, :], ACT.Exp, scale=-1.0)
                    act.drain()
                    act.activation(soft[:, :, :], soft[:, :, :], ACT.Ln, bias=one[:, :]).then_inc(soft_ready, 1)

                @block.vector
                def _(dve):
                    dve.memset(one[:, :], 1.0).then_inc(one_ready, 1)
                    dve.wait_ge(soft_ready, 1)
                    dve.scalar_tensor_tensor(out=m.LG[:, :, :], in0=m.LG[:, :, :], scalar=0.0, in1=soft[:, :, :],
                                             op0=ALU.min, op1=ALU.subtract)
                    dve.drain()
                    dve.tensor_scalar(m.LG[:, :, :], m.LG[:, :, :], 1.0 / G_TAU, None, ALU.mult)

        with Stage(nc, "gs") as s:
            up, down, stay = (s.sb(x, [P, 2, W]) for x in ("up", "down", "stay"))
            summed, exped, diffed = s.sem("summed"), s.sem("exped"), s.sem("diffed")
            stay_ready, scaled, banks_free = s.sem("stay_ready"), s.sem("scaled"), s.sem("banks_free")
            turned, copied = s.sem("turned"), s.sem("copied")
            with nc.Block() as block:
                @block.tensor
                def _(pe):
                    def turn(t):
                        x = t - CT
                        pe.wait_ge(scaled, t + 1)
                        if x >= 1:
                            pe.wait_ge(copied, x)
                        for n in range(4):
                            tr = pe.transpose(m.ps[:, 4, n * P:(n + 1) * P], up[:, t % 2, n * P:(n + 1) * P], m.ident[:, :])
                            tr = pe.transpose(m.ps[:, 5, n * P:(n + 1) * P], down[:, t % 2, n * P:(n + 1) * P], m.ident[:, :])
                        tr.then_inc(turned, 1)

                    for t in range(NT):
                        if t >= 1:
                            pe.wait_ge(banks_free, t)
                            pe.wait_ge(exped, t)
                        for d in range(2):
                            pe.matmul(m.ps[:, 0, d * KW:(d + 1) * KW], tri[:, d, :], m.LG[:, t, d * KW:(d + 1) * KW],
                                      start=True, stop=True)
                        pe.matmul(m.ps[:, 1, :], tri[:, 2, :], m.LG[:, t, :], start=True, stop=True)
                        for n in range(4):
                            mm = pe.matmul(m.ps[:, 2, 2 * n:2 * n + 2], m.LG[:, t, n * P:(n + 1) * P],
                                           tri[:, 2, 0:P:G_CHUNK], start=True, stop=True)
                        mm.then_inc(summed, 1)
                        if t > CT:
                            turn(t - 1)
                    turn(NT - 1)

                def copy(act, t):
                    x = t - CT
                    act.wait_ge(turned, x + 1)
                    act.copy(qT[:, :, x * P:(x + 1) * P], m.ps[:, 4, :].rearrange("p (n c) -> p n c", c=P))
                    act.copy(kT[:, :, x * P:(x + 1) * P], m.ps[:, 5, :].rearrange("p (n c) -> p n c", c=P)).then_inc(copied, 1)

                @block.scalar
                def _(act):
                    for t in range(NT):
                        act.wait_ge(summed, t + 1)
                        if t >= 2:
                            act.wait_ge(scaled, t - 1)
                            if t - 2 >= CT:
                                act.wait_ge(turned, t - 1 - CT)
                        act.activation(up[:, t % 2, :], m.ps[:, 0, :], ACT.Exp)
                        act.activation(down[:, t % 2, :], m.ps[:, 0, :], ACT.Exp, scale=-1.0)
                        act.activation(decay[:, :, 2 * t:2 * t + 2],
                                       m.ps[:, 2, 0:8].rearrange("p (n c) -> p n c", c=2), ACT.Exp).then_inc(exped, 1)
                        act.wait_ge(diffed, t + 1)
                        act.activation(stay[:, t % 2, :], stay[:, t % 2, :], ACT.Exp).then_inc(stay_ready, 1)
                        if t > CT:
                            copy(act, t - 1)
                    copy(act, NT - 1)

                @block.vector
                def _(dve):
                    for t in range(NT):
                        dve.wait_ge(exped, t + 1)
                        dve.tensor_copy(stay[:, t % 2, :], m.ps[:, 0, :])
                        dve.drain()
                        dve.tensor_tensor(stay[:, t % 2, :], m.ps[:, 1, :], stay[:, t % 2, :], ALU.subtract)
                        dve.drain()
                        dve.sem_inc(diffed, 1)
                        dve.sem_inc(banks_free, 1)
                        k2 = m.Z[:, t, DK:DK + KW].unsqueeze(1).broadcast_to([P, 2, KW])
                        q2 = m.Z[:, t, DQ:DQ + KW].unsqueeze(1).broadcast_to([P, 2, KW])
                        both = lambda x: x[:, t % 2, :].rearrange("p (d n) -> p d n", d=2)
                        if t >= CT:
                            dve.scalar_tensor_tensor(out=both(up), in0=both(up), scalar=G_DK ** -0.5, in1=q2,
                                                     op0=ALU.mult, op1=ALU.mult)
                            dve.tensor_tensor(both(down), both(down), k2, ALU.mult)
                        dve.wait_ge(stay_ready, t + 1)
                        dve.tensor_tensor(m.LG[:, t, :].rearrange("p (d n) -> p d n", d=2), both(stay), k2,
                                          ALU.mult).then_inc(scaled, 1)

        def chunk_at(d, n):
            if d == 0:
                return n
            return CCH - 1 - n if n < CCH else CCH + XCH - 1 - (n - CCH)

        with Stage(nc, "gc") as s:
            kv_done, bank_read = s.sems("kv_done", 4), s.sems("bank_read", 4)
            with nc.Block() as block:
                @block.tensor
                def _(pe):
                    for n in range(NCH - 1):
                        for d in range(2):
                            b, use = (2 * n + d) % 4, (2 * n + d) // 4
                            c = chunk_at(d, n)
                            r = slice((c % 2) * G_CHUNK, (c % 2 + 1) * G_CHUNK)
                            pe.wait_ge(bank_read[b], use)
                            for pair in range(2):
                                at = d * KW + pair * P
                                mm = pe.matmul(m.ps[:, b, pair * 2 * G_DV:(pair + 1) * 2 * G_DV], m.LG[r, c // 2, at:at + P],
                                               m.Z[r, c // 2, DV + pair * 2 * G_DV:DV + (pair + 1) * 2 * G_DV],
                                               start=True, stop=True)
                            mm.then_inc(kv_done[b], 1)

                @block.vector
                def _(dve):
                    dve.memset(state[:, :, 0, :], 0.0)
                    dve.drain()
                    for n in range(NCH - 1):
                        for d in range(2):
                            b, use = (2 * n + d) % 4, (2 * n + d) // 4
                            c = chunk_at(d, n)
                            dve.wait_ge(kv_done[b], use + 1)
                            for h in range(G_HEADS):
                                pair, r = h // 2, slice((h % 2) * G_DK, (h % 2 + 1) * G_DK)
                                cols = slice(pair * G_DV, (pair + 1) * G_DV)
                                upd = dve.scalar_tensor_tensor(
                                    out=state[r, d, n + 1, cols], in0=state[r, d, n, cols],
                                    scalar=decay[r, 2 * d + pair, c:c + 1],
                                    in1=m.ps[r, b, h * G_DV:(h + 1) * G_DV], op0=ALU.mult, op1=ALU.add)
                            upd.then_inc(bank_read[b], 1)
                        dve.drain()

        with Stage(nc, "go") as s:
            within = s.sb("within", [P, 2, 2, P])
            cleared = s.sem("cleared")
            products, masked = s.sems("products", 4), s.sems("masked", 4)
            o_done, o_taken = s.sems("o_done", 2), s.sems("o_taken", 2)
            units = [(x, h, d) for x in range(XT) for h in range(G_HEADS) for d in range(2)]
            with nc.Block() as block:
                @block.tensor
                def _(pe):
                    def product(u):
                        x, h, d = units[u]
                        r = slice((h % 2) * G_DK, (h % 2 + 1) * G_DK)
                        n, cols = 2 * d + h // 2, slice(x * P, (x + 1) * P)
                        pe.wait_ge(masked[u % 4], u // 4)
                        pe.matmul(m.ps[:, 4 + u % 4, 0:P], kT[r, n, cols], qT[r, n, cols], start=True, stop=True)\
                            .then_inc(products[u % 4], 1)

                    def output(u):
                        x, h, d = units[u]
                        r = slice((h % 2) * G_DK, (h % 2 + 1) * G_DK)
                        n, cols = 2 * d + h // 2, slice(h // 2 * G_DV, (h // 2 + 1) * G_DV)
                        bank = 2 * (x % 2) + h % 2
                        if h == 0 and d == 0:
                            pe.wait_ge(o_taken[x % 2], x // 2)
                        pe.wait_ge(masked[u % 4], u // 4 + 1)
                        pe.matmul(m.ps[:, bank, cols], within[:, d, (u // 2) % 2, :],
                                  m.Z[:, CT + x, DV + h * G_DV:DV + (h + 1) * G_DV], start=(d == 0), stop=False,
                                  skip_group_check=True)
                        for c in range(2):
                            chunk = 2 * x + c
                            step = CCH + (chunk if d == 0 else XCH - 1 - chunk)
                            tok = slice(x * P + c * G_CHUNK, x * P + (c + 1) * G_CHUNK)
                            mm = pe.matmul(m.ps[c * G_CHUNK:(c + 1) * G_CHUNK, bank, cols], qT[r, n, tok],
                                           state[r, d, step, (h // 2) * G_DV:(h // 2 + 1) * G_DV],
                                           start=False, stop=(d == 1), skip_group_check=True)
                        if h == G_HEADS - 1 and d == 1:
                            mm.then_inc(o_done[x % 2], 1)

                    product(0)
                    product(1)
                    for u in range(len(units)):
                        if u + 2 < len(units):
                            product(u + 2)
                        output(u)

                @block.vector
                def _(dve):
                    dve.memset(within[:, :, :, :], 0.0)
                    dve.drain()
                    for u, (x, h, d) in enumerate(units):
                        dve.wait_ge(products[u % 4], u // 4 + 1)
                        dve.copy_predicated(within[:, d, (u // 2) % 2, :], tri[:, d, :].bitcast(U32),
                                            m.ps[:, 4 + u % 4, 0:P]).then_inc(masked[u % 4], 1)

                @block.scalar
                def _(act):
                    for x in range(XT):
                        act.wait_ge(o_done[x % 2], x // 2 + 1)
                        act.copy(m.H[:, CT + x, C_HEADS * C_DV:D].rearrange("p (a b v) -> p b a v", b=2, v=G_DV),
                                 m.ps[:, 2 * (x % 2):2 * (x % 2) + 2, 0:2 * G_DV].rearrange("p b (a v) -> p b a v", v=G_DV))\
                            .then_inc(o_taken[x % 2], 1)

        head_norm(nc, m, a, "gn1", m.H, range(CT, NT), [(C_HEADS * C_DV, G_HEADS, G_DV, a["d_gn"])])
        with Stage(nc, "gr") as s:
            den = s.sb("den", [P, XT, VW])
            exped = s.sem("exped")
            with nc.Block() as block:
                @block.scalar
                def _(act):
                    act.activation(den[:, :, :], m.Z[:, CT:NT, DR:DR + VW], ACT.Exp, scale=-1.0).then_inc(exped, 1)

                @block.vector
                def _(dve):
                    dve.wait_ge(exped, 1)
                    dve.tensor_scalar(den[:, :, :], den[:, :, :], 1.0, None, ALU.add)
                    dve.drain()
                    dve.reciprocal(den[:, :, :], den[:, :, :])
                    dve.drain()
                    dve.tensor_tensor(den[:, :, :], den[:, :, :], m.Z[:, CT:NT, DR:DR + VW], ALU.mult)
                    dve.drain()
                    out = m.H[:, CT:NT, C_HEADS * C_DV:D]
                    dve.tensor_tensor(out, out, den[:, :, :], ALU.mult)


def expert_scores(nc, m, a, layer, tiles):
    NH, HALF = 2 * PH, len(tiles) * P // 2
    t0, PER = tiles[0], 8
    with Stage(nc, f"es{layer}") as s:
        keys, keysT = s.sb("keys", [P, NH, P]), s.sb("keysT", [P, NH, P])
        w = s.sb("w", [P, 2, KC, BANK])
        qT = s.sb("qT", [P, 2, 2, HALF])
        out = s.sb("out", [P, 2, len(tiles), BANK])
        out_ready, out_stored = s.sems("out_ready", 2), s.pool_dma_sems(m, "out_stored", 2)
        keys_loaded, keys_turned, keysT_ready = s.sem("keys_loaded"), s.sem("keys_turned"), s.sem("keysT_ready")
        loaded, used = s.sems("loaded", 2), s.sems("used", 2)
        q_done, qT_ready = s.sems("q_done", 2), s.sems("qT_ready", 2)
        scored, taken = s.sems("scored", 2), s.sems("taken", 2)
        with nc.Block() as block:
            @block.sync
            def _(sp):
                sp.dma_start(keys[:, :, :], a["p_keys"][layer].rearrange("h s n d -> n (h s) d")).then_inc(keys_loaded, 16)
                with sp.Fori(0, NH // PER) as i:
                    for q in range(2):
                        sp.wait_ge(used[q], i)
                        sp.dma_start(w[:, q], a["p_wq"][layer][:, ds((i * 2 + q) * BANK, BANK)]
                                     .rearrange("(k p) n -> p k n", p=P)).then_inc(loaded[q], 16)

            @block.tensor
            def _(pe):
                pe.wait_ge(keys_loaded, 16)
                for h in range(NH):
                    tr = pe.transpose(m.ps[:, h // 4, (h % 4) * P:(h % 4 + 1) * P], keys[:, h, :], m.ident[:, :])
                tr.then_inc(keys_turned, 1)
                pe.wait_ge(keysT_ready, 1)
                with pe.Fori(0, NH // PER) as i:
                    def query(h):
                        b, use = h % 2, i * (PER // 2) + h // 2
                        if h % 4 == 0:
                            pe.wait_ge(loaded[h // 4], i * 16 + 16)
                        pe.wait_ge(qT_ready[b], use)
                        for half in range(2):
                            for k in range(KC):
                                mm = pe.matmul(m.ps[:, 2 * b + half, 0:HALF], w[:, h // 4, k, (h % 4) * P:(h % 4 + 1) * P],
                                               m.hT[:, k, t0 * P + half * HALF:t0 * P + (half + 1) * HALF],
                                               start=(k == 0), stop=(k == KC - 1))
                        mm.then_inc(q_done[b], 1)
                        if h % 4 == 3:
                            pe.drain()
                            pe.sem_inc(used[h // 4], 1)

                    def score(h):
                        b, use = h % 2, i * (PER // 2) + h // 2
                        pe.wait_ge(qT_ready[b], use + 1)
                        pe.wait_ge(taken[b], use)
                        for n in range(len(tiles)):
                            mm = pe.matmul(m.ps[:, 4 + 2 * b + n // 4, (n % 4) * P:(n % 4 + 1) * P],
                                           qT[:, b, :, :].rearrange("p a c -> p (a c)")[:, n * P:(n + 1) * P],
                                           keysT[:, ds(i * PER + h, 1), :].rearrange("p o n -> p (o n)"),
                                           start=True, stop=True)
                        mm.then_inc(scored[b], 1)

                    for h in range(PER):
                        query(h)
                        if h:
                            score(h - 1)
                    score(PER - 1)

            @block.gpsimd
            def _(pool):
                with pool.Fori(0, NH // PER) as i:
                    for q in range(2):
                        pool.wait_ge(out_ready[q], i + 1)
                        pool.dma_start(m.scores[t0:NT, :, ds((i * 2 + q) * BANK, BANK)].rearrange("t p n -> p t n"),
                                       out[:, q]).then_inc(out_stored[q], 16)
                for q in range(2):
                    pool.wait_ge(out_stored[q], 16 * NH // PER)

            @block.scalar
            def _(act):
                act.wait_ge(keys_turned, 1)
                act.copy(keysT[:, :, :].rearrange("p h n -> p (h n)"),
                         m.ps[:, 0:4, :].rearrange("p b c -> p (b c)")).then_inc(keysT_ready, 1)
                with act.Fori(0, NH // PER) as i:
                    for h in range(PER):
                        b, use = h % 2, i * (PER // 2) + h // 2
                        act.wait_ge(q_done[b], use + 1)
                        act.wait_ge(scored[b], use)
                        act.copy(qT[:, b, :, :], m.ps[:, 2 * b:2 * b + 2, 0:HALF]).then_inc(qT_ready[b], 1)

            @block.vector
            def _(dve):
                with dve.Fori(0, NH // PER) as i:
                    for h in range(PER):
                        b, use = h % 2, i * (PER // 2) + h // 2
                        dve.wait_ge(scored[b], use + 1)
                        if h % 4 == 0:
                            dve.wait_ge(out_stored[h // 4], i * 16)
                        src = m.ps[:, 4 + 2 * b:6 + 2 * b, :].rearrange("p b (t n) -> p (b t) n", n=P)
                        dve.tensor_copy(out[:, h // 4, :, (h % 4) * P:(h % 4 + 1) * P], src[:, 0:len(tiles), :])\
                            .then_inc(taken[b], 1)
                        if h % 4 == 3:
                            dve.drain()
                            dve.sem_inc(out_ready[h // 4], 1)


def run_experts(nc, m, a, layer, tiles, last):
    T, t0 = len(tiles), tiles[0]
    NH = 2 * PH
    RING, IDX, BODY = 16, 8, 32
    NBODY, ROUNDS, NIDX = SLOTS // BODY, BODY // RING, BODY // IDX
    VDVE = 3
    LOW = -3.0e38
    u_rows, v_rows = a["p_u"].rearrange("l e d -> (l e) d"), a["p_v"].rearrange("l e d -> (l e) d")
    with Stage(nc, f"ex{layer}") as s:
        ring = s.sb("ring", [P, RING, D])
        idx = s.sb("idx", [P, NIDX, IDX], U32)
        expert, weight = s.sb("expert", [P, 2 * SLOTS], U32), s.sb("weight", [P, SLOTS])
        gates = s.sb("gates", [P, 2 * SLOTS])
        dots, product = s.sb("dots", [P, SLOTS]), s.sb("product", [P, 2, D])
        mixed = s.sb("mixed", [P, D])
        diag = s.sb("diag", [P, 4, P])
        zeros = s.sb("zeros", [P, BANK], mybir.dt.bfloat16)
        g = s.sb("g", [P, 2, D])
        landed, used = s.pool_dma_sems(m, "landed", RING), s.sems("used", RING)
        idx_landed = s.sems("idx_landed", NIDX)
        dve_group, pe_group = s.sems("dve_group", NIDX), s.sems("pe_group", NIDX)
        idx_free = s.sem("idx_free")
        claimed, zeroed, g_loaded = s.sem("claimed"), s.sem("zeroed"), s.sem("g_loaded")
        dots_ready, gelu_done, weights_ready = s.sem("dots_ready"), s.sem("gelu_done"), s.sem("weights_ready")
        diag_ready, diag_used = s.sems("diag_ready", 4), s.sems("diag_used", 4)
        summed, mix_taken, added, stored = s.sem("summed"), s.sem("mix_taken"), s.sem("added"), s.sem("stored")

        sc, rest = s.sb("sc", [P, NH, NK]), s.sb("rest", [P, NH, NK])
        val, pos, posf = s.sb("val", [P, NH, TOPK]), s.sb("pos", [P, NH, TOPK], U32), s.sb("posf", [P, NH, TOPK])
        best, at_ = s.sb("best", [P, PH, TOPK]), s.sb("at", [P, PH, TOPK], U32)
        shift = s.sb("shift", [P, PH, TOPK])
        part, partf = s.sb("part", [P, 2, SLOTS], U32), s.sb("partf", [P, 2, SLOTS])
        iota, num, total = s.sb("iota", [P, TOPK]), s.sb("num", [P, 2, SLOTS]), s.sb("total", [P, PH])
        iota_loaded, sc_loaded, sc_read = s.sem("iota_loaded"), s.sem("sc_loaded"), s.sem("sc_read")
        shifted, exped, chosen = s.sem("shifted"), s.sem("exped"), s.sem("chosen")
        cand = sc[:, :, :].rearrange("p h k -> p (h k)").rearrange("p (h c) -> p h c", c=TOPK * TOPK)
        left = rest[:, :, :].rearrange("p h k -> p (h k)").rearrange("p (h c) -> p h c", c=TOPK * TOPK)
        hot = rest[:, :, :].rearrange("p h k -> p (h k)").rearrange("p (n i) -> p n i", i=TOPK)

        def tiles_loop(eng, tile):
            if T > 1:
                with eng.Fori(0, T - 1) as t:
                    tile(t, True)
            tile(T - 1, False)

        def bodies(eng, t, phase):
            with eng.Fori(0, NBODY) as i:
                yield (t * 2 + phase) * NBODY + i, i

        def side(t):
            return (t % 2) * SLOTS

        with nc.Block() as block:
            @block.sync
            def _(sp):
                sp.dma_start(iota[:, :], rows(a["iota"])).then_inc(iota_loaded, 16)
                sp.dma_start(sc[:, :, :].rearrange("p h n -> p (h n)"), m.scores[t0]).then_inc(sc_loaded, 16)
                for st in range(2):
                    sp.dma_start(g[:, st, :], rows(m.mods[layer, 1 - st:2 - st, 5 * D:6 * D])).then_inc(g_loaded, 16)

                def tile(t, more):
                    first = sp.snap(side(t))
                    sp.wait_ge(chosen, t + 1)
                    sp.sem_inc(idx_free, 1)
                    for phase in range(2):
                        if phase == 1 and more:
                            sp.wait_ge(sc_read, t + 1)
                            sp.dma_start(sc[:, :, :].rearrange("p h n -> p (h n)"),
                                         m.scores[ds(t + (t0 + 1), 1)].rearrange("o p n -> p (o n)")).then_inc(sc_loaded, 16)
                        for turn, i in bodies(sp, t, phase):
                            for b in range(NIDX):
                                sp.wait_ge(dve_group[b], turn)
                                sp.sem_inc(idx_free, 1)
                                sp.wait_ge(pe_group[b], t * NBODY + (i if phase else 0))
                                sp.dma_start(idx[:, b, :], expert[:, ds(first + i * BODY + b * IDX, IDX)])\
                                    .then_inc(idx_landed[b], 16)
                tiles_loop(sp, tile)

            @block.gpsimd
            def _(pool):
                def tile(t, more):
                    for phase in range(2):
                        for turn, i in bodies(pool, t, phase):
                            for n in range(BODY):
                                r = n % RING
                                if n % IDX == 0:
                                    pool.wait_ge(idx_landed[n // IDX], turn * 16 + 16)
                                pool.wait_ge(used[r], turn * ROUNDS + n // RING)
                                pool.sem_inc(claimed, 1)
                                pool.indirect_dma_start(ring[:, r, :], None, v_rows if phase else u_rows,
                                                        bass.IndirectOffsetOnAxis(ap=idx[:, n // IDX, n % IDX:n % IDX + 1], axis=0),
                                                        ).then_inc(landed[r], 16)
                tiles_loop(pool, tile)

            @block.vector
            def _(dve):
                def choose(t):
                    def top16(n, values, src, spare, index):
                        for half in (slice(0, n // 2), slice(n // 2, n)):
                            hs = range(half.start, half.stop)
                            for h in hs:
                                dve.max(values[:, h, 0:8], src[:, h, :])
                            dve.drain()
                            yield
                            for h in hs:
                                dve.max_index(index[:, h, 0:8], values[:, h, 0:8], src[:, h, :])
                            yield
                            for h in hs:
                                dve.match_replace(spare[:, h, :], values[:, h, 0:8], src[:, h, :], LOW)
                            dve.drain()
                            yield
                            for h in hs:
                                dve.max(values[:, h, 8:16], spare[:, h, :])
                            dve.drain()
                            for h in hs:
                                dve.max_index(index[:, h, 8:16], values[:, h, 8:16], spare[:, h, :])
                            dve.drain()
                            yield

                    dve.wait_ge(sc_loaded, t * 16 + 16)
                    dve.sem_inc(claimed, 1)
                    yield from top16(NH, val, sc, rest, pos)
                    dve.tensor_copy(posf[:, :, :], pos[:, :, :])
                    pairs = val[:, :, :].rearrange("p (h s) k -> p h s k", s=2)
                    dve.tensor_tensor(cand.rearrange("p h (i j) -> p h i j", j=TOPK),
                                      pairs[:, :, 0, :].unsqueeze(3).broadcast_to([P, PH, TOPK, TOPK]),
                                      pairs[:, :, 1, :].unsqueeze(2).broadcast_to([P, PH, TOPK, TOPK]), ALU.add)
                    dve.drain()
                    yield
                    yield from top16(PH, best, cand, left, at_)
                    dve.sem_inc(sc_read, 1)
                    flat = at_[:, :, :].rearrange("p h k -> p (h k)")
                    dve.tensor_scalar(part[:, 0, :], flat, 4, None, ALU.logical_shift_right)
                    dve.tensor_scalar(part[:, 1, :], flat, TOPK - 1, None, ALU.bitwise_and)
                    dve.tensor_tensor(shift[:, :, :], best[:, :, :], best[:, :, 0:1].broadcast_to([P, PH, TOPK]),
                                      ALU.subtract)
                    dve.drain()
                    dve.sem_inc(shifted, 1)
                    dve.tensor_copy(partf[:, :, :], part[:, :, :])
                    dve.drain()
                    halves = posf[:, :, :].rearrange("p (h s) k -> p h s k", s=2)
                    h4 = hot.rearrange("p (h k) i -> p h k i", k=TOPK)
                    for half in range(2):
                        dve.tensor_tensor(hot, iota[:, :].unsqueeze(1).broadcast_to([P, SLOTS, TOPK]),
                                          partf[:, half, :].unsqueeze(2).broadcast_to([P, SLOTS, TOPK]), ALU.is_equal)
                        dve.drain()
                        yield
                        dve.tensor_tensor(h4, h4, halves[:, :, half, :].unsqueeze(2).broadcast_to([P, PH, TOPK, TOPK]), ALU.mult)
                        dve.drain()
                        dve.tensor_reduce(num[:, half, :], hot, AX.X, ALU.add)
                        dve.drain()
                        yield
                    dve.scalar_tensor_tensor(out=num[:, 0, :], in0=num[:, 0, :], scalar=float(NK), in1=num[:, 1, :],
                                             op0=ALU.mult, op1=ALU.add)
                    dve.drain()
                    dve.tensor_scalar(expert[:, ds(side(t), SLOTS)], num[:, 0, :], float(layer * NK * NK), None, ALU.add)
                    dve.drain()
                    dve.sem_inc(chosen, 1)
                    yield

                def weigh(t):
                    dve.wait_ge(exped, t + 1)
                    dve.tensor_reduce(total[:, :], shift[:, :, :], AX.X, ALU.add)
                    dve.drain()
                    dve.reciprocal(total[:, :], total[:, :])
                    dve.drain()
                    dve.tensor_tensor(gates[:, ds(side(t), SLOTS)].rearrange("p (h k) -> p h k", k=TOPK),
                                      shift[:, :, :], total[:, :].unsqueeze(2).broadcast_to([P, PH, TOPK]), ALU.mult)
                    dve.drain()

                def tile(t, more):
                    for turn, i in bodies(dve, t, 0):
                        for n in range(BODY):
                            r = n % RING
                            dve.wait_ge(landed[r], turn * (ROUNDS * 16) + (n // RING + 1) * 16)
                            dve.scalar_tensor_tensor(out=product[:, n % 2, :], in0=ring[:, r, :], scalar=1.0,
                                                     in1=m.H[:, t + t0, :], op0=ALU.mult, op1=ALU.mult,
                                                     accum_out=dots[:, ds(i * BODY + n, 1)]).then_inc(used[r], 1)
                            if n % IDX == IDX - 1:
                                dve.sem_inc(dve_group[n // IDX], 1)
                            if n % 2:
                                dve.drain()
                    dve.sem_inc(dots_ready, 1)
                    dve.memset(mixed[:, :], 0.0)
                    dve.wait_ge(gelu_done, t + 1)
                    dve.tensor_tensor(weight[:, :], dots[:, :], gates[:, ds(side(t), SLOTS)], ALU.mult)
                    dve.drain()
                    dve.sem_inc(weights_ready, 1)
                    steps = choose(t + 1) if more else iter(())
                    for body in range(NBODY):
                        turn = (t * 2 + 1) * NBODY + body
                        for n in range(BODY):
                            r = n % RING
                            if n % 4 == VDVE:
                                dve.wait_ge(landed[r], turn * (ROUNDS * 16) + (n // RING + 1) * 16)
                                dve.scalar_tensor_tensor(out=mixed[:, :], in0=ring[:, r, :],
                                                         scalar=weight[:, body * BODY + n:body * BODY + n + 1],
                                                         in1=mixed[:, :], op0=ALU.mult, op1=ALU.add).then_inc(used[r], 1)
                                dve.drain()
                                next(steps, None)
                            if n % IDX == IDX - 1:
                                dve.sem_inc(dve_group[n // IDX], 1)
                    for _ in steps:
                        pass
                    if more:
                        weigh(t + 1)
                    dve.wait_ge(summed, t + 1)
                    dve.tensor_tensor(mixed[:, :], mixed[:, :], m.ps[:, 0:2, :].rearrange("p b c -> p (b c)"), ALU.add)\
                        .then_inc(mix_taken, 1)
                    dve.drain()
                    stream = dve.snap((t + t0 + 4) // 6)
                    dve.tensor_tensor(mixed[:, :], mixed[:, :], g[:, ds(stream, 1), :].rearrange("p o d -> p (o d)"), ALU.mult)
                    dve.drain()
                    dve.tensor_tensor(m.R[:, t + t0, :], m.R[:, t + t0, :], mixed[:, :], ALU.add).then_inc(added, 1)
                    dve.drain()

                dve.memset(zeros[:, :], 0.0).then_inc(zeroed, 1)
                dve.wait_ge(iota_loaded, 16)
                dve.wait_ge(g_loaded, 32)
                for _ in choose(0):
                    pass
                weigh(0)
                tiles_loop(dve, tile)

            @block.scalar
            def _(act):
                def shift_exp(t):
                    act.wait_ge(shifted, t + 1)
                    act.activation(shift[:, :, :], shift[:, :, :], ACT.Exp).then_inc(exped, 1)

                def tile(t, more):
                    act.wait_ge(dots_ready, t + 1)
                    act.activation(dots[:, :], dots[:, :], ACT.Gelu).then_inc(gelu_done, 1)
                    act.wait_ge(weights_ready, t + 1)
                    for body in range(NBODY):
                        for n in range(BODY):
                            if n % 4 != VDVE:
                                k = n - n // 4 - (n % 4 > VDVE)
                                act.wait_ge(diag_used[k % 4], (t * NBODY + body) * (BODY * 3 // 16) + k // 4)
                                act.activation(diag[:, k % 4, :], m.ident[:, :], ACT.Copy,
                                               scale=weight[:, body * BODY + n:body * BODY + n + 1]).then_inc(diag_ready[k % 4], 1)
                    if more:
                        shift_exp(t + 1)
                    if last:
                        act.wait_ge(added, t + 1)
                        act.sem_inc(claimed, 1)
                        act.dma_start(m.out[0, ds((t + t0 - CT) * P, P), :], m.R[:, t + t0, :]).then_inc(stored, 16)

                shift_exp(0)
                tiles_loop(act, tile)
                if last:
                    act.wait_ge(stored, 16 * T)

            @block.tensor
            def _(pe):
                pe.wait_ge(zeroed, 1)

                def tile(t, more):
                    pe.wait_ge(mix_taken, t)
                    for b in range(2):
                        pe.matmul(m.ps[:, b, :], zeros[:, 0:P], zeros[:, :], start=True, stop=False, skip_group_check=True)
                    for turn, i in bodies(pe, t, 1):
                        for n in range(BODY):
                            r = n % RING
                            if n % 4 != VDVE:
                                k = n - n // 4 - (n % 4 > VDVE)
                                pe.wait_ge(diag_ready[k % 4], (t * NBODY + i) * (BODY * 3 // 16) + k // 4 + 1)
                                pe.wait_ge(landed[r], turn * (ROUNDS * 16) + (n // RING + 1) * 16)
                                for b in range(2):
                                    mm = pe.matmul(m.ps[:, b, :], diag[:, k % 4, :], ring[:, r, b * BANK:(b + 1) * BANK],
                                                   start=False, stop=False, skip_group_check=True)
                                mm.then_inc(used[r], 1)
                                pe.drain()
                                pe.sem_inc(diag_used[k % 4], 1)
                            if n % IDX == IDX - 1:
                                pe.sem_inc(pe_group[n // IDX], 1)
                    pe.drain()
                    pe.sem_inc(summed, 1)
                tiles_loop(pe, tile)


def experts(nc, m, a, layer, tiles, last):
    modulated_norm(nc, m, a, layer, 1, "norm2", tiles)
    expert_scores(nc, m, a, layer, tiles)
    run_experts(nc, m, a, layer, tiles, last)


def shape_constants():
    def rope(dim, name):
        pos = np.arange(SEQ)
        axis = dim // 2
        inv = (1.0 / (THETA ** (np.arange(0, axis, 2, dtype=np.float32) / axis))).astype(np.float32)
        ang = np.concatenate([(pos // GRID_W)[:, None].astype(np.float32) * inv,
                              (pos % GRID_W)[:, None].astype(np.float32) * inv], axis=-1)
        cos = np.ones((TOK, dim), np.float32)
        sin = np.zeros((TOK, dim), np.float32)
        cos[CTX:] = np.repeat(np.cos(ang), 2, axis=1)
        sin[CTX:] = np.repeat(np.sin(ang), 2, axis=1) * np.tile([-1.0, 1.0], dim // 2)
        return {name + "_cos": cos, name + "_sin": sin}

    k, q = np.arange(P)[None, :], np.arange(P)[:, None]
    band = np.stack([np.where(k >= q, 0.0, NEG), np.where(k <= q, 0.0, NEG)]).astype(np.float32)
    s_, c_ = np.arange(P)[:, None], np.arange(P)[None, :]
    same = s_ // G_CHUNK == c_ // G_CHUNK
    tri = np.stack([same & (s_ <= c_), same & (s_ >= c_), same]).astype(np.float32)
    return {"tri": tri, "iota": np.arange(TOPK, dtype=np.float32)[None, :], "ident": np.eye(P, dtype=np.float32), "band": band} | rope(B_DH, "rope_ab") | rope(C_ROPE, "rope_c")


def program(nc, a, out):
    with ExitStack() as ctx:
        m = Memory()
        m.ctx = ctx
        m.mods = nc.dram_tensor("modulations", [2, 2, 6 * D], F32, kind="Internal").ap()
        m.scores = nc.dram_tensor("key_scores", [NT, P, 2 * PH * NK], F32, kind="Internal").ap()
        m.R = ctx.enter_context(nc.sbuf_tensor("R", [P, NT, D], F32))
        m.H = ctx.enter_context(nc.sbuf_tensor("H", [P, NT, D], F32))
        m.hT = ctx.enter_context(nc.sbuf_tensor("hT", [P, KC, TOK], F32))
        m.ident = ctx.enter_context(nc.sbuf_tensor("ident_sb", [P, P], F32))
        m.eps = ctx.enter_context(nc.sbuf_tensor("eps", [P, 1], F32))
        m.ps = ctx.enter_context(nc.psum_tensor("ps", [P, 8, BANK], F32))
        m.neg_lam = ctx.enter_context(nc.sbuf_tensor("neg_lam", [P, 1], F32))
        m.sink = ctx.enter_context(nc.sbuf_tensor("sink", [P, B_HEADS], F32))
        m.neg_sink = ctx.enter_context(nc.sbuf_tensor("neg_sink", [P, B_HEADS], F32))
        m.band = ctx.enter_context(nc.sbuf_tensor("band_sb", [P, 2, P], F32))
        m.Z = None
        m.out = out

        load_streams(nc, m, a)
        modulation_rows(nc, m, a)
        modulated_norm(nc, m, a, 0, 0, "norm1", range(NT))
        with nc.sbuf_tensor("Z", [P, NT, EVEN_IN], F32) as m.Z:
            project(nc, m, "pin0", a["e_w_in"][0], range(NT), EVEN_IN // 6, out=m.Z)
            head_norm(nc, m, a, "qk0", m.Z, range(NT),
                      [(AQ, 2 * A_HEADS, A_DQK, a["a_qn"]), (AK, 2 * A_HEADS, A_DQK, a["a_kn"]),
                       (BQ, B_HEADS, B_DH, a["b_qn"]), (BK, B_KV, B_DH, a["b_kn"])], rope=(0, B_DH, "rope_ab"))
            lambda_and_sinks(nc, m, a)
            differential_attention(nc, m)
            windowed_attention(nc, m)
        m.Z = None
        head_norm(nc, m, a, "gn0", m.H, range(NT), [(0, A_HEADS, A_DV, a["a_gn"])], factor=1.0 - LAM_INIT)
        turn_h(nc, m, "th0", range(NT))
        project(nc, m, "pout0", a["e_w_out"][0], range(NT), BANK, gate=m.mods[0, :, 2 * D:3 * D])
        experts(nc, m, a, 0, range(NT), False)

        XTILES = range(CT, NT)
        modulated_norm(nc, m, a, 1, 0, "norm1", range(NT))
        with nc.sbuf_tensor("Z1", [P, NT, ODD_IN], F32) as m.Z:
            project(nc, m, "pin1", a["o_w_in"][0], range(NT), ODD_IN // 4, out=m.Z)
            head_norm(nc, m, a, "lat", m.Z, range(NT), [(CQ, 1, CKV - CQ, a["c_gq"]), (CKV, 1, KPE - CKV, a["c_gkv"])])
            with nc.sbuf_tensor("LG", [P, NT, 2 * G_HEADS * G_DK], F32) as m.LG:
                m.KV = m.hT[:, :, :].rearrange("p k c -> p (k c)").rearrange("p (t d) -> p t d", d=D)
                with (nc.sbuf_tensor("Q", [P, XT, C_HEADS * C_DQ], F32) as m.Q,
                      nc.sbuf_tensor("K", [P, NT, C_HEADS * C_DQ], F32) as m.K):
                    latent_up(nc, m, a)
                    head_norm(nc, m, a, "qn1", m.Q, XTILES, [(0, C_HEADS, C_DQ, a["c_qn"])], rope=(C_NOPE, C_ROPE, "rope_c"))
                    head_norm(nc, m, a, "kn1", m.K, range(NT), [(0, C_HEADS, C_DQ, a["c_kn"])], rope=(C_NOPE, C_ROPE, "rope_c"))
                    latent_attention(nc, m)
                linear_attention(nc, m, a)
        m.Z = None
        turn_h(nc, m, "th1", XTILES)
        project(nc, m, "pout1", a["o_w_out"][0], XTILES, BANK, gate=m.mods[1, :, 2 * D:3 * D])
        experts(nc, m, a, 1, XTILES, True)


def _(sp):
                sp.dma_start(debug["out_r"].rearrange("p (t d) -> p t d", t=NT), m.R[:, :, :]).then_inc(done, 16)
                sp.dma_start(debug["out_h"].rearrange("p (t d) -> p t d", t=NT), m.H[:, :, :]).then_inc(done, 16)
                n = 2
                if m.Z is not None:
                    sp.dma_start(debug["out_z"].rearrange("p (t d) -> p t d", t=NT), m.Z[:, :, :]).then_inc(done, 16)
                    n = 3
                sp.wait_ge(done, 16 * n)


def kernel(**inputs):
    import concourse.bacc as bacc
    from concourse.bass_utils import run_bass_kernel_spmd

    nc = bacc.Bacc("TRN2", target_bir_lowering=False, num_devices=1)
    arrays, a = {}, {}
    for name, x in (inputs | shape_constants()).items():
        x = np.ascontiguousarray(x)
        arrays[f"in_{name}"] = x
        a[name] = nc.dram_tensor(f"in_{name}", x.shape, mybir.dt.from_np(x.dtype), kind="ExternalInput").ap()
    out = nc.dram_tensor("out_x", (1, SEQ, D), F32, kind="ExternalOutput").ap()
    program(nc, a, out)
    return run_bass_kernel_spmd(nc, [arrays], core_ids=[0]).results[0]["out_x"]
```

```python
from contextlib import ExitStack, contextmanager

import numpy as np

import concourse.bass as bass
from concourse import mybir

P = 128
D = 1024
KC = D // P
CTX, SEQ = 256, 512
CT, XT = CTX // P, SEQ // P
NT = CT + XT
TOK = NT * P
BANK = 512
EPS = 1e-6
NEG = -1e30
GRID_W = 64
THETA = 10000.0

A_HEADS, A_DQK, A_DV = 4, 64, 128
B_HEADS, B_KV, B_DH = 8, 2, 64
AQ, AK, AV = 0, 512, 1024
BQ, BK, BV = 1536, 2048, 2176
EVEN_IN = 2304
LAM_INIT = 0.8 - 0.6

C_HEADS, C_NOPE, C_ROPE, C_DV = 8, 64, 32, 64
C_DQ = C_NOPE + C_ROPE
G_HEADS, G_DK, G_DV, G_CHUNK, G_RANK, G_TAU = 4, 64, 128, 64, 16, 16.0
CQ, CKV, KPE, DQ, DK, DV, GF, DR = 0, 256, 384, 416, 672, 928, 1440, 1472
ODD_IN = 1984

PH, NK, TOPK = 8, 128, 16
SLOTS = PH * TOPK
LOW = -3.0e38

F32 = mybir.dt.float32
U32 = mybir.dt.uint32
ALU = mybir.AluOpType
ACT = mybir.ActivationFunctionType
AX = mybir.AxisListType
ds = bass.ds


@contextmanager
def repeat(eng, n):
    if n == 1:
        yield 0
    else:
        with eng.Fori(0, n) as i:
            yield i


def rows(ap, n=P):
    return ap.broadcast_to([n, ap.shape[-1]])


class Memory:
    pass


class Stage:

    def __init__(self, nc, name):
        self.nc, self.name, self.ctx = nc, name, ExitStack()
        self.used = []

    def __enter__(self):
        return self

    def __exit__(self, *err):
        for sem in self.used:
            self.nc.sync.sem_clear(sem)
        return self.ctx.__exit__(*err)

    def sb(self, name, shape, dt=F32):
        return self.ctx.enter_context(self.nc.sbuf_tensor(f"{self.name}_{name}", shape, dt))

    def sem(self, name):
        self.used.append(self.ctx.enter_context(self.nc.semaphore(f"{self.name}_{name}")))
        return self.used[-1]

    def pool_dma_sems(self, m, name, n):
        return [m.ctx.enter_context(self.nc.semaphore(f"{self.name}_{name}{i}")) for i in range(n)]

    def sems(self, name, n):
        return [self.sem(f"{name}{i}") for i in range(n)]


class NextModulation:
    ROUNDS = 2

    def __init__(self, nc, m, a, s):
        self.m, self.a = m, a
        self.chunk = 6 * D // (8 * self.ROUNDS)
        self.w = s.sb("w", [P, 2, KC, self.chunk])
        self.loaded, self.used = s.sems("mod_loaded", 2), s.sems("mod_used", 2)
        self.bias_loaded, self.done = s.sem("bias_loaded"), s.sem("mod_done")
        self.ready, self.stored = s.sem("mod_ready"), s.sem("mod_stored")
        flat = self.w[0:2 * self.ROUNDS].rearrange("p q k n -> p q (k n)")
        self.bias, self.row = flat[:, 0, :], flat[:, 1, :]

    def sync(self, sp):
        for n in range(8 * self.ROUNDS):
            if n >= 2:
                sp.wait_ge(self.used[n % 2], n // 2)
            sp.dma_start(self.w[:, n % 2], self.a["w_mod"][1, :, n * self.chunk:(n + 1) * self.chunk]
                         .rearrange("(p k) n -> p k n", k=KC)).then_inc(self.loaded[n % 2], 16)
        sp.wait_ge(self.done, 1)
        b = self.a["b_mod"][1:2, :].rearrange("o (j n) -> o j n", j=self.ROUNDS)
        for j in range(self.ROUNDS):
            sp.dma_start(self.bias[2 * j:2 * j + 2, :], rows(b[:, j, :], 2)).then_inc(self.bias_loaded, 16)
        sp.wait_ge(self.ready, 1)
        for j in range(self.ROUNDS):
            sp.dma_start(self.m.mods[1, :, j * 3 * D:(j + 1) * 3 * D], self.row[2 * j:2 * j + 2, :]).then_inc(self.stored, 16)
        sp.wait_ge(self.stored, 16 * self.ROUNDS)

    def tensor(self, pe):
        m = self.m
        for n in range(8 * self.ROUNDS):
            j = n // 8
            pe.wait_ge(self.loaded[n % 2], n // 2 * 16 + 16)
            for k in range(KC):
                mm = pe.matmul(m.ps[0:4, n % 8, 0:self.chunk], m.csil[:, k, 2 - 2 * j:6 - 2 * j], self.w[:, n % 2, k, :],
                               start=(n < 8 and k == 0), stop=(k == KC - 1), skip_group_check=True)
            mm.then_inc(self.used[n % 2], 1)
        pe.drain()
        pe.sem_inc(self.done, 1)

    def vector(self, dve):
        dve.wait_ge(self.done, 1)
        dve.wait_ge(self.bias_loaded, 16 * self.ROUNDS)
        dve.tensor_tensor(self.row.rearrange("p (b n) -> p b n", b=8), self.m.ps[0:4, :, 0:self.chunk],
                          self.bias.rearrange("p (b n) -> p b n", b=8), ALU.add).then_inc(self.ready, 1)


def start(nc, m, a):
    NCH = 6 * D // BANK
    RG = 4
    with Stage(nc, "mod") as s:
        craw = s.sb("craw", [P, 2, KC])
        den = s.sb("den", [P, 2, KC])
        w = s.sb("w", [P, RG, KC, BANK])
        bias = s.sb("bias", [2, RG, BANK])
        row = s.sb("row", [2, RG, BANK])
        c_loaded, exp_done, silu_done = s.sem("c_loaded"), s.sem("exp_done"), s.sem("silu_done")
        loaded, used = s.sems("loaded", RG), s.sems("used", RG)
        row_ready, row_stored = s.sems("row_ready", RG), s.pool_dma_sems(m, "row_stored", RG)
        v, junk, dots = s.sb("v", [P, 4, A_DQK]), s.sb("junk", [P, 2, A_DQK]), s.sb("dots", [P, 2])
        v_loaded, streams_loaded = s.sem("v_loaded"), s.sem("streams_loaded")
        dots_ready, lam_exp_done = s.sem("dots_ready"), s.sem("lam_exp_done")
        with nc.Block() as block:
            @block.sync
            def _(sp):
                sp.dma_start(craw[:, 0, :], a["c"].rearrange("o (p k) -> p (o k)", k=KC)).then_inc(c_loaded, 16)
                sp.dma_start(craw[:, 1, :], a["c_ctx"].rearrange("(p k) -> p k", k=KC)).then_inc(c_loaded, 16)
                with sp.Fori(0, NCH // RG) as i:
                    for q in range(RG):
                        sp.wait_ge(used[q], i)
                        sp.wait_ge(row_ready[q], i)
                        sp.dma_start(w[:, q], a["w_mod"][0][:, ds((i * RG + q) * BANK, BANK)]
                                     .rearrange("(p k) n -> p k n", k=KC)).then_inc(loaded[q], 16)
                        sp.dma_start(bias[:, q], a["b_mod"][0:1, ds((i * RG + q) * BANK, BANK)]
                                     .broadcast_to([2, BANK])).then_inc(loaded[q], 16)

            @block.scalar
            def _(act):
                act.wait_ge(c_loaded, 32)
                act.activation(den[:, :, :], craw[:, :, :], ACT.Exp, scale=-1.0).then_inc(exp_done, 1)
                for n, key in enumerate(("a_lq1", "a_lk1", "a_lq2", "a_lk2")):
                    act.dma_start(v[:, n, :], rows(a[key])).then_inc(v_loaded, 16)
                act.dma_start(m.sink[:, :], rows(a["b_sink"])).then_inc(v_loaded, 16)
                act.dma_start(m.band[:, :, :], a["band"].rearrange("s p k -> p s k")).then_inc(streams_loaded, 16)
                act.dma_start(m.R[:, 0:CT, :], a["ctx"].rearrange("b (t p) d -> p (b t) d", p=P)).then_inc(streams_loaded, 16)
                act.dma_start(m.R[:, CT:NT, :], a["x"].rearrange("b (t p) d -> p (b t) d", p=P)).then_inc(streams_loaded, 16)
                act.dma_start(m.ident[:, :], a["ident"]).then_inc(streams_loaded, 16)
                act.wait_ge(dots_ready, 1)
                act.activation(dots[:, :], dots[:, :], ACT.Exp).then_inc(lam_exp_done, 1)
                act.wait_ge(streams_loaded, 64)

            @block.tensor
            def _(pe):
                pe.wait_ge(silu_done, 1)
                with pe.Fori(0, NCH // RG) as i:
                    for q in range(RG):
                        pe.wait_ge(loaded[q], i * 32 + 32)
                        pe.wait_ge(row_ready[q], i)
                        for k in range(KC):
                            mm = pe.matmul(m.ps[0:2, q, :], m.csil[:, k, 2:4], w[:, q, k, :],
                                           start=(k == 0), stop=(k == KC - 1))
                        mm.then_inc(used[q], 1)

            @block.vector
            def _(dve):
                dve.memset(m.csil[:, :, :], 0.0)
                dve.wait_ge(exp_done, 1)
                dve.tensor_scalar(den[:, :, :], den[:, :, :], 1.0, None, ALU.add)
                dve.drain()
                dve.reciprocal(den[:, :, :], den[:, :, :])
                dve.drain()
                dve.tensor_tensor(m.csil[:, :, 2:4].rearrange("p k s -> p s k"), craw[:, :, :], den[:, :, :],
                                  ALU.mult).then_inc(silu_done, 1)
                dve.memset(m.eps[:, :], EPS)
                dve.wait_ge(v_loaded, 80)
                for n in range(2):
                    dve.scalar_tensor_tensor(out=junk[:, n, :], in0=v[:, 2 * n, :], scalar=1.0, in1=v[:, 2 * n + 1, :],
                                             op0=ALU.mult, op1=ALU.mult, accum_out=dots[:, n:n + 1])
                dve.tensor_scalar(m.neg_sink[:, :], m.sink[:, :], -1.0, None, ALU.mult)
                dve.drain()
                dve.sem_inc(dots_ready, 1)
                dve.wait_ge(lam_exp_done, 1)
                dve.scalar_tensor_tensor(out=m.neg_lam[:, :], in0=dots[:, 1:2], scalar=-LAM_INIT, in1=dots[:, 0:1],
                                         op0=ALU.add, op1=ALU.subtract)
                with dve.Fori(0, NCH // RG) as i:
                    for q in range(RG):
                        dve.wait_ge(used[q], i + 1)
                        dve.wait_ge(row_stored[q], i * 16)
                        dve.tensor_tensor(row[:, q, :], m.ps[0:2, q, :], bias[:, q, :], ALU.add)\
                           .then_inc(row_ready[q], 1)

            @block.gpsimd
            def _(pool):
                with pool.Fori(0, NCH // RG) as i:
                    for q in range(RG):
                        pool.wait_ge(row_ready[q], i + 1)
                        pool.dma_start(m.mods[0][:, ds((i * RG + q) * BANK, BANK)], row[:, q, :]).then_inc(row_stored[q], 16)
                for q in range(RG):
                    pool.wait_ge(row_stored[q], NCH // RG * 16)


def modulated_norm(nc, m, a, layer, sub, gain_name, tiles, prefetch=None):
    shift_at, scale_at = 3 * sub * D, (3 * sub + 1) * D
    with Stage(nc, f"n{layer}{sub}") as s:
        gain = s.sb("gain", [P, D])
        scale, shift = s.sb("scale", [P, 2, D]), s.sb("shift", [P, 2, D])
        sq = s.sb("sq", [P, D])
        ss = s.sb("ss", [P, NT])
        loaded, rms_ready, h_ready = s.sem("loaded"), s.sem("rms_ready"), s.sem("h_ready")
        turned, copied = s.sem("turned"), s.sem("copied")
        with nc.Block() as block:
            @block.sync
            def _(sp):
                sp.dma_start(gain[:, :], rows(a[gain_name][layer:layer + 1, :])).then_inc(loaded, 16)
                for st in range(2):
                    sp.dma_start(scale[:, st, :], rows(m.mods[layer, st:st + 1, scale_at:scale_at + D])).then_inc(loaded, 16)
                    sp.dma_start(shift[:, st, :], rows(m.mods[layer, st:st + 1, shift_at:shift_at + D])).then_inc(loaded, 16)
                if prefetch:
                    prefetch(sp)

            @block.scalar
            def _(act):
                for t in tiles:
                    act.activation(sq[:, :], m.R[:, t, :], ACT.Square, accum_out=ss[:, t:t + 1])
                    act.drain()
                act.activation(ss[:, tiles[0]:NT], ss[:, tiles[0]:NT], ACT.Sqrt, bias=m.eps[:, :],
                               scale=1.0 / D).then_inc(rms_ready, 1)
                for n, t in enumerate(tiles):
                    act.wait_ge(turned, n + 1)
                    act.copy(m.hT[:, :, t * P:(t + 1) * P],
                             m.ps[:, 2 * (n % 2):2 * (n % 2) + 2, :].rearrange("p b (k c) -> p (b k) c", c=P))\
                       .then_inc(copied, 1)

            @block.vector
            def _(dve):
                dve.wait_ge(loaded, 80)
                for st in range(2):
                    dve.scalar_tensor_tensor(out=scale[:, st, :], in0=scale[:, st, :], scalar=1.0,
                                             in1=gain[:, :], op0=ALU.add, op1=ALU.mult)
                dve.wait_ge(rms_ready, 1)
                dve.reciprocal(ss[:, tiles[0]:NT], ss[:, tiles[0]:NT])
                dve.drain()
                for t in tiles:
                    st = 1 if t < CT else 0
                    dve.scalar_tensor_tensor(out=m.H[:, t, :], in0=m.R[:, t, :], scalar=ss[:, t:t + 1],
                                             in1=scale[:, st, :], op0=ALU.mult, op1=ALU.mult)
                    dve.drain()
                    dve.tensor_tensor(m.H[:, t, :], m.H[:, t, :], shift[:, st, :], ALU.add).then_inc(h_ready, 1)

            @block.tensor
            def _(pe):
                for n, t in enumerate(tiles):
                    pe.wait_ge(h_ready, n + 1)
                    if n >= 2:
                        pe.wait_ge(copied, n - 1)
                    for k in range(KC):
                        tr = pe.transpose(m.ps[:, 2 * (n % 2) + k // 4, (k % 4) * P:(k % 4 + 1) * P],
                                          m.H[:, t, k * P:(k + 1) * P], m.ident[:, :])
                    tr.then_inc(turned, 1)


def turn_h(nc, m, name, tiles, prefetch):
    with Stage(nc, name) as s:
        turned, copied = s.sem("turned"), s.sem("copied")
        with nc.Block() as block:
            @block.sync
            def _(sp):
                prefetch(sp)

            @block.tensor
            def _(pe):
                for n, t in enumerate(tiles):
                    if n >= 2:
                        pe.wait_ge(copied, n - 1)
                    for k in range(KC):
                        tr = pe.transpose(m.ps[:, 2 * (n % 2) + k // 4, (k % 4) * P:(k % 4 + 1) * P],
                                          m.H[:, t, k * P:(k + 1) * P], m.ident[:, :])
                    tr.then_inc(turned, 1)

            @block.scalar
            def _(act):
                for n, t in enumerate(tiles):
                    act.wait_ge(turned, n + 1)
                    act.copy(m.hT[:, :, t * P:(t + 1) * P],
                             m.ps[:, 2 * (n % 2):2 * (n % 2) + 2, :].rearrange("p b (k c) -> p (b k) c", c=P))\
                       .then_inc(copied, 1)


class ProjectWeights:

    def __init__(self, nc, m, s, weight, chunk, gate=None):
        self.weight, self.chunk, self.gate = weight, chunk, gate
        self.pairs = weight.shape[1] // chunk // 2
        self.w = s.sb("w", [P, 2, KC, chunk])
        self.loaded = s.sems("loaded", 2)
        if gate is not None:
            self.g, self.g_loaded = s.sb("g", [P, 2, D]), s.sem("g_loaded")

    def load(self, sp, q, i):
        sp.dma_start(self.w[:, q], self.weight[:, ds((i * 2 + q) * self.chunk, self.chunk)]
                     .rearrange("(k p) n -> p k n", p=P)).then_inc(self.loaded[q], 16)

    def prefetch(self, sp):
        for q in range(2):
            self.load(sp, q, 0)
        if self.gate is not None:
            for st in range(2):
                sp.dma_start(self.g[:, st, :], rows(self.gate[st:st + 1, :])).then_inc(self.g_loaded, 16)


def project(nc, m, name, pre, tiles, out=None):
    pairs, chunk, gate, w, loaded = pre.pairs, pre.chunk, pre.gate, pre.w, pre.loaded
    n_t = len(tiles)
    body = 2 * n_t
    with Stage(nc, name) as s:
        used = s.sems("used", 2)
        done, free = s.sems("done", 4), s.sems("free", 4)
        if gate is not None:
            g, g_loaded = pre.g, pre.g_loaded
            tmp = s.sb("tmp", [P, 2, chunk])
            scaled, added = s.sem("scaled"), s.sem("added")
        with nc.Block() as block:
            @block.sync
            def _(sp):
                for i in range(1, pairs):
                    for q in range(2):
                        sp.wait_ge(used[q], i)
                        pre.load(sp, q, i)

            @block.tensor
            def _(pe):
                with repeat(pe, pairs) as i:
                    for q in range(2):
                        pe.wait_ge(loaded[q], i * 16 + 16)
                        for n, t in enumerate(tiles):
                            b, use = (q * n_t + n) % 4, (q * n_t + n) // 4
                            pe.wait_ge(free[b], i * (body // 4) + use)
                            for k in range(KC):
                                mm = pe.matmul(m.ps[:, b, 0:chunk], m.hT[:, k, t * P:(t + 1) * P], w[:, q, k, :],
                                               start=(k == 0), stop=(k == KC - 1))
                            mm.then_inc(done[b], 1)
                            if n == n_t - 1:
                                pe.drain()
                                pe.sem_inc(used[q], 1)

            if gate is None:
                def evict(eng, copy, parity):
                    with repeat(eng, pairs) as i:
                        for c in range(parity, body, 2):
                            q, t, b, use = c // n_t, tiles[c % n_t], c % 4, c // 4
                            eng.wait_ge(done[b], i * (body // 4) + use + 1)
                            copy(out[:, t, ds((i * 2 + q) * chunk, chunk)], m.ps[:, b, 0:chunk]).then_inc(free[b], 1)

                @block.scalar
                def _(act):
                    evict(act, act.copy, 0)

                @block.vector
                def _(dve):
                    evict(dve, dve.tensor_copy, 1)
            else:
                @block.vector
                def _(dve):
                    dve.wait_ge(g_loaded, 32)
                    for c in range(body):
                        q, t, b, use = c // n_t, tiles[c % n_t], c % 4, c // 4
                        cols = slice(q * chunk, (q + 1) * chunk)
                        dve.wait_ge(done[b], use + 1)
                        if c >= 2:
                            dve.wait_ge(added, c - 1)
                        dve.tensor_tensor(tmp[:, c % 2, :], m.ps[:, b, 0:chunk], g[:, 1 if t < CT else 0, cols],
                                          ALU.mult).then_inc(free[b], 1)
                        dve.drain()
                        dve.sem_inc(scaled, 1)

                @block.gpsimd
                def _(pool):
                    for c in range(body):
                        q, t = c // n_t, tiles[c % n_t]
                        cols = slice(q * chunk, (q + 1) * chunk)
                        pool.wait_ge(scaled, c + 1)
                        pool.tensor_tensor(m.R[:, t, cols], m.R[:, t, cols], tmp[:, c % 2, :], ALU.add)\
                            .then_inc(added, 1)


def head_norm(nc, m, a, name, buf, tiles, segs, rope=None, factor=1.0, beside=None):
    turns = len(tiles) // 2
    extra = None
    S = sum(g * d for _, g, d, _ in segs)
    G = sum(g for _, g, _, _ in segs)
    with Stage(nc, name) as s:
        sq = s.sb("sq", [P, 2, S])
        ss = s.sb("ss", [P, 2, G])
        gains = s.sb("gains", [P, sum(d for _, _, d, _ in segs)])
        loaded = s.sem("loaded")
        squared, summed, rooted = s.sems("squared", 2), s.sems("summed", 2), s.sems("rooted", 2)
        if rope:
            r0, nr, tables = rope
            cos, sin = s.sb("cos", [P, NT, nr]), s.sb("sin", [P, NT, nr])
            near, far = s.sb("near", [P, 2, G, nr]), s.sb("far", [P, 2, G, nr])
            scaled, near_ready = s.sems("scaled", 2), s.sems("near_ready", 2)

        if beside:
            extra = beside(nc, m, a, s)

        def parts(i, q):
            at = g0 = gain0 = 0
            for c, g, d, _ in segs:
                yield (buf[:, i * 2 + q + (tiles[0] if tiles[0] and buf.shape[1] == NT else 0), c:c + g * d]
                       .rearrange("p (g d) -> p g d", d=d),
                       sq[:, q, at:at + g * d].rearrange("p (g d) -> p g d", d=d), ss[:, q, g0:g0 + g],
                       gains[:, gain0:gain0 + d], g, d, g0)
                at, g0, gain0 = at + g * d, g0 + g, gain0 + d

        def table(tab, i, q, g):
            return tab[:, ds(i * 2 + q + tiles[0], 1), :].broadcast_to([P, g, nr])

        def pairs(x, which):
            return x.rearrange("p g (f two) -> p g f two", two=2)[:, :, :, which]

        with nc.Block() as block:
            @block.sync
            def _(sp):
                at = 0
                for _, _, d, gain in segs:
                    sp.dma_start(gains[:, at:at + d], rows(gain)).then_inc(loaded, 16)
                    at += d
                if rope:
                    sp.dma_start(cos[:, :, :], a[tables + "_cos"].rearrange("(t p) d -> p t d", p=P)).then_inc(loaded, 16)
                    sp.dma_start(sin[:, :, :], a[tables + "_sin"].rearrange("(t p) d -> p t d", p=P)).then_inc(loaded, 16)

                if extra:
                    extra.sync(sp)

            if extra:
                @block.tensor
                def _(pe):
                    extra.tensor(pe)

            n_loads = len(segs) + (2 if rope else 0)

            @block.scalar
            def _(act):
                with repeat(act, turns) as i:
                    for q in range(2):
                        act.wait_ge(rooted[q], i)
                        act.wait_ge(summed[q], i)
                        for x, x2, *_ in parts(i, q):
                            sqr = act.activation(x2, x, ACT.Square)
                        sqr.then_inc(squared[q], 1)
                    for q in range(2):
                        act.wait_ge(summed[q], i + 1)
                        for x, x2, r, gn, g, d, g0 in parts(i, q):
                            root = act.activation(r, r, ACT.Sqrt, bias=m.eps[:, :], scale=1.0 / d)
                        root.then_inc(rooted[q], 1)

            @block.vector
            def _(dve):
                dve.wait_ge(loaded, 16 * n_loads)
                if factor != 1.0:
                    dve.tensor_scalar(gains[:, :], gains[:, :], factor, None, ALU.mult)
                    dve.drain()
                with repeat(dve, turns) as i:
                    for q in range(2):
                        dve.wait_ge(squared[q], i + 1)
                        for x, x2, r, gn, g, d, g0 in parts(i, q):
                            red = dve.tensor_reduce(r, x2, AX.X, ALU.add)
                        red.then_inc(summed[q], 1)
                    for q in range(2):
                        dve.wait_ge(rooted[q], i + 1)
                        dve.reciprocal(ss[:, q, :], ss[:, q, :])
                        dve.drain()
                        for x, x2, r, gn, g, d, g0 in parts(i, q):
                            dve.tensor_tensor(x, x, r.unsqueeze(2).broadcast_to([P, g, d]), ALU.mult)
                        dve.drain()
                        for x, x2, r, gn, g, d, g0 in parts(i, q):
                            mul = dve.tensor_tensor(x, x, gn.unsqueeze(1).broadcast_to([P, g, d]), ALU.mult)
                        if rope:
                            mul.then_inc(scaled[q], 1)
                            dve.drain()
                            for x, x2, r, gn, g, d, g0 in parts(i, q):
                                tail, f = x[:, :, r0:r0 + nr], far[:, q, g0:g0 + g, :]
                                tab = table(sin, i, q, g)
                                for e in range(2):
                                    dve.tensor_tensor(pairs(f, e), pairs(tail, 1 - e), pairs(tab, e), ALU.mult)
                            dve.drain()
                            dve.wait_ge(near_ready[q], i + 1)
                            for x, x2, r, gn, g, d, g0 in parts(i, q):
                                dve.tensor_tensor(x[:, :, r0:r0 + nr], near[:, q, g0:g0 + g, :],
                                                  far[:, q, g0:g0 + g, :], ALU.add)
                if extra:
                    extra.vector(dve)

            if rope:
                @block.gpsimd
                def _(pool):
                    pool.wait_ge(loaded, 16 * n_loads)
                    with repeat(pool, turns) as i:
                        for q in range(2):
                            pool.wait_ge(scaled[q], i + 1)
                            for x, x2, r, gn, g, d, g0 in parts(i, q):
                                mul = pool.tensor_tensor(near[:, q, g0:g0 + g, :], x[:, :, r0:r0 + nr],
                                                         table(cos, i, q, g), ALU.mult)
                            mul.then_inc(near_ready[q], 1)


def attention(nc, m, kind, scale, turns, maps, dq, dv, tiles, blocks_of, q_of, k_of, v_of, out_of):
    per = 2 if kind == "A" else 1
    jobs = [(t, mp) for t in tiles for mp in range(maps)]
    vals = jobs if per == 1 else [(t, 0) for t in tiles]
    NS, NV, NQ = len(jobs), len(vals), len(tiles)
    W = NT * P

    def runs(t):
        out = []
        for j, kt in enumerate(blocks_of(t)):
            if out and (j * P) % BANK and out[-1][1] + out[-1][2] == kt:
                out[-1][2] += 1
            else:
                out.append([j * P, kt, 1])
        return out

    with Stage(nc, f"at{kind}") as s:
        wq_ = dq if maps == 1 else 2 * dq
        q_in, k_in = s.sb("q_in", [P, NQ, wq_]), s.sb("k_in", [P, NT, wq_])
        qT, kT = s.sb("qT", [P, NQ * P]), s.sb("kT", [P, TOK])
        probs = s.sb("probs", [P, 4, W])
        probsT = s.sb("probsT", [P, 2, W])
        top, bias, den, rec = (s.sb(x, [P, 4]) for x in ("top", "bias", "den", "rec"))
        if kind == "A":
            mixed = s.sb("mixed", [P, 2, W])
            mixed_ready = s.sems("mixed_ready", 2)
        if kind == "B":
            sunk = s.sb("sunk", [P, 4])
        staged, q_turned, k_turned, q_ready, k_ready = (s.sem(x) for x in (
            "staged", "q_turned", "k_turned", "q_ready", "k_ready"))
        scored, biased, exped = s.sems("scored", 2), s.sems("biased", 2), s.sems("exped", 2)
        probs_turned, probsT_ready = s.sem("probs_turned"), s.sem("probsT_ready")
        valued, taken = s.sems("valued", 2), s.sems("taken", 2)

        def width(n):
            return len(blocks_of(jobs[n][0])) * P

        def score_bank(n):
            return m.ps[:, 2 * (n % 2):2 * (n % 2) + 2, :].rearrange("p b c -> p (b c)")

        turn_bank = m.ps[:, 4:6, :].rearrange("p b c -> p (b c)")
        k_bank = m.ps[:, 6:8, :].rearrange("p b c -> p (b c)")

        with nc.Block() as block:
            @block.gpsimd
            def _(pool):
                with pool.Fori(0, turns) as i:
                    pool.wait_ge(k_turned, i)
                    pool.sem_inc(staged, 1)
                    pool.tensor_copy(q_in[:, :, :], q_of(pool, i))
                    for part, src in k_of(pool, i):
                        last = pool.tensor_copy(k_in[:, :, part], src)
                    last.then_inc(staged, 1)

            @block.tensor
            def _(pe):
                with pe.Fori(0, turns) as i:
                    pe.wait_ge(staged, 2 * i + 2)
                    pe.wait_ge(probsT_ready, i * NV)
                    for n in range(NQ):
                        tr = pe.transpose(turn_bank[0:wq_, n * P:(n + 1) * P], q_in[:, n, :], m.ident[:, :])
                    tr.then_inc(q_turned, 1)
                    for b in range(2):
                        pe.wait_ge(taken[b], i * (NV // 2))
                    for n in range(NT):
                        tr = pe.transpose(k_bank[0:wq_, n * P:(n + 1) * P], k_in[:, n, :], m.ident[:, :])
                    tr.then_inc(k_turned, 1)
                    pe.wait_ge(q_ready, i + 1)
                    pe.wait_ge(k_ready, i + 1)

                    def score(n):
                        t, mp = jobs[n]
                        r = slice(mp * dq, (mp + 1) * dq)
                        pe.wait_ge(exped[n % 2], i * (NS // 2) + n // 2)
                        for c, kt, cnt in runs(t):
                            mm = pe.matmul(score_bank(n)[:, c:c + cnt * P], qT[r, tiles.index(t) * P:(tiles.index(t) + 1) * P],
                                           kT[r, kt * P:(kt + cnt) * P], start=True, stop=True)
                        mm.then_inc(scored[n % 2], 1)

                    def turn(v):
                        if per == 2:
                            pe.wait_ge(mixed_ready[v % 2], i * (NV // 2) + v // 2 + 1)
                            src = mixed[:, v % 2, :]
                        else:
                            pe.wait_ge(exped[v % 2], i * (NS // 2) + v // 2 + 1)
                            src = probs[:, v % 4, :]
                        pe.wait_ge(probsT_ready, i * NV + v)
                        for j in range(len(blocks_of(vals[v][0]))):
                            tr = pe.transpose(turn_bank[:, j * P:(j + 1) * P], src[:, j * P:(j + 1) * P], m.ident[:, :])
                        tr.then_inc(probs_turned, 1)

                    def value(v):
                        pe.wait_ge(probsT_ready, i * NV + v + 1)
                        pe.wait_ge(taken[v % 2], i * (NV // 2) + v // 2)
                        bl = blocks_of(vals[v][0])
                        for j, kt in enumerate(bl):
                            mm = pe.matmul(m.ps[:, 6 + v % 2, 0:dv], probsT[:, v % 2, j * P:(j + 1) * P],
                                           v_of(pe, i, kt), start=(j == 0), stop=(j == len(bl) - 1))
                        mm.then_inc(valued[v % 2], 1)

                    for n in range(per):
                        score(n)
                    for v in range(NV):
                        for n in range((v + 1) * per, min((v + 2) * per, NS)):
                            score(n)
                        turn(v)
                        if v:
                            value(v - 1)
                    value(NV - 1)

            @block.vector
            def _(dve):
                with dve.Fori(0, turns) as i:
                    dve.wait_ge(k_turned, i + 1)
                    dve.tensor_copy(kT[0:wq_, :], k_bank[0:wq_, 0:TOK]).then_inc(k_ready, 1)

                    def find_max(n):
                        t, mp = jobs[n]
                        sl = slice(n % 4, n % 4 + 1)
                        dve.wait_ge(scored[n % 2], i * (NS // 2) + n // 2 + 1)
                        if kind == "B" and t >= CT:
                            for j, kt in enumerate(blocks_of(t)):
                                if kt >= CT and kt != t:
                                    cols = score_bank(n)[:, j * P:(j + 1) * P]
                                    dve.tensor_tensor(cols, cols, m.band[:, 0 if kt < t else 1, :], ALU.add)
                            dve.drain()
                        dve.tensor_reduce(top[:, sl], score_bank(n)[:, 0:width(n)], AX.X, ALU.max)
                        dve.drain()
                        if kind == "B":
                            b = dve.tensor_scalar(bias[:, sl], top[:, sl], -scale, m.neg_sink[:, ds(i * 2 + mp, 1)],
                                                  ALU.mult, ALU.min)
                        else:
                            b = dve.tensor_scalar(bias[:, sl], top[:, sl], -scale, None, ALU.mult)
                        b.then_inc(biased[n % 2], 1)

                    def mix(v):
                        for b in range(2):
                            dve.wait_ge(exped[b], i * (NS // 2) + v + 1)
                        c0 = (2 * v) % 4
                        w = width(2 * v)
                        dve.reciprocal(rec[:, c0:c0 + 2], den[:, c0:c0 + 2])
                        dve.drain()
                        dve.tensor_scalar(rec[:, c0 + 1:c0 + 2], rec[:, c0 + 1:c0 + 2], m.neg_lam[:, :], None, ALU.mult)
                        dve.tensor_scalar(mixed[:, v % 2, 0:w], probs[:, c0, 0:w], rec[:, c0:c0 + 1], None, ALU.mult)
                        dve.drain()
                        dve.scalar_tensor_tensor(out=mixed[:, v % 2, 0:w], in0=probs[:, c0 + 1, 0:w],
                                                 scalar=rec[:, c0 + 1:c0 + 2], in1=mixed[:, v % 2, 0:w],
                                                 op0=ALU.mult, op1=ALU.add).then_inc(mixed_ready[v % 2], 1)

                    def take(v):
                        t, mp = vals[v]
                        sl = slice(v % 4, v % 4 + 1)
                        if per == 1:
                            dve.wait_ge(exped[v % 2], i * (NS // 2) + v // 2 + 1)
                            if kind == "B":
                                dve.tensor_tensor(den[:, sl], den[:, sl], sunk[:, sl], ALU.add)
                                dve.drain()
                            dve.reciprocal(rec[:, sl], den[:, sl])
                            dve.drain()
                        dve.wait_ge(valued[v % 2], i * (NV // 2) + v // 2 + 1)
                        src, dst = m.ps[:, 6 + v % 2, 0:dv], out_of(i, t, mp)
                        if per == 2:
                            o = dve.tensor_copy(dst, src)
                        else:
                            o = dve.tensor_scalar(dst, src, rec[:, sl], None, ALU.mult)
                        o.then_inc(taken[v % 2], 1)

                    for n in range(per):
                        find_max(n)
                    for v in range(NV):
                        if per == 2:
                            mix(v)
                        for n in range((v + 1) * per, min((v + 2) * per, NS)):
                            find_max(n)
                        if v:
                            take(v - 1)
                    take(NV - 1)

            @block.scalar
            def _(act):
                with act.Fori(0, turns) as i:
                    act.wait_ge(q_turned, i + 1)
                    act.copy(qT[0:wq_, :], turn_bank[0:wq_, 0:NQ * P]).then_inc(q_ready, 1)

                    def exponential(n):
                        mp = jobs[n][1]
                        sl = slice(n % 4, n % 4 + 1)
                        act.wait_ge(biased[n % 2], i * (NS // 2) + n // 2 + 1)
                        e = act.activation(probs[:, n % 4, 0:width(n)], score_bank(n)[:, 0:width(n)], ACT.Exp,
                                           bias=bias[:, sl], scale=scale, accum_out=den[:, sl])
                        if kind == "B":
                            e = act.activation(sunk[:, sl], m.sink[:, ds(i * 2 + mp, 1)], ACT.Exp, bias=bias[:, sl])
                        e.then_inc(exped[n % 2], 1)

                    def copy_turned(v):
                        w = len(blocks_of(vals[v][0])) * P
                        act.wait_ge(probs_turned, i * NV + v + 1)
                        act.copy(probsT[:, v % 2, 0:w], turn_bank[:, 0:w]).then_inc(probsT_ready, 1)

                    for n in range(per):
                        exponential(n)
                    for v in range(NV):
                        for n in range((v + 1) * per, min((v + 2) * per, NS)):
                            exponential(n)
                        copy_turned(v)


def differential_attention(nc, m):
    attention(nc, m, "A", A_DQK ** -0.5, A_HEADS, 2, A_DQK, A_DV, list(range(NT)),
              lambda t: list(range(NT if t >= CT else CT)),
              lambda e, i: m.Z[:, :, ds(AQ + i * 2 * A_DQK, 2 * A_DQK)],
              lambda e, i: [(slice(0, 2 * A_DQK), m.Z[:, :, ds(AK + i * 2 * A_DQK, 2 * A_DQK)])],
              lambda e, i, kt: m.Z[:, kt, ds(AV + i * A_DV, A_DV)],
              lambda i, t, mp: m.H[:, t, ds(i * A_DV, A_DV)])


def windowed_attention(nc, m):
    def blocks_of(t):
        if t < CT:
            return list(range(CT))
        return list(range(CT)) + list(range(max(t - 1, CT), min(t + 1, NT - 1) + 1))

    def kv(e, i):
        return e.snap(i // 2)

    def k_of(e, i):
        src = m.Z[:, :, ds(kv(e, i) * B_DH + BK, B_DH)]
        return [(slice(0, B_DH), src), (slice(B_DH, 2 * B_DH), src)]

    attention(nc, m, "B", B_DH ** -0.5, B_HEADS // 2, 2, B_DH, B_DH, list(range(NT)), blocks_of,
              lambda e, i: m.Z[:, :, ds(BQ + i * 2 * B_DH, 2 * B_DH)], k_of,
              lambda e, i, kt: m.Z[:, kt, ds(kv(e, i) * B_DH + BV, B_DH)],
              lambda i, t, mp: m.H[:, t, ds(A_HEADS * A_DV + (i * 2 + mp) * B_DH, B_DH)])


def latent_up(nc, m, a):
    QW, KVW, GW = C_HEADS * C_DQ, C_HEADS * (C_NOPE + C_DV), 2 * G_HEADS * G_DK
    with Stage(nc, "up") as s:
        wq, wkv, wg = s.sb("wq", [P, 2, QW]), s.sb("wkv", [P, KVW]), s.sb("wg", [2 * G_RANK, GW])
        gate_bias = s.sb("gate_bias", [P, GW])
        lat = s.sb("lat", [P, 2, 4, P])
        cleared, loaded = s.sem("cleared"), s.sem("loaded")
        turned, lat_ready = s.sem("turned"), s.sem("lat_ready")
        upped, act_taken, dve_taken = s.sem("upped"), s.sem("act_taken"), s.sem("dve_taken")
        with nc.Block() as block:
            @block.sync
            def _(sp):
                half = GW // 2
                sp.wait_ge(cleared, 1)
                sp.dma_start(wg[0:G_RANK, 0:half], a["d_wg_f"][0]).then_inc(loaded, 16)
                sp.dma_start(wg[G_RANK:2 * G_RANK, half:GW], a["d_wg_b"][0]).then_inc(loaded, 16)
                sp.dma_start(gate_bias[:, 0:half], rows(a["d_bg_f"])).then_inc(loaded, 16)
                sp.dma_start(gate_bias[:, half:GW], rows(a["d_bg_b"])).then_inc(loaded, 16)
                sp.dma_start(wq[:, :, :], a["c_wq_up"][0].rearrange("(k p) n -> p k n", p=P)).then_inc(loaded, 16)
                sp.dma_start(wkv[:, :], a["c_wkv_up"][0]).then_inc(loaded, 16)

            @block.tensor
            def _(pe):
                def turn(t):
                    if t >= 2:
                        pe.wait_ge(lat_ready, t - 1)
                    cols = [CKV, GF] + ([CQ, CQ + P] if t >= CT else [])
                    for n, c in enumerate(cols):
                        w = 2 * G_RANK if c == GF else P
                        tr = pe.transpose(m.ps[0:w, t % 2, n * P:(n + 1) * P], m.Z[:, t, c:c + w], m.ident[:, :])
                    tr.then_inc(turned, 1)

                def up(t):
                    pe.wait_ge(lat_ready, t + 1)
                    if t >= 1:
                        pe.wait_ge(act_taken, t)
                        pe.wait_ge(dve_taken, t)
                    for h in range(2):
                        mm = pe.matmul(m.ps[:, 2 + h, :], lat[:, t % 2, 0, :], wkv[:, h * BANK:(h + 1) * BANK], start=True, stop=True)
                    mm = pe.matmul(m.ps[:, 4, :], lat[0:2 * G_RANK, t % 2, 1, :], wg[:, :], start=True, stop=True)
                    if t >= CT:
                        for c, w in ((0, BANK), (BANK, QW - BANK)):
                            for k in range(2):
                                mm = pe.matmul(m.ps[:, 6 + c // BANK, 0:w], lat[:, t % 2, 2 + k, :], wq[:, k, c:c + w],
                                               start=(k == 0), stop=(k == 1))
                    mm.then_inc(upped, 1)

                pe.wait_ge(loaded, 96)
                for t in range(NT):
                    turn(t)
                    if t:
                        up(t - 1)
                up(NT - 1)

            @block.scalar
            def _(act):
                def take(t):
                    act.wait_ge(upped, t + 1)
                    c = act.copy(m.KV[:, t, :], m.ps[:, 2:4, :].rearrange("p b c -> p (b c)"))
                    if t >= CT:
                        c = act.copy(m.Q[:, t - CT, :], m.ps[:, 6:8, :].rearrange("p b c -> p (b c)")[:, 0:QW])
                    c.then_inc(act_taken, 1)

                for t in range(NT):
                    act.wait_ge(turned, t + 1)
                    n = 4 if t >= CT else 1
                    act.copy(lat[0:2 * G_RANK, t % 2, 1, :], m.ps[0:2 * G_RANK, t % 2, P:2 * P])
                    if t >= CT:
                        act.copy(lat[:, t % 2, 2:4, :].rearrange("p k c -> p (k c)"), m.ps[:, t % 2, 2 * P:4 * P])
                    act.copy(lat[:, t % 2, 0, :], m.ps[:, t % 2, 0:P]).then_inc(lat_ready, 1)
                    if t:
                        take(t - 1)
                take(NT - 1)

            @block.vector
            def _(dve):
                dve.memset(wg[:, :], 0.0).then_inc(cleared, 1)
                dve.wait_ge(loaded, 96)
                for t in range(NT):
                    dve.wait_ge(upped, t + 1)
                    dve.tensor_tensor(m.LG[:, t, :], m.ps[:, 4, :], gate_bias[:, :], ALU.add).then_inc(dve_taken, 1)

            @block.gpsimd
            def _(pool):
                for t in range(NT):
                    pool.wait_ge(act_taken, t + 1)
                    kh = m.K[:, t, :].rearrange("p (h d) -> p h d", d=C_DQ)
                    pool.tensor_copy(kh[:, :, 0:C_NOPE], m.KV[:, t, :].rearrange("p (h d) -> p h d", h=C_HEADS)[:, :, 0:C_NOPE])
                    pool.tensor_copy(kh[:, :, C_NOPE:C_DQ], m.Z[:, t, KPE:KPE + C_ROPE].unsqueeze(1)
                                     .broadcast_to([P, C_HEADS, C_ROPE]))


def latent_attention(nc, m):
    KVD = C_NOPE + C_DV
    attention(nc, m, "C", C_DQ ** -0.5, C_HEADS, 1, C_DQ, C_DV, list(range(CT, NT)), lambda t: list(range(NT)),
              lambda e, i: m.Q[:, :, ds(i * C_DQ, C_DQ)],
              lambda e, i: [(slice(0, C_DQ), m.K[:, :, ds(i * C_DQ, C_DQ)])],
              lambda e, i, kt: m.KV[:, kt, ds(i * KVD + C_NOPE, C_DV)],
              lambda i, t, mp: m.H[:, t, ds(i * C_DV, C_DV)])


def linear_attention(nc, m, a):
    KW = G_HEADS * G_DK
    W = 2 * KW
    NCH = NT * P // G_CHUNK
    CCH, XCH = CT * 2, XT * 2
    VW = G_HEADS * G_DV
    with ExitStack() as ctx:
        sb = lambda name, shape: ctx.enter_context(nc.sbuf_tensor("gla_" + name, shape, F32))
        tri = sb("tri", [P, 3, P])
        qT, kT = sb("qT", [P, 4, XT * P]), sb("kT", [P, 4, XT * P])
        decay = sb("decay", [P, 4, NCH])
        state = sb("state", [P, 2, NCH + 1, 2 * G_DV])

        with Stage(nc, "gg") as s:
            one = s.sb("one", [P, 1])
            soft = s.sb("soft", [P, NT, W])
            loaded, one_ready, soft_ready = s.sem("loaded"), s.sem("one_ready"), s.sem("soft_ready")
            with nc.Block() as block:
                @block.sync
                def _(sp):
                    sp.dma_start(tri[:, :, :], a["tri"].rearrange("s p c -> p s c")).then_inc(loaded, 16)
                    sp.wait_ge(loaded, 16)

                @block.scalar
                def _(act):
                    act.wait_ge(one_ready, 1)
                    act.activation(soft[:, :, :], m.LG[:, :, :], ACT.Abs)
                    act.drain()
                    act.activation(soft[:, :, :], soft[:, :, :], ACT.Exp, scale=-1.0)
                    act.drain()
                    act.activation(soft[:, :, :], soft[:, :, :], ACT.Ln, bias=one[:, :]).then_inc(soft_ready, 1)

                @block.vector
                def _(dve):
                    dve.memset(one[:, :], 1.0).then_inc(one_ready, 1)
                    dve.wait_ge(soft_ready, 1)
                    dve.scalar_tensor_tensor(out=m.LG[:, :, :], in0=m.LG[:, :, :], scalar=0.0, in1=soft[:, :, :],
                                             op0=ALU.min, op1=ALU.subtract)
                    dve.drain()
                    dve.tensor_scalar(m.LG[:, :, :], m.LG[:, :, :], 1.0 / G_TAU, None, ALU.mult)

        with Stage(nc, "gs") as s:
            up, down, stay = (s.sb(x, [P, 2, W]) for x in ("up", "down", "stay"))
            summed, exped, diffed = s.sem("summed"), s.sem("exped"), s.sem("diffed")
            stay_ready, scaled, banks_free = s.sem("stay_ready"), s.sem("scaled"), s.sem("banks_free")
            turned, copied = s.sem("turned"), s.sem("copied")
            with nc.Block() as block:
                @block.tensor
                def _(pe):
                    def turn(t):
                        x = t - CT
                        pe.wait_ge(scaled, t + 1)
                        if x >= 1:
                            pe.wait_ge(copied, x)
                        for n in range(4):
                            tr = pe.transpose(m.ps[:, 4, n * P:(n + 1) * P], up[:, t % 2, n * P:(n + 1) * P], m.ident[:, :])
                            tr = pe.transpose(m.ps[:, 5, n * P:(n + 1) * P], down[:, t % 2, n * P:(n + 1) * P], m.ident[:, :])
                        tr.then_inc(turned, 1)

                    for t in range(NT):
                        if t >= 1:
                            pe.wait_ge(banks_free, t)
                            pe.wait_ge(exped, t)
                        for d in range(2):
                            pe.matmul(m.ps[:, 0, d * KW:(d + 1) * KW], tri[:, d, :], m.LG[:, t, d * KW:(d + 1) * KW],
                                      start=True, stop=True)
                        pe.matmul(m.ps[:, 1, :], tri[:, 2, :], m.LG[:, t, :], start=True, stop=True)
                        for n in range(4):
                            mm = pe.matmul(m.ps[:, 2, 2 * n:2 * n + 2], m.LG[:, t, n * P:(n + 1) * P],
                                           tri[:, 2, 0:P:G_CHUNK], start=True, stop=True)
                        mm.then_inc(summed, 1)
                        if t > CT:
                            turn(t - 1)
                    turn(NT - 1)

                def copy(act, t):
                    x = t - CT
                    act.wait_ge(turned, x + 1)
                    act.copy(qT[:, :, x * P:(x + 1) * P], m.ps[:, 4, :].rearrange("p (n c) -> p n c", c=P))
                    act.copy(kT[:, :, x * P:(x + 1) * P], m.ps[:, 5, :].rearrange("p (n c) -> p n c", c=P)).then_inc(copied, 1)

                @block.scalar
                def _(act):
                    for t in range(NT):
                        act.wait_ge(summed, t + 1)
                        if t >= 2:
                            act.wait_ge(scaled, t - 1)
                            if t - 2 >= CT:
                                act.wait_ge(turned, t - 1 - CT)
                        act.activation(up[:, t % 2, :], m.ps[:, 0, :], ACT.Exp)
                        act.activation(down[:, t % 2, :], m.ps[:, 0, :], ACT.Exp, scale=-1.0)
                        act.activation(decay[:, :, 2 * t:2 * t + 2],
                                       m.ps[:, 2, 0:8].rearrange("p (n c) -> p n c", c=2), ACT.Exp).then_inc(exped, 1)
                        act.wait_ge(diffed, t + 1)
                        act.activation(stay[:, t % 2, :], stay[:, t % 2, :], ACT.Exp).then_inc(stay_ready, 1)
                        if t > CT:
                            copy(act, t - 1)
                    copy(act, NT - 1)

                @block.vector
                def _(dve):
                    for t in range(NT):
                        dve.wait_ge(exped, t + 1)
                        dve.tensor_copy(stay[:, t % 2, :], m.ps[:, 0, :])
                        dve.drain()
                        dve.tensor_tensor(stay[:, t % 2, :], m.ps[:, 1, :], stay[:, t % 2, :], ALU.subtract)
                        dve.drain()
                        dve.sem_inc(diffed, 1)
                        dve.sem_inc(banks_free, 1)
                        k2 = m.Z[:, t, DK:DK + KW].unsqueeze(1).broadcast_to([P, 2, KW])
                        q2 = m.Z[:, t, DQ:DQ + KW].unsqueeze(1).broadcast_to([P, 2, KW])
                        both = lambda x: x[:, t % 2, :].rearrange("p (d n) -> p d n", d=2)
                        if t >= CT:
                            dve.scalar_tensor_tensor(out=both(up), in0=both(up), scalar=G_DK ** -0.5, in1=q2,
                                                     op0=ALU.mult, op1=ALU.mult)
                            dve.tensor_tensor(both(down), both(down), k2, ALU.mult)
                        dve.wait_ge(stay_ready, t + 1)
                        dve.tensor_tensor(m.LG[:, t, :].rearrange("p (d n) -> p d n", d=2), both(stay), k2,
                                          ALU.mult).then_inc(scaled, 1)

        def chunk_at(d, n):
            if d == 0:
                return n
            return CCH - 1 - n if n < CCH else CCH + XCH - 1 - (n - CCH)

        with Stage(nc, "gc") as s:
            kv_done, bank_read = s.sems("kv_done", 4), s.sems("bank_read", 4)
            with nc.Block() as block:
                @block.tensor
                def _(pe):
                    for n in range(NCH - 1):
                        for d in range(2):
                            b, use = (2 * n + d) % 4, (2 * n + d) // 4
                            c = chunk_at(d, n)
                            r = slice((c % 2) * G_CHUNK, (c % 2 + 1) * G_CHUNK)
                            pe.wait_ge(bank_read[b], use)
                            for pair in range(2):
                                at = d * KW + pair * P
                                mm = pe.matmul(m.ps[:, b, pair * 2 * G_DV:(pair + 1) * 2 * G_DV], m.LG[r, c // 2, at:at + P],
                                               m.Z[r, c // 2, DV + pair * 2 * G_DV:DV + (pair + 1) * 2 * G_DV],
                                               start=True, stop=True)
                            mm.then_inc(kv_done[b], 1)

                @block.vector
                def _(dve):
                    dve.memset(state[:, :, 0, :], 0.0)
                    dve.drain()
                    for n in range(NCH - 1):
                        for d in range(2):
                            b, use = (2 * n + d) % 4, (2 * n + d) // 4
                            c = chunk_at(d, n)
                            dve.wait_ge(kv_done[b], use + 1)
                            for h in range(G_HEADS):
                                pair, r = h // 2, slice((h % 2) * G_DK, (h % 2 + 1) * G_DK)
                                cols = slice(pair * G_DV, (pair + 1) * G_DV)
                                upd = dve.scalar_tensor_tensor(
                                    out=state[r, d, n + 1, cols], in0=state[r, d, n, cols],
                                    scalar=decay[r, 2 * d + pair, c:c + 1],
                                    in1=m.ps[r, b, h * G_DV:(h + 1) * G_DV], op0=ALU.mult, op1=ALU.add)
                            upd.then_inc(bank_read[b], 1)
                        dve.drain()

        with Stage(nc, "go") as s:
            within = s.sb("within", [P, 2, 2, P])
            cleared = s.sem("cleared")
            products, masked = s.sems("products", 4), s.sems("masked", 4)
            o_done, o_taken = s.sems("o_done", 2), s.sems("o_taken", 2)
            units = [(x, h, d) for x in range(XT) for h in range(G_HEADS) for d in range(2)]
            with nc.Block() as block:
                @block.tensor
                def _(pe):
                    def product(u):
                        x, h, d = units[u]
                        r = slice((h % 2) * G_DK, (h % 2 + 1) * G_DK)
                        n, cols = 2 * d + h // 2, slice(x * P, (x + 1) * P)
                        pe.wait_ge(masked[u % 4], u // 4)
                        pe.matmul(m.ps[:, 4 + u % 4, 0:P], kT[r, n, cols], qT[r, n, cols], start=True, stop=True)\
                            .then_inc(products[u % 4], 1)

                    def output(u):
                        x, h, d = units[u]
                        r = slice((h % 2) * G_DK, (h % 2 + 1) * G_DK)
                        n, cols = 2 * d + h // 2, slice(h // 2 * G_DV, (h // 2 + 1) * G_DV)
                        bank = 2 * (x % 2) + h % 2
                        if h == 0 and d == 0:
                            pe.wait_ge(o_taken[x % 2], x // 2)
                        pe.wait_ge(masked[u % 4], u // 4 + 1)
                        pe.matmul(m.ps[:, bank, cols], within[:, d, (u // 2) % 2, :],
                                  m.Z[:, CT + x, DV + h * G_DV:DV + (h + 1) * G_DV], start=(d == 0), stop=False,
                                  skip_group_check=True)
                        for c in range(2):
                            chunk = 2 * x + c
                            step = CCH + (chunk if d == 0 else XCH - 1 - chunk)
                            tok = slice(x * P + c * G_CHUNK, x * P + (c + 1) * G_CHUNK)
                            mm = pe.matmul(m.ps[c * G_CHUNK:(c + 1) * G_CHUNK, bank, cols], qT[r, n, tok],
                                           state[r, d, step, (h // 2) * G_DV:(h // 2 + 1) * G_DV],
                                           start=False, stop=(d == 1), skip_group_check=True)
                        if h == G_HEADS - 1 and d == 1:
                            mm.then_inc(o_done[x % 2], 1)

                    product(0)
                    product(1)
                    for u in range(len(units)):
                        if u + 2 < len(units):
                            product(u + 2)
                        output(u)

                @block.vector
                def _(dve):
                    dve.memset(within[:, :, :, :], 0.0)
                    dve.drain()
                    for u, (x, h, d) in enumerate(units):
                        dve.wait_ge(products[u % 4], u // 4 + 1)
                        dve.copy_predicated(within[:, d, (u // 2) % 2, :], tri[:, d, :].bitcast(U32),
                                            m.ps[:, 4 + u % 4, 0:P]).then_inc(masked[u % 4], 1)

                @block.scalar
                def _(act):
                    for x in range(XT):
                        act.wait_ge(o_done[x % 2], x // 2 + 1)
                        act.copy(m.H[:, CT + x, C_HEADS * C_DV:D].rearrange("p (a b v) -> p b a v", b=2, v=G_DV),
                                 m.ps[:, 2 * (x % 2):2 * (x % 2) + 2, 0:2 * G_DV].rearrange("p b (a v) -> p b a v", v=G_DV))\
                            .then_inc(o_taken[x % 2], 1)

        head_norm(nc, m, a, "gn1", m.H, range(CT, NT), [(C_HEADS * C_DV, G_HEADS, G_DV, a["d_gn"])])
        with Stage(nc, "gr") as s:
            den = s.sb("den", [P, XT, VW])
            exped = s.sem("exped")
            with nc.Block() as block:
                @block.scalar
                def _(act):
                    act.activation(den[:, :, :], m.Z[:, CT:NT, DR:DR + VW], ACT.Exp, scale=-1.0).then_inc(exped, 1)

                @block.vector
                def _(dve):
                    dve.wait_ge(exped, 1)
                    dve.tensor_scalar(den[:, :, :], den[:, :, :], 1.0, None, ALU.add)
                    dve.drain()
                    dve.reciprocal(den[:, :, :], den[:, :, :])
                    dve.drain()
                    dve.tensor_tensor(den[:, :, :], den[:, :, :], m.Z[:, CT:NT, DR:DR + VW], ALU.mult)
                    dve.drain()
                    out = m.H[:, CT:NT, C_HEADS * C_DV:D]
                    dve.tensor_tensor(out, out, den[:, :, :], ALU.mult)


def top16(dve, heads, values, src, spare, index):
    for h in heads:
        dve.max(values[:, h, 0:8], src[:, h, :])
    dve.drain()
    yield
    for h in heads:
        dve.max_index(index[:, h, 0:8], values[:, h, 0:8], src[:, h, :])
    yield
    for h in heads:
        dve.match_replace(spare[:, h, :], values[:, h, 0:8], src[:, h, :], LOW)
    dve.drain()
    yield
    for h in heads:
        dve.max(values[:, h, 8:16], spare[:, h, :])
    dve.drain()
    for h in heads:
        dve.max_index(index[:, h, 8:16], values[:, h, 8:16], spare[:, h, :])
    dve.drain()
    yield


class FirstWeights:

    def __init__(self, nc, m, a, s, layer):
        self.a, self.layer = a, layer
        self.keys, self.w = s.sb("keys", [P, 2 * PH, P]), s.sb("w", [P, 2, KC, BANK])
        self.keys_loaded, self.loaded = s.sem("keys_loaded"), s.sems("loaded", 2)

    def load(self, sp, n):
        sp.dma_start(self.w[:, n % 2], self.a["p_wq"][self.layer][:, n * BANK:(n + 1) * BANK]
                     .rearrange("(k p) n -> p k n", p=P)).then_inc(self.loaded[n % 2], 16)

    def prefetch(self, sp):
        sp.dma_start(self.keys[:, :, :], self.a["p_keys"][self.layer].rearrange("h s n d -> n (h s) d"))\
            .then_inc(self.keys_loaded, 16)
        for n in range(2):
            self.load(sp, n)


def first_scores(nc, m, a, layer, t0, pre):
    NH, PER = 2 * PH, 8
    with Stage(nc, f"es{layer}") as s:
        keys, w, keys_loaded, loaded = pre.keys, pre.w, pre.keys_loaded, pre.loaded
        keysT = s.sb("keysT", [P, NH, P])
        qT = s.sb("qT", [P, 2, P])
        sc, rest = s.sb("sc", [P, NH, NK]), s.sb("rest", [P, NH, NK])
        claimed, sc_ready = s.sem("claimed"), s.sem("sc_ready")
        keys_stored, = s.pool_dma_sems(m, "keys_stored", 1)
        keys_turned, keysT_ready = s.sem("keys_turned"), s.sem("keysT_ready")
        used = s.sems("used", 2)
        q_done, qT_ready = s.sems("q_done", 2), s.sems("qT_ready", 2)
        scored, taken = s.sems("scored", 2), s.sems("taken", 2)
        with nc.Block() as block:
            @block.sync
            def _(sp):
                for n in range(2, NH * P // BANK):
                    sp.wait_ge(used[n % 2], n // 2)
                    pre.load(sp, n)

            @block.tensor
            def _(pe):
                pe.wait_ge(keys_loaded, 16)
                for h in range(NH):
                    tr = pe.transpose(m.ps[:, h // 4, (h % 4) * P:(h % 4 + 1) * P], keys[:, h, :], m.ident[:, :])
                tr.then_inc(keys_turned, 1)
                pe.wait_ge(keysT_ready, 1)
                with pe.Fori(0, NH // PER) as i:
                    def query(h):
                        b, use = h % 2, i * (PER // 2) + h // 2
                        if h % 4 == 0:
                            pe.wait_ge(loaded[h // 4], i * 16 + 16)
                        pe.wait_ge(qT_ready[b], use)
                        for k in range(KC):
                            mm = pe.matmul(m.ps[:, b, 0:P], w[:, h // 4, k, (h % 4) * P:(h % 4 + 1) * P],
                                           m.hT[:, k, t0 * P:(t0 + 1) * P], start=(k == 0), stop=(k == KC - 1))
                        mm.then_inc(q_done[b], 1)
                        if h % 4 == 3:
                            pe.drain()
                            pe.sem_inc(used[h // 4], 1)

                    def score(h):
                        b, use = h % 2, i * (PER // 2) + h // 2
                        pe.wait_ge(qT_ready[b], use + 1)
                        pe.wait_ge(taken[b], use)
                        pe.matmul(m.ps[:, 4 + b, 0:P], qT[:, b, :],
                                  keysT[:, ds(i * PER + h, 1), :].rearrange("p o n -> p (o n)"),
                                  start=True, stop=True).then_inc(scored[b], 1)

                    for h in range(PER):
                        query(h)
                        if h:
                            score(h - 1)
                    score(PER - 1)

            @block.gpsimd
            def _(pool):
                pool.wait_ge(keysT_ready, 1)
                pool.dma_start(m.keysT[:, :, :], keysT[:, :, :]).then_inc(keys_stored, 16)
                pool.wait_ge(keys_stored, 16)

            @block.scalar
            def _(act):
                act.wait_ge(keys_turned, 1)
                act.copy(keysT[:, :, :].rearrange("p h n -> p (h n)"),
                         m.ps[:, 0:4, :].rearrange("p b c -> p (b c)")).then_inc(keysT_ready, 1)
                with act.Fori(0, NH // PER) as i:
                    def query(h):
                        b, use = h % 2, i * (PER // 2) + h // 2
                        act.wait_ge(q_done[b], use + 1)
                        act.wait_ge(scored[b], use)
                        act.copy(qT[:, b, :], m.ps[:, b, 0:P]).then_inc(qT_ready[b], 1)

                    def score(h):
                        b, use = h % 2, i * (PER // 2) + h // 2
                        act.wait_ge(scored[b], use + 1)
                        act.sem_inc(claimed, 1)
                        act.copy(sc[:, ds(i * PER + h, 1), :].rearrange("p o n -> p (o n)"), m.ps[:, 4 + b, 0:P])\
                            .then_inc(taken[b], 1)
                        act.drain()
                        act.sem_inc(sc_ready, 1)

                    for h in range(PER):
                        query(h)
                        if h:
                            score(h - 1)
                    score(PER - 1)

            @block.vector
            def _(dve):
                for h in range(0, NH, 4):
                    dve.wait_ge(sc_ready, h + 4)
                    for _ in top16(dve, range(h, h + 4), m.val, sc, rest, m.pos):
                        pass


def run_experts(nc, m, a, layer, tiles, last):
    T, t0 = len(tiles), tiles[0]
    NH = 2 * PH
    RING, IDX, BODY = 8, 8, 32
    NBODY, ROUNDS, NIDX = SLOTS // BODY, BODY // RING, BODY // IDX
    VDVE = 3
    u_rows, v_rows = a["p_u"].rearrange("l e d -> (l e) d"), a["p_v"].rearrange("l e d -> (l e) d")
    with Stage(nc, f"ex{layer}") as s:
        ring = s.sb("ring", [P, RING, D])
        idx = s.sb("idx", [P, NIDX, IDX], U32)
        expert, weight = s.sb("expert", [P, 2 * SLOTS], U32), s.sb("weight", [P, SLOTS])
        gates = s.sb("gates", [P, SLOTS])
        dots, product = s.sb("dots", [P, SLOTS]), s.sb("product", [P, 2, D])
        mixed = s.sb("mixed", [P, D])
        NDIAG = RING - RING // 4
        diag = s.sb("diag", [P, NDIAG, P])
        zeros = s.sb("zeros", [P, BANK], mybir.dt.bfloat16)
        g = s.sb("g", [P, 2, D])
        landed, used = s.pool_dma_sems(m, "landed", RING), s.sems("used", RING)
        idx_landed = s.sems("idx_landed", NIDX)
        dve_group, pe_group = s.sems("dve_group", NIDX), s.sems("pe_group", NIDX)
        idx_free = s.sem("idx_free")
        claimed, zeroed, g_loaded = s.sem("claimed"), s.sem("zeroed"), s.sem("g_loaded")
        dots_ready, gelu_done, weights_ready = s.sem("dots_ready"), s.sem("gelu_done"), s.sem("weights_ready")
        diag_ready = s.sems("diag_ready", 4)
        summed, mix_taken, added, stored = s.sem("summed"), s.sem("mix_taken"), s.sem("added"), s.sem("stored")

        sc, rest = s.sb("sc", [P, NH, NK]), s.sb("rest", [P, NH, NK])
        val, pos, posf = m.val, m.pos, s.sb("posf", [P, NH, TOPK])
        best, at_ = s.sb("best", [P, PH, TOPK]), s.sb("at", [P, PH, TOPK], U32)
        shift = s.sb("shift", [P, PH, TOPK])
        part, partf = s.sb("part", [P, 2, SLOTS], U32), s.sb("partf", [P, 2, SLOTS])
        iota, num, total = s.sb("iota", [P, TOPK]), s.sb("num", [P, 2, SLOTS]), s.sb("total", [P, PH])
        iota_loaded, sc_loaded, sc_read = s.sem("iota_loaded"), s.sem("sc_loaded"), s.sem("sc_read")
        shifted, exped, chosen = s.sem("shifted"), s.sem("exped"), s.sem("chosen")
        LATE = T - 1
        COLS = LATE * P // (2 if LATE * P > BANK else 1)
        NB = LATE * P // COLS
        LPER = 4
        keysT, wq = s.sb("keysT", [P, NH, NK]), s.sb("wq", [P, LPER, KC, P])
        qT, late = s.sb("qT", [P, 2, LATE * P]), s.sb("late", [P, 2, LATE, P])
        keysT_loaded, wq_loaded, late_stored = s.sem("keysT_loaded"), s.sems("wq_loaded", LPER), s.sems("late_stored", 2)
        q_done, qT_ready = s.sems("q_done", 2), s.sems("qT_ready", 2)
        scored, score_taken = s.sems("scored", 2), s.sems("score_taken", 2)
        cand = sc[:, :, :].rearrange("p h k -> p (h k)").rearrange("p (h c) -> p h c", c=TOPK * TOPK)
        left = rest[:, :, :].rearrange("p h k -> p (h k)").rearrange("p (h c) -> p h c", c=TOPK * TOPK)
        hot = rest[:, :, :].rearrange("p h k -> p (h k)").rearrange("p (n i) -> p n i", i=TOPK)

        def tiles_loop(eng, tile):
            if T > 1:
                with eng.Fori(0, T - 1) as t:
                    tile(t, True)
            tile(T - 1, False)

        def bodies(eng, t, phase):
            with eng.Fori(0, NBODY) as i:
                yield (t * 2 + phase) * NBODY + i, i

        def side(t):
            return (t % 2) * SLOTS

        with nc.Block() as block:
            @block.sync
            def _(sp):
                sp.dma_start(iota[:, :], rows(a["iota"])).then_inc(iota_loaded, 16)
                for st in range(2):
                    sp.dma_start(g[:, st, :], rows(m.mods[layer, 1 - st:2 - st, 5 * D:6 * D])).then_inc(g_loaded, 16)

                def tile(t, more):
                    first = sp.snap(side(t))
                    sp.wait_ge(chosen, t + 1)
                    sp.sem_inc(idx_free, 1)
                    for phase in range(2):
                        if phase == 1 and more:
                            for b in range(2):
                                sp.wait_ge(late_stored[b], 16 * PH)
                            sp.wait_ge(sc_read, t + 1)
                            sp.dma_start(sc[:, :, :].rearrange("p h n -> p (h n)"),
                                         m.scores[ds(t + (t0 + 1), 1)].rearrange("o p n -> p (o n)")).then_inc(sc_loaded, 16)
                        for turn, i in bodies(sp, t, phase):
                            for b in range(NIDX):
                                sp.wait_ge(dve_group[b], turn)
                                sp.sem_inc(idx_free, 1)
                                sp.wait_ge(pe_group[b], t * NBODY + (i if phase else 0))
                                sp.dma_start(idx[:, b, :], expert[:, ds(first + i * BODY + b * IDX, IDX)])\
                                    .then_inc(idx_landed[b], 16)
                tiles_loop(sp, tile)

            @block.gpsimd
            def _(pool):
                def tile(t, more):
                    for phase in range(2):
                        for turn, i in bodies(pool, t, phase):
                            for n in range(BODY):
                                r = n % RING
                                if n % IDX == 0:
                                    pool.wait_ge(idx_landed[n // IDX], turn * 16 + 16)
                                pool.wait_ge(used[r], turn * ROUNDS + n // RING)
                                pool.sem_inc(claimed, 1)
                                pool.indirect_dma_start(ring[:, r, :], None, v_rows if phase else u_rows,
                                                        bass.IndirectOffsetOnAxis(ap=idx[:, n // IDX, n % IDX:n % IDX + 1], axis=0),
                                                        ).then_inc(landed[r], 16)
                tiles_loop(pool, tile)

            @block.vector
            def _(dve):
                def choose(t, first=False):
                    if not first:
                        dve.wait_ge(sc_loaded, t * 16)
                        dve.sem_inc(claimed, 1)
                        yield from top16(dve, range(0, PH), val, sc, rest, pos)
                        yield from top16(dve, range(PH, NH), val, sc, rest, pos)
                    dve.tensor_copy(posf[:, :, :], pos[:, :, :])
                    pairs = val[:, :, :].rearrange("p (h s) k -> p h s k", s=2)
                    dve.tensor_tensor(cand.rearrange("p h (i j) -> p h i j", j=TOPK),
                                      pairs[:, :, 0, :].unsqueeze(3).broadcast_to([P, PH, TOPK, TOPK]),
                                      pairs[:, :, 1, :].unsqueeze(2).broadcast_to([P, PH, TOPK, TOPK]), ALU.add)
                    dve.drain()
                    yield
                    yield from top16(dve, range(0, PH // 2), best, cand, left, at_)
                    yield from top16(dve, range(PH // 2, PH), best, cand, left, at_)
                    dve.sem_inc(sc_read, 1)
                    flat = at_[:, :, :].rearrange("p h k -> p (h k)")
                    dve.tensor_scalar(part[:, 0, :], flat, 4, None, ALU.logical_shift_right)
                    dve.tensor_scalar(part[:, 1, :], flat, TOPK - 1, None, ALU.bitwise_and)
                    dve.tensor_tensor(shift[:, :, :], best[:, :, :], best[:, :, 0:1].broadcast_to([P, PH, TOPK]),
                                      ALU.subtract)
                    dve.drain()
                    dve.sem_inc(shifted, 1)
                    dve.tensor_copy(partf[:, :, :], part[:, :, :])
                    dve.drain()
                    halves = posf[:, :, :].rearrange("p (h s) k -> p h s k", s=2)
                    h4 = hot.rearrange("p (h k) i -> p h k i", k=TOPK)
                    for half in range(2):
                        dve.tensor_tensor(hot, iota[:, :].unsqueeze(1).broadcast_to([P, SLOTS, TOPK]),
                                          partf[:, half, :].unsqueeze(2).broadcast_to([P, SLOTS, TOPK]), ALU.is_equal)
                        dve.drain()
                        yield
                        dve.tensor_tensor(h4, h4, halves[:, :, half, :].unsqueeze(2).broadcast_to([P, PH, TOPK, TOPK]), ALU.mult)
                        dve.drain()
                        dve.tensor_reduce(num[:, half, :], hot, AX.X, ALU.add)
                        dve.drain()
                        yield
                    dve.scalar_tensor_tensor(out=num[:, 0, :], in0=num[:, 0, :], scalar=float(NK), in1=num[:, 1, :],
                                             op0=ALU.mult, op1=ALU.add)
                    dve.drain()
                    dve.tensor_scalar(expert[:, ds(side(t), SLOTS)], num[:, 0, :], float(layer * NK * NK), None, ALU.add)
                    dve.drain()
                    dve.sem_inc(chosen, 1)
                    yield

                def weigh(t):
                    dve.wait_ge(exped, t + 1)
                    dve.tensor_reduce(total[:, :], shift[:, :, :], AX.X, ALU.add)
                    dve.drain()
                    dve.reciprocal(total[:, :], total[:, :])
                    dve.drain()
                    dve.tensor_tensor(gates[:, :].rearrange("p (h k) -> p h k", k=TOPK),
                                      shift[:, :, :], total[:, :].unsqueeze(2).broadcast_to([P, PH, TOPK]), ALU.mult)
                    dve.drain()

                def tile(t, more):
                    for turn, i in bodies(dve, t, 0):
                        for n in range(BODY):
                            r = n % RING
                            dve.wait_ge(landed[r], turn * (ROUNDS * 16) + (n // RING + 1) * 16)
                            dve.scalar_tensor_tensor(out=product[:, n % 2, :], in0=ring[:, r, :], scalar=1.0,
                                                     in1=m.H[:, t + t0, :], op0=ALU.mult, op1=ALU.mult,
                                                     accum_out=dots[:, ds(i * BODY + n, 1)]).then_inc(used[r], 1)
                            if n % IDX == IDX - 1:
                                dve.sem_inc(dve_group[n // IDX], 1)
                            if n % 2:
                                dve.drain()
                    dve.sem_inc(dots_ready, 1)
                    dve.memset(mixed[:, :], 0.0)
                    weigh(t)
                    dve.wait_ge(gelu_done, t + 1)
                    dve.tensor_tensor(weight[:, :], dots[:, :], gates[:, :], ALU.mult)
                    dve.drain()
                    dve.sem_inc(weights_ready, 1)
                    steps = choose(t + 1) if more else iter(())
                    for body in range(NBODY):
                        turn = (t * 2 + 1) * NBODY + body
                        for n in range(BODY):
                            r = n % RING
                            if n % 4 == VDVE:
                                dve.wait_ge(landed[r], turn * (ROUNDS * 16) + (n // RING + 1) * 16)
                                dve.scalar_tensor_tensor(out=mixed[:, :], in0=ring[:, r, :],
                                                         scalar=weight[:, body * BODY + n:body * BODY + n + 1],
                                                         in1=mixed[:, :], op0=ALU.mult, op1=ALU.add).then_inc(used[r], 1)
                                dve.drain()
                                next(steps, None)
                            if n % IDX == IDX - 1:
                                dve.sem_inc(dve_group[n // IDX], 1)
                    for _ in steps:
                        pass
                    dve.wait_ge(summed, t + 1)
                    dve.tensor_tensor(mixed[:, :], mixed[:, :], m.ps[:, 0:2, :].rearrange("p b c -> p (b c)"), ALU.add)\
                        .then_inc(mix_taken, 1)
                    dve.drain()
                    stream = dve.snap((t + t0 + 4) // 6)
                    dve.tensor_tensor(mixed[:, :], mixed[:, :], g[:, ds(stream, 1), :].rearrange("p o d -> p (o d)"), ALU.mult)
                    dve.drain()
                    dve.tensor_tensor(m.R[:, t + t0, :], m.R[:, t + t0, :], mixed[:, :], ALU.add).then_inc(added, 1)
                    dve.drain()

                dve.memset(zeros[:, :], 0.0).then_inc(zeroed, 1)
                dve.wait_ge(iota_loaded, 16)
                dve.wait_ge(g_loaded, 32)
                for _ in choose(0, True):
                    pass
                tiles_loop(dve, tile)

            @block.scalar
            def _(act):
                def shift_exp(t):
                    act.wait_ge(shifted, t + 1)
                    act.activation(shift[:, :, :], shift[:, :, :], ACT.Exp).then_inc(exped, 1)

                def load_wq(h, i):
                    act.sem_inc(claimed, 1)
                    act.dma_start(wq[:, h], a["p_wq"][layer][:, ds((i * LPER + h) * P, P)]
                                  .rearrange("(k p) n -> p k n", p=P)).then_inc(wq_loaded[h], 16)

                def late_scores(i, more):
                    for pair in range(LPER // 2):
                        use = i * (LPER // 2) + pair
                        for b in range(2):
                            act.wait_ge(q_done[b], use + 1)
                            act.wait_ge(scored[b], use)
                            act.copy(qT[:, b, :].rearrange("p (n c) -> p n c", c=COLS), m.ps[:, 2 + 2 * b:2 + 2 * b + NB, 0:COLS])\
                                .then_inc(qT_ready[b], 1)
                            if more:
                                load_wq(2 * pair + b, i + 1)
                        for b in range(2):
                            act.wait_ge(scored[b], use + 1)
                            act.wait_ge(late_stored[b], use * 16)
                            act.copy(late[:, b], m.ps[:, 6:8, :].rearrange("p b (t n) -> p (b t) n", n=P)[:, 0:LATE, :])\
                                .then_inc(score_taken[b], 1)
                            act.drain()
                            act.sem_inc(claimed, 1)
                            act.dma_start(m.scores[t0 + 1:NT, :, ds((use * 2 + b) * P, P)].rearrange("t p n -> p t n"),
                                          late[:, b]).then_inc(late_stored[b], 16)

                def tile(t, more):
                    shift_exp(t)
                    act.wait_ge(dots_ready, t + 1)
                    act.activation(dots[:, :], dots[:, :], ACT.Gelu).then_inc(gelu_done, 1)
                    act.wait_ge(weights_ready, t + 1)
                    for body in range(NBODY):
                        for n in range(BODY):
                            if n % 4 != VDVE:
                                k = n - n // 4 - (n % 4 > VDVE)
                                act.wait_ge(used[n % RING], ((t * 2 + 1) * NBODY + body) * ROUNDS + n // RING)
                                act.activation(diag[:, k % NDIAG, :], m.ident[:, :], ACT.Copy,
                                               scale=weight[:, body * BODY + n:body * BODY + n + 1]).then_inc(diag_ready[k % 4], 1)
                    if last:
                        act.wait_ge(added, t + 1)
                        act.sem_inc(claimed, 1)
                        act.dma_start(m.out[0, ds((t + t0 - CT) * P, P), :], m.R[:, t + t0, :]).then_inc(stored, 16)

                act.dma_start(keysT[:, :, :], m.keysT[:, :, :]).then_inc(keysT_loaded, 16)
                for h in range(LPER):
                    load_wq(h, 0)
                with act.Fori(0, NH // LPER - 1) as i:
                    late_scores(i, True)
                late_scores(NH // LPER - 1, False)
                tiles_loop(act, tile)
                if last:
                    act.wait_ge(stored, 16 * T)

            @block.tensor
            def _(pe):
                pe.wait_ge(zeroed, 1)
                pe.wait_ge(keysT_loaded, 16)
                with pe.Fori(0, NH // LPER) as i:
                    for pair in range(LPER // 2):
                        use = i * (LPER // 2) + pair
                        for b in range(2):
                            pe.wait_ge(wq_loaded[2 * pair + b], i * 16 + 16)
                            pe.wait_ge(qT_ready[b], use)
                            for n in range(NB):
                                for k in range(KC):
                                    at = (t0 + 1) * P + n * COLS
                                    mm = pe.matmul(m.ps[:, 2 + 2 * b + n, 0:COLS], wq[:, 2 * pair + b, k, :],
                                                   m.hT[:, k, at:at + COLS], start=(k == 0), stop=(k == KC - 1))
                            mm.then_inc(q_done[b], 1)
                        for b in range(2):
                            pe.wait_ge(qT_ready[b], use + 1)
                            pe.wait_ge(score_taken[1 - b], use + b)
                            for n in range(LATE):
                                mm = pe.matmul(m.ps[:, 6 + n // 4, (n % 4) * P:(n % 4 + 1) * P], qT[:, b, n * P:(n + 1) * P],
                                               keysT[:, ds(i * LPER + 2 * pair + b, 1), :].rearrange("p o n -> p (o n)"),
                                               start=True, stop=True)
                            mm.then_inc(scored[b], 1)

                def tile(t, more):
                    pe.wait_ge(mix_taken, t)
                    for b in range(2):
                        pe.matmul(m.ps[:, b, :], zeros[:, 0:P], zeros[:, :], start=True, stop=False, skip_group_check=True)
                    for turn, i in bodies(pe, t, 1):
                        for n in range(BODY):
                            r = n % RING
                            if n % 4 != VDVE:
                                k = n - n // 4 - (n % 4 > VDVE)
                                pe.wait_ge(diag_ready[k % 4], (t * NBODY + i) * (BODY * 3 // 16) + k // 4 + 1)
                                pe.wait_ge(landed[r], turn * (ROUNDS * 16) + (n // RING + 1) * 16)
                                for b in range(2):
                                    mm = pe.matmul(m.ps[:, b, :], diag[:, k % NDIAG, :], ring[:, r, b * BANK:(b + 1) * BANK],
                                                   start=False, stop=False, skip_group_check=True)
                                mm.then_inc(used[r], 1)
                            if n % IDX == IDX - 1:
                                pe.sem_inc(pe_group[n // IDX], 1)
                    pe.drain()
                    pe.sem_inc(summed, 1)
                tiles_loop(pe, tile)


def experts(nc, m, a, layer, tiles, last):
    with (nc.sbuf_tensor(f"val{layer}", [P, 2 * PH, TOPK], F32) as m.val,
          nc.sbuf_tensor(f"pos{layer}", [P, 2 * PH, TOPK], U32) as m.pos):
        with Stage(nc, f"pre{layer}") as s:
            pre = FirstWeights(nc, m, a, s, layer)
            modulated_norm(nc, m, a, layer, 1, "norm2", tiles, pre.prefetch)
            first_scores(nc, m, a, layer, tiles[0], pre)
        run_experts(nc, m, a, layer, tiles, last)


def shape_constants():
    def rope(dim, name):
        pos = np.arange(SEQ)
        axis = dim // 2
        inv = (1.0 / (THETA ** (np.arange(0, axis, 2, dtype=np.float32) / axis))).astype(np.float32)
        ang = np.concatenate([(pos // GRID_W)[:, None].astype(np.float32) * inv,
                              (pos % GRID_W)[:, None].astype(np.float32) * inv], axis=-1)
        cos = np.ones((TOK, dim), np.float32)
        sin = np.zeros((TOK, dim), np.float32)
        cos[CTX:] = np.repeat(np.cos(ang), 2, axis=1)
        sin[CTX:] = np.repeat(np.sin(ang), 2, axis=1) * np.tile([-1.0, 1.0], dim // 2)
        return {name + "_cos": cos, name + "_sin": sin}

    k, q = np.arange(P)[None, :], np.arange(P)[:, None]
    band = np.stack([np.where(k >= q, 0.0, NEG), np.where(k <= q, 0.0, NEG)]).astype(np.float32)
    s_, c_ = np.arange(P)[:, None], np.arange(P)[None, :]
    same = s_ // G_CHUNK == c_ // G_CHUNK
    tri = np.stack([same & (s_ <= c_), same & (s_ >= c_), same]).astype(np.float32)
    return {"tri": tri, "iota": np.arange(TOPK, dtype=np.float32)[None, :], "ident": np.eye(P, dtype=np.float32), "band": band} | rope(B_DH, "rope_ab") | rope(C_ROPE, "rope_c")


def program(nc, a, out):
    with ExitStack() as ctx:
        m = Memory()
        m.ctx = ctx
        m.mods = nc.dram_tensor("modulations", [2, 2, 6 * D], F32, kind="Internal").ap()
        m.scores = nc.dram_tensor("key_scores", [NT, P, 2 * PH * NK], F32, kind="Internal").ap()
        m.keysT = nc.dram_tensor("keys_transposed", [P, 2 * PH, NK], F32, kind="Internal").ap()
        m.R = ctx.enter_context(nc.sbuf_tensor("R", [P, NT, D], F32))
        m.H = ctx.enter_context(nc.sbuf_tensor("H", [P, NT, D], F32))
        m.hT = ctx.enter_context(nc.sbuf_tensor("hT", [P, KC, TOK], F32))
        m.ident = ctx.enter_context(nc.sbuf_tensor("ident_sb", [P, P], F32))
        m.eps = ctx.enter_context(nc.sbuf_tensor("eps", [P, 1], F32))
        m.csil = ctx.enter_context(nc.sbuf_tensor("csil", [P, KC, 6], F32))
        m.ps = ctx.enter_context(nc.psum_tensor("ps", [P, 8, BANK], F32))
        m.neg_lam = ctx.enter_context(nc.sbuf_tensor("neg_lam", [P, 1], F32))
        m.sink = ctx.enter_context(nc.sbuf_tensor("sink", [P, B_HEADS], F32))
        m.neg_sink = ctx.enter_context(nc.sbuf_tensor("neg_sink", [P, B_HEADS], F32))
        m.band = ctx.enter_context(nc.sbuf_tensor("band_sb", [P, 2, P], F32))
        m.Z = None
        m.out = out

        start(nc, m, a)
        with nc.sbuf_tensor("Z", [P, NT, EVEN_IN], F32) as m.Z:
            with Stage(nc, "win0") as s:
                pre = ProjectWeights(nc, m, s, a["e_w_in"][0], EVEN_IN // 6)
                modulated_norm(nc, m, a, 0, 0, "norm1", range(NT), pre.prefetch)
                project(nc, m, "pin0", pre, range(NT), out=m.Z)
            head_norm(nc, m, a, "qk0", m.Z, range(NT),
                      [(AQ, 2 * A_HEADS, A_DQK, a["a_qn"]), (AK, 2 * A_HEADS, A_DQK, a["a_kn"]),
                       (BQ, B_HEADS, B_DH, a["b_qn"]), (BK, B_KV, B_DH, a["b_kn"])], rope=(0, B_DH, "rope_ab"),
                      beside=NextModulation)
            differential_attention(nc, m)
            windowed_attention(nc, m)
        m.Z = None
        head_norm(nc, m, a, "gn0", m.H, range(NT), [(0, A_HEADS, A_DV, a["a_gn"])], factor=1.0 - LAM_INIT)
        with Stage(nc, "wout0") as s:
            pre = ProjectWeights(nc, m, s, a["e_w_out"][0], BANK, gate=m.mods[0, :, 2 * D:3 * D])
            turn_h(nc, m, "th0", range(NT), pre.prefetch)
            project(nc, m, "pout0", pre, range(NT))
        experts(nc, m, a, 0, range(NT), False)

        XTILES = range(CT, NT)
        with nc.sbuf_tensor("Z1", [P, NT, ODD_IN], F32) as m.Z:
            with Stage(nc, "win1") as s:
                pre = ProjectWeights(nc, m, s, a["o_w_in"][0], ODD_IN // 4)
                modulated_norm(nc, m, a, 1, 0, "norm1", range(NT), pre.prefetch)
                project(nc, m, "pin1", pre, range(NT), out=m.Z)
            head_norm(nc, m, a, "lat", m.Z, range(NT), [(CQ, 1, CKV - CQ, a["c_gq"]), (CKV, 1, KPE - CKV, a["c_gkv"])])
            with nc.sbuf_tensor("LG", [P, NT, 2 * G_HEADS * G_DK], F32) as m.LG:
                m.KV = m.hT[:, :, :].rearrange("p k c -> p (k c)").rearrange("p (t d) -> p t d", d=D)
                with (nc.sbuf_tensor("Q", [P, XT, C_HEADS * C_DQ], F32) as m.Q,
                      nc.sbuf_tensor("K", [P, NT, C_HEADS * C_DQ], F32) as m.K):
                    latent_up(nc, m, a)
                    head_norm(nc, m, a, "qn1", m.Q, XTILES, [(0, C_HEADS, C_DQ, a["c_qn"])], rope=(C_NOPE, C_ROPE, "rope_c"))
                    head_norm(nc, m, a, "kn1", m.K, range(NT), [(0, C_HEADS, C_DQ, a["c_kn"])], rope=(C_NOPE, C_ROPE, "rope_c"))
                    latent_attention(nc, m)
                linear_attention(nc, m, a)
        m.Z = None
        with Stage(nc, "wout1") as s:
            pre = ProjectWeights(nc, m, s, a["o_w_out"][0], BANK, gate=m.mods[1, :, 2 * D:3 * D])
            turn_h(nc, m, "th1", XTILES, pre.prefetch)
            project(nc, m, "pout1", pre, XTILES)
        experts(nc, m, a, 1, XTILES, True)


def _(sp):
                sp.dma_start(debug["out_r"].rearrange("p (t d) -> p t d", t=NT), m.R[:, :, :]).then_inc(done, 16)
                sp.dma_start(debug["out_h"].rearrange("p (t d) -> p t d", t=NT), m.H[:, :, :]).then_inc(done, 16)
                n = 2
                if m.Z is not None:
                    sp.dma_start(debug["out_z"].rearrange("p (t d) -> p t d", t=NT), m.Z[:, :, :]).then_inc(done, 16)
                    n = 3
                sp.wait_ge(done, 16 * n)


def kernel(**inputs):
    import concourse.bacc as bacc
    from concourse.bass_utils import run_bass_kernel_spmd

    nc = bacc.Bacc("TRN2", target_bir_lowering=False, num_devices=1)
    arrays, a = {}, {}
    for name, x in (inputs | shape_constants()).items():
        x = np.ascontiguousarray(x)
        arrays[f"in_{name}"] = x
        a[name] = nc.dram_tensor(f"in_{name}", x.shape, mybir.dt.from_np(x.dtype), kind="ExternalInput").ap()
    out = nc.dram_tensor("out_x", (1, SEQ, D), F32, kind="ExternalOutput").ap()
    program(nc, a, out)
    return run_bass_kernel_spmd(nc, [arrays], core_ids=[0]).results[0]["out_x"]
```
